# Optimizing a Trainium2 kernel written in Bass

```python
import math
import jax, jax.numpy as jnp
from jax import lax
import numpy as np

D_MODEL = 1024
BATCH = 1
SEQ = 512
DEPTH = 2

MIX_WIDTH = D_MODEL
A_HEADS = 4
A_HEAD_DIM = MIX_WIDTH // 2 // A_HEADS
A_WIDTH = A_HEADS * A_HEAD_DIM
B_HEADS = 4
B_HEAD_DIM = MIX_WIDTH // 2 // B_HEADS
B_WIDTH = B_HEADS * B_HEAD_DIM
IN_AB = A_WIDTH + 2 * B_WIDTH
CONV_WIDTH = 31
POOL_WINDOWS = (2, 4, 8, 16)
C_GROUPS = len(POOL_WINDOWS)
C_GROUP_DIM = D_MODEL // C_GROUPS
D_FF = int(math.ceil((8 * D_MODEL / 3) / 256) * 256)
N_EVEN = (DEPTH + 1) // 2
N_ODD = DEPTH // 2
RMS_EPS = 1e-6
LN_EPS = 1e-5


def rmsnorm(x, g):
    xf = x.astype(jnp.float32)
    inv = lax.rsqrt(jnp.mean(xf * xf, axis=-1, keepdims=True) + RMS_EPS)
    return (xf * inv).astype(x.dtype) * g

def layernorm(x, g, b):
    xf = x.astype(jnp.float32)
    mu = jnp.mean(xf, axis=-1, keepdims=True)
    var = jnp.mean(jnp.square(xf - mu), axis=-1, keepdims=True)
    return ((xf - mu) * lax.rsqrt(var + LN_EPS)).astype(x.dtype) * g + b

def swiglu_ffn(h, w_gate, w_up, w_down):
    return (jax.nn.silu(h @ w_gate) * (h @ w_up)) @ w_down

def fnet_heads(a, fnet_map):
    bsz, seq, _ = a.shape
    a4 = a.reshape(bsz, seq, A_HEADS, A_HEAD_DIM).astype(jnp.float32)
    f = jnp.fft.fft2(a4, axes=(1, 3), norm="ortho").real.astype(a.dtype)
    y = jnp.einsum("bshd,hde->bshe", f, fnet_map)
    return y.reshape(bsz, seq, A_WIDTH)

def conformer_conv_heads(v, gate, conv_w, conv_b, ln_g, ln_b):
    u = v * jax.nn.sigmoid(gate)
    pad = CONV_WIDTH // 2
    u = lax.conv_general_dilated(
        u, conv_w[:, None, :].astype(u.dtype),
        window_strides=(1,), padding=[(pad, pad)],
        dimension_numbers=("NWC", "WIO", "NWC"),
        feature_group_count=B_WIDTH) + conv_b
    bsz, seq, _ = u.shape
    u = u.reshape(bsz, seq, B_HEADS, B_HEAD_DIM)
    u = layernorm(u, ln_g.reshape(B_HEADS, B_HEAD_DIM), ln_b.reshape(B_HEADS, B_HEAD_DIM))
    return jax.nn.silu(u).reshape(bsz, seq, B_WIDTH)

def centred_pool_minus_self(u, window):
    seq = u.shape[1]
    uf = u.astype(jnp.float32)
    cs = jnp.concatenate([jnp.zeros_like(uf[:, :1]), lax.cumsum(uf, axis=1)], axis=1)
    pos = jnp.arange(seq, dtype=jnp.int32)
    lo = jnp.clip(pos - window // 2, 0, seq)
    hi = jnp.clip(pos - window // 2 + window, 0, seq)
    win_sum = jnp.take(cs, hi, axis=1) - jnp.take(cs, lo, axis=1)
    cnt = (hi - lo).astype(jnp.float32)[None, :, None]
    return (win_sum / cnt - uf).astype(u.dtype)

def pool_mixer(h, pool_map, pool_scale):
    outs = []
    for gi, w in enumerate(POOL_WINDOWS):
        hg = h[..., gi * C_GROUP_DIM:(gi + 1) * C_GROUP_DIM]
        pg = centred_pool_minus_self(hg, w)
        outs.append(pg @ pool_map[gi])
    return jnp.concatenate(outs, axis=-1) * pool_scale

def first_inputs(seed: int = 0) -> dict:
    key = jax.random.key(seed)
    ks = jax.random.split(key, 20)
    f32 = jnp.float32
    nrm = lambda k, shape, fan_in: jax.random.normal(k, shape, f32) * (fan_in ** -0.5)
    gain = lambda k, shape: 1.0 + 0.05 * jax.random.normal(k, shape, f32)
    return {
        "x": jax.random.normal(ks[0], (BATCH, SEQ, D_MODEL), f32),
        "norm_mix_g": gain(ks[1], (DEPTH, D_MODEL)),
        "norm_ffn_g": gain(ks[2], (DEPTH, D_MODEL)),
        "w_in_ab": nrm(ks[3], (N_EVEN, D_MODEL, IN_AB), D_MODEL),
        "fnet_map": nrm(ks[4], (N_EVEN, A_HEADS, A_HEAD_DIM, A_HEAD_DIM), A_HEAD_DIM),
        "conv_w": nrm(ks[5], (N_EVEN, CONV_WIDTH, B_WIDTH), CONV_WIDTH),
        "conv_b": 0.02 * jax.random.normal(ks[6], (N_EVEN, B_WIDTH), f32),
        "conv_ln_g": gain(ks[7], (N_EVEN, B_WIDTH)),
        "conv_ln_b": 0.02 * jax.random.normal(ks[8], (N_EVEN, B_WIDTH), f32),
        "w_out_ab": nrm(ks[9], (N_EVEN, MIX_WIDTH, D_MODEL), MIX_WIDTH),
        "pool_map": nrm(ks[10], (N_ODD, C_GROUPS, C_GROUP_DIM, C_GROUP_DIM), C_GROUP_DIM),
        "pool_scale": 1.0 + 0.1 * jax.random.normal(ks[11], (N_ODD, D_MODEL), f32),
        "ffn_w_gate": nrm(ks[12], (DEPTH, D_MODEL, D_FF), D_MODEL),
        "ffn_w_up": nrm(ks[13], (DEPTH, D_MODEL, D_FF), D_MODEL),
        "ffn_w_down": nrm(ks[14], (DEPTH, D_FF, D_MODEL), D_FF),
        "final_g": gain(ks[15], (D_MODEL,)),
    }

def first_block(x, norm_mix_g, norm_ffn_g, w_in_ab, fnet_map, conv_w, conv_b, conv_ln_g,
              conv_ln_b, w_out_ab, pool_map, pool_scale, ffn_w_gate, ffn_w_up, ffn_w_down,
              final_g):
    for layer in range(DEPTH):
        h = rmsnorm(x, norm_mix_g[layer])
        if layer % 2 == 0:
            e = layer // 2
            p = h @ w_in_ab[e]
            ya = fnet_heads(p[..., :A_WIDTH], fnet_map[e])
            yb = conformer_conv_heads(p[..., A_WIDTH:A_WIDTH + B_WIDTH],
                                      p[..., A_WIDTH + B_WIDTH:],
                                      conv_w[e], conv_b[e], conv_ln_g[e], conv_ln_b[e])
            y = jnp.concatenate([ya, yb], axis=-1) @ w_out_ab[e]
        else:
            o = layer // 2
            y = pool_mixer(h, pool_map[o], pool_scale[o])
        x = x + y
        h = rmsnorm(x, norm_ffn_g[layer])
        x = x + swiglu_ffn(h, ffn_w_gate[layer], ffn_w_up[layer], ffn_w_down[layer])
    return rmsnorm(x, final_g)


GRID_W = 64
CTX_LEN = 256
N_MIXERS = 2
BLOCK = 128
WINDOW = 128
HEAD_DIM = 64
A_HEADS_2 = D_MODEL // HEAD_DIM
A_KV_HEADS = max(1, A_HEADS_2 // 8)
B_HEADS_2 = D_MODEL // (2 * HEAD_DIM)
D_FF_2 = 4 * D_MODEL
N_MOD = 6
ROPE_BASE = 10000.0
SUBLN_EPS = 1e-5
NEG_INF = -1e30
DEEPNORM_ALPHA = (2 * DEPTH) ** 0.25
DEEPNORM_BETA = (8 * DEPTH) ** -0.25
N_A_LAYERS = (DEPTH + 1) // 2
N_B_LAYERS = DEPTH // 2


def layer_norm(x, g, b):
    x32 = x.astype(jnp.float32)
    mu = jnp.mean(x32, axis=-1, keepdims=True)
    var = jnp.mean(jnp.square(x32 - mu), axis=-1, keepdims=True)
    return ((x32 - mu) * lax.rsqrt(var + LN_EPS) * g + b).astype(x.dtype)

def axial_rope_tables(L):
    rows = L // GRID_W
    row = jnp.repeat(jnp.arange(rows, dtype=jnp.float32), GRID_W)
    col = jnp.tile(jnp.arange(GRID_W, dtype=jnp.float32), rows)
    n_freq = HEAD_DIM // 4
    inv = ROPE_BASE ** (-jnp.arange(n_freq, dtype=jnp.float32) / n_freq)
    ang = jnp.concatenate([row[:, None] * inv, col[:, None] * inv], axis=-1)
    return jnp.cos(ang), jnp.sin(ang)

def apply_rope(x, cos, sin):
    L = x.shape[1]
    shp = (1, L) + (1,) * (x.ndim - 3) + (HEAD_DIM // 2,)
    cs = cos.reshape(shp).astype(x.dtype)
    sn = sin.reshape(shp).astype(x.dtype)
    x1, x2 = jnp.split(x, 2, axis=-1)
    return jnp.concatenate([x1 * cs - x2 * sn, x1 * sn + x2 * cs], axis=-1)

def softmax_with_sink(s, sink):
    m = jnp.maximum(jnp.max(s, axis=-1, keepdims=True), sink)
    p = jnp.exp(s - m)
    return p / (jnp.sum(p, axis=-1, keepdims=True) + jnp.exp(sink - m))

def window_gqa(hx, hc, wq, wk, wv, wo, sink, cos, sin, need_ctx):
    B, L, _ = hx.shape
    C = hc.shape[1]
    G = A_HEADS_2 // A_KV_HEADS
    nb = L // BLOCK
    scale = HEAD_DIM ** -0.5
    q = apply_rope((hx @ wq).reshape(B, L, A_KV_HEADS, G, HEAD_DIM), cos, sin)
    k = apply_rope((hx @ wk).reshape(B, L, A_KV_HEADS, HEAD_DIM), cos, sin)
    v = (hx @ wv).reshape(B, L, A_KV_HEADS, HEAD_DIM)
    kc = (hc @ wk).reshape(B, C, A_KV_HEADS, HEAD_DIM)
    vc = (hc @ wv).reshape(B, C, A_KV_HEADS, HEAD_DIM)
    sink_f = sink.astype(jnp.float32).reshape(A_KV_HEADS, G, 1, 1)
    pad = ((0, 0), (BLOCK, BLOCK), (0, 0), (0, 0))
    kp = jnp.pad(k, pad)
    vp = jnp.pad(v, pad)
    qb = jnp.moveaxis(q.reshape(B, nb, BLOCK, A_KV_HEADS, G, HEAD_DIM), 1, 0)
    qi = jnp.arange(BLOCK)[:, None]
    kj = jnp.arange(3 * BLOCK)[None, :]
    rel = qi + BLOCK - kj

    def block_fn(args):
        n, qblk = args
        kblk = lax.dynamic_slice_in_dim(kp, n * BLOCK, 3 * BLOCK, axis=1)
        vblk = lax.dynamic_slice_in_dim(vp, n * BLOCK, 3 * BLOCK, axis=1)
        kpos = n * BLOCK - BLOCK + kj
        valid = (jnp.abs(rel) <= WINDOW) & (kpos >= 0) & (kpos < L)
        s_lat = jnp.einsum('bqhgd,bkhd->bhgqk', qblk, kblk).astype(jnp.float32) * scale
        s_lat = jnp.where(valid, s_lat, NEG_INF)
        s_ctx = jnp.einsum('bqhgd,bchd->bhgqc', qblk, kc).astype(jnp.float32) * scale
        p = softmax_with_sink(jnp.concatenate([s_lat, s_ctx], axis=-1), sink_f).astype(v.dtype)
        o = jnp.einsum('bhgqk,bkhd->bqhgd', p[..., :3 * BLOCK], vblk)
        return o + jnp.einsum('bhgqc,bchd->bqhgd', p[..., 3 * BLOCK:], vc)

    ob = lax.map(block_fn, (jnp.arange(nb), qb))
    out_x = jnp.moveaxis(ob, 0, 1).reshape(B, L, A_HEADS_2 * HEAD_DIM) @ wo
    out_c = None
    if need_ctx:
        qc = (hc @ wq).reshape(B, C, A_KV_HEADS, G, HEAD_DIM)
        s = jnp.einsum('bqhgd,bkhd->bhgqk', qc, kc).astype(jnp.float32) * scale
        p = softmax_with_sink(s, sink_f).astype(vc.dtype)
        out_c = jnp.einsum('bhgqk,bkhd->bqhgd', p, vc).reshape(B, C, A_HEADS_2 * HEAD_DIM) @ wo
    return out_x, out_c

def diff_attention(hx, hc, wq, wk, wv, wo, lq1, lk1, lq2, lk2, subln_g, lam_init, cos, sin, need_ctx):
    B, L, _ = hx.shape
    C = hc.shape[1]
    H, d = B_HEADS_2, HEAD_DIM
    nb = L // BLOCK
    scale = d ** -0.5
    q = apply_rope((hx @ wq).reshape(B, L, H, 2, d), cos, sin)
    k = apply_rope((hx @ wk).reshape(B, L, H, 2, d), cos, sin)
    v = (hx @ wv).reshape(B, L, H, 2 * d)
    kc = (hc @ wk).reshape(B, C, H, 2, d)
    vc = (hc @ wv).reshape(B, C, H, 2 * d)
    lam = (jnp.exp(jnp.sum((lq1 * lk1).astype(jnp.float32)))
           - jnp.exp(jnp.sum((lq2 * lk2).astype(jnp.float32))) + lam_init)
    k_all = jnp.concatenate([k, kc], axis=1)
    v_all = jnp.concatenate([v, vc], axis=1)

    def diff_weights(qblk, keys):
        s = jnp.einsum('bqhtd,bkhtd->bhtqk', qblk, keys).astype(jnp.float32) * scale
        p = jax.nn.softmax(s, axis=-1)
        return p[:, :, 0] - lam * p[:, :, 1]

    def block_fn(qblk):
        a = diff_weights(qblk, k_all).astype(v.dtype)
        return jnp.einsum('bhqk,bkhe->bqhe', a, v_all)

    qb = jnp.moveaxis(q.reshape(B, nb, BLOCK, H, 2, d), 1, 0)
    ob = lax.map(block_fn, qb)
    ox = jnp.moveaxis(ob, 0, 1).reshape(B, L, H, 2 * d)

    def head_out(o):
        n = o.shape[1]
        o32 = o.astype(jnp.float32)
        o32 = o32 * lax.rsqrt(jnp.mean(jnp.square(o32), axis=-1, keepdims=True) + SUBLN_EPS)
        o32 = o32 * subln_g * (1.0 - lam_init)
        return o32.astype(o.dtype).reshape(B, n, H * 2 * d) @ wo

    out_x = head_out(ox)
    out_c = None
    if need_ctx:
        qc = (hc @ wq).reshape(B, C, H, 2, d)
        a = diff_weights(qc, kc).astype(vc.dtype)
        out_c = head_out(jnp.einsum('bhqk,bkhe->bqhe', a, vc))
    return out_x, out_c

def sqrelu_mlp(h, w1, w2):
    return jnp.square(jax.nn.relu(h @ w1)) @ w2

def second_inputs(seed: int = 0) -> dict:
    key = jax.random.key(seed)
    ks = jax.random.split(key, 32)
    D = D_MODEL
    f32 = jnp.float32

    def nrm(k, shape, fan_in, gain=1.0):
        return jax.random.normal(k, shape, f32) * (gain * fan_in ** -0.5)

    def small(k, shape, s):
        return jax.random.normal(k, shape, f32) * s

    return {
        'x': jax.random.normal(ks[0], (BATCH, SEQ, D), f32),
        'c': jax.random.normal(ks[1], (BATCH, D), f32),
        'ctx': jax.random.normal(ks[2], (BATCH, CTX_LEN, D), f32),
        'c_ctx': jax.random.normal(ks[3], (D,), f32),
        'w_ada': nrm(ks[4], (DEPTH, D, N_MOD * D), D, 0.5),
        'b_ada': small(ks[5], (DEPTH, N_MOD * D), 0.02),
        'ln1_g': 1.0 + small(ks[6], (DEPTH, D), 0.05),
        'ln1_b': small(ks[7], (DEPTH, D), 0.02),
        'ln2_g': 1.0 + small(ks[8], (DEPTH, D), 0.05),
        'ln2_b': small(ks[9], (DEPTH, D), 0.02),
        'a_wq': nrm(ks[10], (N_A_LAYERS, D, A_HEADS_2 * HEAD_DIM), D),
        'a_wk': nrm(ks[11], (N_A_LAYERS, D, A_KV_HEADS * HEAD_DIM), D),
        'a_wv': nrm(ks[12], (N_A_LAYERS, D, A_KV_HEADS * HEAD_DIM), D),
        'a_wo': nrm(ks[13], (N_A_LAYERS, A_HEADS_2 * HEAD_DIM, D), A_HEADS_2 * HEAD_DIM, DEEPNORM_BETA),
        'a_sink': small(ks[14], (N_A_LAYERS, A_HEADS_2), 1.0),
        'b_wq': nrm(ks[15], (N_B_LAYERS, D, B_HEADS_2 * 2 * HEAD_DIM), D),
        'b_wk': nrm(ks[16], (N_B_LAYERS, D, B_HEADS_2 * 2 * HEAD_DIM), D),
        'b_wv': nrm(ks[17], (N_B_LAYERS, D, B_HEADS_2 * 2 * HEAD_DIM), D),
        'b_wo': nrm(ks[18], (N_B_LAYERS, B_HEADS_2 * 2 * HEAD_DIM, D), B_HEADS_2 * 2 * HEAD_DIM, DEEPNORM_BETA),
        'b_lq1': small(ks[19], (N_B_LAYERS, HEAD_DIM), 0.1),
        'b_lk1': small(ks[20], (N_B_LAYERS, HEAD_DIM), 0.1),
        'b_lq2': small(ks[21], (N_B_LAYERS, HEAD_DIM), 0.1),
        'b_lk2': small(ks[22], (N_B_LAYERS, HEAD_DIM), 0.1),
        'b_subln_g': 1.0 + small(ks[23], (N_B_LAYERS, 2 * HEAD_DIM), 0.05),
        'mlp_w1': nrm(ks[24], (DEPTH, D, D_FF_2), D),
        'mlp_w2': nrm(ks[25], (DEPTH, D_FF_2, D), D_FF_2, DEEPNORM_BETA),
    }

def second_block(x, c, ctx, c_ctx, w_ada, b_ada, ln1_g, ln1_b, ln2_g, ln2_b,
              a_wq, a_wk, a_wv, a_wo, a_sink,
              b_wq, b_wk, b_wv, b_wo, b_lq1, b_lk1, b_lq2, b_lk2, b_subln_g,
              mlp_w1, mlp_w2):
    L = x.shape[1]
    cos, sin = axial_rope_tables(L)
    alpha = DEEPNORM_ALPHA
    for i in range(DEPTH):
        need_ctx = i < DEPTH - 1
        mod_x = jax.nn.silu(c) @ w_ada[i] + b_ada[i]
        mod_c = jax.nn.silu(c_ctx) @ w_ada[i] + b_ada[i]
        sh1, sc1, g1, sh2, sc2, g2 = jnp.split(mod_x[:, None, :], N_MOD, axis=-1)
        csh1, csc1, cg1, csh2, csc2, cg2 = jnp.split(mod_c, N_MOD, axis=-1)
        hx = x * (1.0 + sc1) + sh1
        hc = ctx * (1.0 + csc1) + csh1
        j = i // N_MIXERS
        if i % N_MIXERS == 0:
            ax, ac = window_gqa(hx, hc, a_wq[j], a_wk[j], a_wv[j], a_wo[j], a_sink[j], cos, sin, need_ctx)
        else:
            lam_init = 0.8 - 0.6 * math.exp(-0.3 * i)
            ax, ac = diff_attention(hx, hc, b_wq[j], b_wk[j], b_wv[j], b_wo[j],
                                    b_lq1[j], b_lk1[j], b_lq2[j], b_lk2[j], b_subln_g[j],
                                    lam_init, cos, sin, need_ctx)
        x = layer_norm(alpha * x + g1 * ax, ln1_g[i], ln1_b[i])
        fx = sqrelu_mlp(x * (1.0 + sc2) + sh2, mlp_w1[i], mlp_w2[i])
        x = layer_norm(alpha * x + g2 * fx, ln2_g[i], ln2_b[i])
        if need_ctx:
            ctx = layer_norm(alpha * ctx + cg1 * ac, ln1_g[i], ln1_b[i])
            fc = sqrelu_mlp(ctx * (1.0 + csc2) + csh2, mlp_w1[i], mlp_w2[i])
            ctx = layer_norm(alpha * ctx + cg2 * fc, ln2_g[i], ln2_b[i])
    return x


def setup_inputs(seed=0):
    out = dict(first_inputs(seed))
    for name, value in second_inputs(seed + 1).items():
        if name != "x":
            out[name + "_2"] = value
    return out


def reference(
    x, norm_mix_g, norm_ffn_g, w_in_ab, fnet_map, conv_w, conv_b, conv_ln_g, conv_ln_b,
    w_out_ab, pool_map, pool_scale, ffn_w_gate, ffn_w_up, ffn_w_down, final_g, c_2, ctx_2,
    c_ctx_2, w_ada_2, b_ada_2, ln1_g_2, ln1_b_2, ln2_g_2, ln2_b_2, a_wq_2, a_wk_2, a_wv_2,
    a_wo_2, a_sink_2, b_wq_2, b_wk_2, b_wv_2, b_wo_2, b_lq1_2, b_lk1_2, b_lq2_2, b_lk2_2,
    b_subln_g_2, mlp_w1_2, mlp_w2_2,
):
    x = first_block(
        x, norm_mix_g, norm_ffn_g, w_in_ab, fnet_map, conv_w, conv_b, conv_ln_g, conv_ln_b,
        w_out_ab, pool_map, pool_scale, ffn_w_gate, ffn_w_up, ffn_w_down, final_g,
    )
    return second_block(
        x, c_2, ctx_2, c_ctx_2, w_ada_2, b_ada_2, ln1_g_2, ln1_b_2, ln2_g_2, ln2_b_2, a_wq_2,
        a_wk_2, a_wv_2, a_wo_2, a_sink_2, b_wq_2, b_wk_2, b_wv_2, b_wo_2, b_lq1_2, b_lk1_2,
        b_lq2_2, b_lk2_2, b_subln_g_2, mlp_w1_2, mlp_w2_2,
    )


_drawn_inputs = setup_inputs


def setup_inputs(seed=0):
    import zlib

    import numpy as np

    out = dict(_drawn_inputs(seed))
    spreads = {}
    factors = {'conv_b': 3.7,
     'conv_ln_b': 7.282,
     'ctx_2': 3.409,
     'b_ada_2': 3.13,
     'a_wq_2': 5.403,
     'a_wk_2': 5.316,
     'a_sink_2': 8.0,
     'b_lq1_2': 64.0,
     'b_lk1_2': 64.0,
     'b_lq2_2': 8.0,
     'b_lk2_2': 64.0,
     'b_subln_g_2': 8.0}
    for name, (base, spread) in spreads.items():
        noise = np.random.default_rng([zlib.crc32(name.encode()), seed]).standard_normal(out[name].shape)
        drawn = base * np.exp(spread * noise) if base else spread * noise
        out[name] = __import__('jax').numpy.asarray(drawn.astype(out[name].dtype))
    for name, factor in factors.items():
        out[name] = (out[name] * factor).astype(out[name].dtype)
    return out
```

```python
import math
from contextlib import ExitStack

import numpy as np

import concourse.bass as bass
import concourse.mybir as mybir

F32 = mybir.dt.float32
F32R = mybir.dt.float32r
ALU = mybir.AluOpType
ACT = mybir.ActivationFunctionType
AX_X = mybir.AxisListType.X

P = 128
D = 1024
KT = D // P
T = 512
C = 256
TT = T + C
BLK = 2048
QT = T // P
NTT = TT // P
DH = 64
HEADS_A = 4
TAPS = 31
PADC = TAPS // 2
UP = T + 2 * PADC
PADP = 8
HPAD = T + 2 * PADP
D_FF = 2816
FF_IT = D_FF // 256
D_FF2 = 4096
ML_IT = D_FF2 // 256
N_MOD = 6
ADA_PAIRS = N_MOD * D // 512
RMS_EPS = 1e-6
LN_EPS = 1e-5
N_SMALL = 8
ALPHA = 4.0 ** 0.25
LAM_INIT = 0.8 - 0.6 * math.exp(-0.3)
SCALE = DH ** -0.5
NEG = -1e30
SUB_SCALE = 2.0 ** -40
SUB_CLAMP = 2.0 ** 30
SUB_OVER = 2.0 ** 48

X_ONLY = [(0, T)]
X_CTX = [(0, T), (T, C)]

B_WIN = 0
B_WOUT = B_WIN + 6
FF_BLOCKS = 5 * FF_IT + 2
B_FF = [B_WOUT + 4, B_WOUT + 4 + FF_BLOCKS + 1]
B_POOL = B_FF[0] + FF_BLOCKS
B_KV = B_FF[1] + FF_BLOCKS
B_WQA = B_KV + 2
B_WOA = B_WQA + 4
ML_BLOCKS = 2 * ML_IT
B_ML0 = B_WOA + 4
B_QKV = B_ML0 + ML_BLOCKS
B_WOB = B_QKV + 12
B_ML1 = B_WOB + 4
N_BLOCKS = B_ML1 + ML_BLOCKS
B_ML = [B_ML0, B_ML1]

_cols = {}
_n = 0
for _name, _w in [
    ("mix_g", 2 * KT), ("ffn_g", 2 * KT), ("conv_w", 4 * TAPS), ("conv_b", 4), ("conv_ln_g", 4), ("conv_ln_b", 4),
    ("pool_scale", KT), ("final_g", KT), ("b_ada", 2 * 48 * 2), ("ln1_g", 2 * KT), ("ln1_b", 2 * KT),
    ("ln2_g", 2 * KT), ("ln2_b", 2 * KT), ("sink", 16), ("subln_g", 1), ("lq1", 64), ("lk1", 64), ("lq2", 64),
    ("lk2", 64), ("c", KT * 2),
]:
    _cols[_name] = (_n, _n + _w)
    _n += _w
N_VEC = _n


def build(nc, ins, out):
    ctx = ExitStack()
    with ctx:
        def sb(name, shape, dt=F32):
            return ctx.enter_context(nc.sbuf_tensor(name, shape, dt))

        shared = {}

        def share(signal, phases):
            before = 0
            for phase, n in phases.items():
                shared[f"{phase}_{signal}"] = (signal, before)
                before += n

        rms_split, with_ctx = ["n1", "n2", "n4"], ["l1", "l2"]
        norms = ["n1", "n2", "n3", "n4", "n5", "l1", "l2", "l3", "l4"]
        tiles = {n: KT for n in norms}
        share("sq", tiles)
        share("sum", tiles)
        share("std", {n: 2 if n in with_ctx else 1 for n in norms})
        share("rstd", {n: 1 for n in norms})
        share("y", {n: KT for n in norms if n != "n3"})
        for signal in ("hi", "out"):
            share(signal, {n: KT for n in norms if n not in ("n3", "l4")})
        share("m", {"n5": 2 * KT, "l1": 2 * KT, "l2": 2 * KT, "l3": KT})
        share("mu", {n: 1 for n in norms[5:]})
        share("d", {"l1": 2 * KT, "l2": 2 * KT, "l3": KT, "l4": KT})
        share("res", {"n5": 2 * KT, "l1": KT, "l2": KT, "l3": KT, "l4": KT})
        for kind, steps in (("ff", FF_IT), ("ml", ML_IT)):
            pair = (kind + "0", kind + "1")
            for signal in ("silu" if kind == "ff" else "relu", "mul", "hi", "h"):
                for n, phase in enumerate(pair):
                    shared[f"{phase}_{signal}"] = (f"{kind}_{signal}", 2 * steps * n)
            for n, phase in enumerate(pair):
                shared[f"{phase}_up"] = (f"{kind}_up", (2 if kind == "ff" else 1) * steps * n)
                shared[f"{phase}_down"] = (f"{kind}_down", (KT - 1) * steps * n)
                shared[f"{phase}_dfree"] = (f"{kind}_dfree", (KT * steps + 8) * n)
        for n in range(2):
            shared[f"ff{n}_ada"] = ("ada", ADA_PAIRS * n)
            shared[f"ff{n}_sel"] = ("ada_sel", ADA_PAIRS * n)
            shared[f"ff{n}_arow"] = ("ada_row", 2 * ADA_PAIRS * n)
        sems = {}

        def sem(name):
            name = shared.get(name, (name, 0))[0]
            if name not in sems:
                sems[name] = ctx.enter_context(nc.semaphore(name))
            return sems[name]

        def when(name, count):
            return sem(name), count + shared.get(name, (name, 0))[1]

        X = sb("X", [P, KT, TT])
        Ahi = sb("Ahi", [P, KT, TT], F32R)
        Alo = sb("Alo", [P, KT, TT], F32R)
        raw = sb("raw", [P, 2, BLK])
        whi = sb("whi", [P, 2, BLK], F32R)
        wlo = sb("wlo", [P, 2, BLK], F32R)
        tmp = sb("tmp", [P, 4, TT])
        std = sb("std", [P, TT])
        rstd = sb("rstd", [P, TT])
        vec = sb("vec", [P, N_VEC])
        ident = sb("ident", [P, P])
        ones = sb("ones", [P, P])
        epsr = sb("epsr", [P, 3])
        modT = sb("modT", [P, 2, N_MOD * KT, 2])
        s1 = sb("s1", [P, 4, KT, 2])
        s2 = sb("s2", [P, 4, KT, 2])
        csil = sb("csil", [P, KT, 2])
        sel4 = sb("sel4", [4, 2])
        lamt = sb("lamt", [P, 8])
        sm = sb("sm", [P, 2, 8])
        ARENA = 16128
        arena = sb("arena", [P, ARENA])
        arena_at = nc.sbuf_base - 4 * ARENA

        def carve(at, *shape):
            n = int(np.prod(shape))
            assert at + n <= ARENA, (at, shape)
            a = arena[:, at:at + n]
            if len(shape) == 2:
                a = a.rearrange("p (a b) -> p a b", a=shape[0])
            if len(shape) == 3:
                a = a.rearrange("p (a b c) -> p a b c", a=shape[0], b=shape[1])
            return a, at + n

        hhi = nc.alloc_sbuf_tensor_at("hhi", [P, 2, 2, TT], F32R, offset=arena_at)
        hlo = nc.alloc_sbuf_tensor_at("hlo", [P, 2, 2, TT], F32R, offset=arena_at + 4 * 4 * TT)
        H_END = 8 * TT
        c4 = nc.alloc_sbuf_tensor_at("c4", [P, KT, P], F32R, offset=arena_at + 4 * (ARENA - KT * P))
        modin, MODIN_END = carve(H_END, 2, TT)
        dft, at = carve(0, 2, QT, T)
        upad, at = carve(at, 4, UP)
        conv, at = carve(at, 4, T)
        pf, at = carve(at, 4, T)
        zz, at = carve(at, 2, QT * 256)
        csd, at = carve(at, 256)
        fmap, at = carve(at, 4 * P)
        csm, at = carve(at, 4, 256)
        assert at <= ARENA - KT * P
        icnt, at = carve(H_END, 4, T)
        hp, at = carve(at, KT, HPAD)
        pa, at = carve(at, 2, HPAD)
        pb, at = carve(at, 2, HPAD)
        arow, at = carve(at, 2, 256)
        arow = arow[0:4]
        assert at <= ARENA - KT * P
        O, at = carve(0, KT, TT)
        assert at == H_END
        cosq, at = carve(MODIN_END, T)
        sinq, at = carve(at, T)
        maskl, at = carve(at, P)
        maskr, base = carve(at, P)
        swap = tmp[:, 0, 0:T]
        vT = tmp[:, 1, :]
        kcur = tmp[:, 1, :]
        probA = tmp[:, 2:4, 0:640]
        kd, at = carve(base, 2, TT)
        vA, at = carve(at, NTT, P)
        vcur, at = carve(at, NTT, DH)
        qA, at = carve(at, 2, TT)
        ptA, at = carve(at, 5, T)
        qB, at = carve(base, 2, T)
        kB, at = carve(at, 2, TT)
        vB, at = carve(at, NTT, 256)
        aT, at = carve(at, NTT, T)
        ps = ctx.enter_context(nc.psum_tensor("ps", [P, 8, 512], F32))
        psf = ps[:, :, :].rearrange("p b n -> p (b n)")

        def window(n):
            return (max(0, n - 1), min(QT, n + 2)) if n < QT else (0, 0)

        def keys(n):
            return [*range(*window(n)), *range(QT, NTT)]

        def v(name, i, n=1):
            a = _cols[name][0] + i
            return vec[:, a:a + n]

        def mod(layer, which, k, src):
            return modT[:, layer, which * KT + k, src:src + 1]

        def wl(w, b, off):
            return w[:, b % 2, off:off + P]

        block = ctx.enter_context(nc.Block())

        @block.sync
        def _(sp):
            def load_small(name, dst):
                sp.dma_start(dst, ins[name]).then_inc(sem("small"), 16)

            load_small("xT", X[:, :, 0:T])
            load_small("vec", vec[:, :])
            load_small("ident", ident[:, :])
            load_small("sel4", sel4[:, :])
            sp.dma_start(raw[:, 0, :], ins["stream"][0]).then_inc(sem("raw0"), 16)
            sp.dma_start(raw[:, 1, :], ins["stream"][1]).then_inc(sem("raw1"), 16)
            load_small("ctxT", X[:, :, T:TT])
            load_small("csd", csd)
            load_small("fmap", fmap)
            load_small("dft", dft.rearrange("p a b c -> p (a b c)"))
            with sp.Fori(1, N_BLOCKS // 2) as i:
                for s in range(2):
                    sp.wait_ge(*when("w_split", 2 * i + s - 1))
                    sp.dma_start(raw[:, s, :], ins["stream"][2 * i + s]).then_inc(sem(f"raw{s}"), 16)
            for b in range(N_BLOCKS // 2 * 2, N_BLOCKS):
                sp.wait_ge(*when("w_split", b - 1))
                sp.dma_start(raw[:, b % 2, :], ins["stream"][b]).then_inc(sem(f"raw{b % 2}"), 16)

            for h in range(2):
                sp.wait_ge(*when("l4_res", 4 * h + 4))
                sp.dma_start(out[:, 4 * h:4 * h + 4, :], X[:, 4 * h:4 * h + 4, 0:T]).then_inc(sem("stored"), 16)
            sp.wait_ge(*when("stored", 32))

        @block.gpsimd
        def _(pool):
            def split(s, loaded, used, nth):
                pool.wait_ge(*when(f"raw{s}", loaded))
                if used is not None:
                    pool.wait_ge(*when("w_used", used))
                pool.sem_inc(sem("w_turn"), 1)
                pool.tensor_scalar(whi[:, s, :], raw[:, s, :], 1.0, 1.0, ALU.mult, ALU.mult).then_inc(sem("w_hi"), 1)
                pool.wait_ge(*when("w_hi", nth))
                pool.tensor_tensor(wlo[:, s, :], raw[:, s, :], whi[:, s, :], ALU.subtract).then_inc(sem("w_split"), 1)

            for s in range(2):
                split(s, 16, None, s + 1)
            with pool.Fori(1, N_BLOCKS // 2) as i:
                for s in range(2):
                    split(s, 16 * i + 16, 2 * i + s - 1, 2 * i + s + 1)
            for b in range(N_BLOCKS // 2 * 2, N_BLOCKS):
                split(b % 2, 16 * (b // 2) + 16, b - 1, b + 1)

        @block.tensor
        def _(pe):
            def gemm(dst, lhs_off, b, kn, rhs, cols, rhs_ready=None):
                mm = None
                for k in range(kn):
                    if rhs_ready:
                        rhs_ready(k)
                    for w, part in ((whi, 0), (whi, 1), (wlo, 0)):
                        for c, (c0, n) in enumerate(cols):
                            mm = pe.matmul(dst[c], wl(w, b, lhs_off(k)), rhs(k, part, c0, n),
                                           start=(k == 0 and w is whi and part == 0),
                                           stop=(k == kn - 1 and w is wlo))
                return mm

            def a_rhs(k, part, c0, n):
                return (Ahi, Alo)[part][:, k, c0:c0 + n]

            def h_rhs(slot):
                return lambda k, part, c0, n: (hhi, hlo)[part][:, slot, k, c0:c0 + n]

            def on_tile(name):
                return lambda k: pe.wait_ge(*when(name, k + 1))

            def column_sums(name, bank, cols, src, src_ready):
                for k in range(KT):
                    pe.wait_ge(*when(src_ready, k + 1))
                    for c, (c0, n) in enumerate(cols):
                        mm = pe.matmul(ps[:, bank + c, 0:n], ones[:, :], src(k)[:, c0:c0 + n],
                                       start=(k == 0), stop=(k == KT - 1))
                    mm.then_inc(sem(name), 1)

            def squares(k):
                return tmp[:, k % 4, :]

            def rms(name, bank):
                column_sums(f"{name}_sum", bank, X_ONLY, squares, f"{name}_sq")

            def layernorm(name, cols, bank, x_ready, x_before):
                for k in range(KT):
                    pe.wait_ge(*when(x_ready, x_before + k + 1))
                    for c, (c0, n) in enumerate(cols):
                        mm = pe.matmul(ps[:, bank + c, 0:n], ones[:, :], X[:, k, c0:c0 + n],
                                       start=(k == 0), stop=(k == KT - 1))
                mm.then_inc(sem(f"{name}_mu"), 1)
                column_sums(f"{name}_sum", bank + 2, cols, squares, f"{name}_sq")

            def done(mm, name, ends_block):
                mm.then_inc(sem("w_used" if ends_block else name), 1)

            def dense(name, b0, n_jobs, cols, ready, banks=4):
                for j in range(n_jobs):
                    b = b0 + j // 2
                    if j % 2 == 0:
                        pe.wait_ge(*when("w_split", b + 1))
                    if j >= banks:
                        pe.wait_ge(*when(f"{name}_evac", j - banks + 1))
                    dst = [ps[:, (j % banks) * len(cols) + c, 0:n] for c, (_, n) in enumerate(cols)]
                    mm = gemm(dst, lambda k: k * 256 + (j % 2) * P, b, KT, a_rhs, cols, on_tile(ready) if j == 0 else None)
                    done(mm, f"{name}_done", j % 2 == 1)

            pe.wait_ge(*when("setup", 1))
            pe.wait_ge(*when("small", 16 * N_SMALL))
            for c in range(2):
                mm = pe.matmul(ps[:, 4 + c, :], csd[:, c * P:(c + 1) * P], fmap, start=True, stop=True)
            mm.then_inc(sem("csm_done"), 1)
            rms("n1", 0)
            for j in range(12):
                if j % 2 == 0:
                    pe.wait_ge(*when("w_split", B_WIN + j // 2 + 1))
                if j == 0:
                    pe.wait_ge(*when("n1_std", 1))
                if j >= 4:
                    pe.wait_ge(*when("u", (1, 2, 2, 2, 3, 4, 4, 4)[j - 4]))
                mm = gemm([ps[:, j % 4, :]], lambda k: k * 256 + (j % 2) * P, B_WIN + j // 2, KT, a_rhs, X_ONLY,
                          on_tile("n1_out") if j == 0 else None)
                done(mm, "win_done", j % 2 == 1)
            for h in range(HEADS_A):
                pe.wait_ge(*when("pf", h + 1))
                if h == 0:
                    pe.wait_ge(*when("csm", 2))
                else:
                    if h >= 2:
                        pe.wait_ge(*when("z", h - 1))
                zb = (4 + 2 * (h % 2)) * 512
                for t in range(QT):
                    mm = pe.matmul(psf[:, zb + t * 256:zb + (t + 1) * 256], pf[:, h, t * P:(t + 1) * P], csm[:, h, :],
                                   start=True, stop=True)
                mm.then_inc(sem("z_done"), 1)
            for h in range(HEADS_A):
                pe.wait_ge(*when("z", h + 1))
                for t in range(QT):
                    for c in range(2):
                        mm = pe.matmul(ps[:, h, :], zz[:, h % 2, t * 256 + c * P:t * 256 + (c + 1) * P], dft[:, c, t, :],
                                       start=(t == 0 and c == 0), stop=(t == QT - 1 and c == 1))
                mm.then_inc(sem("y_done"), 1)
            for h in range(4):
                pe.wait_ge(*when("conv", h + 1))
                pe.matmul(ps[:, 4 + h, :], ones[:, :], conv[:, h, :], start=True, stop=True).then_inc(sem("cmu"), 1)
            for h in range(4):
                pe.wait_ge(*when("csq", h + 1))
                if h == 0:
                    pe.wait_ge(*when("mix_out", 4))
                pe.matmul(ps[:, h, :], ones[:, :], tmp[:, h, 0:T], start=True, stop=True).then_inc(sem("cvar"), 1)
            pe.wait_ge(*when("cstd", 4))
            dense("wout", B_WOUT, 8, X_ONLY, "mix_out")

            def ada(b, slot, e):
                pe.wait_ge(*when("w_split", b + 1))
                for k in range(KT):
                    for w in (whi, wlo):
                        mm = pe.matmul(ps[:, 6 + e, 0:256], c4[:, k, :], w[:, slot, k * 256:(k + 1) * 256],
                                       start=(k == 0 and w is whi), stop=(k == KT - 1 and w is wlo))
                mm.then_inc(sem("w_used"), 1)

            def ada_select(name, pairs):
                pe.wait_ge(*when(f"{name}_arow", 2 * pairs))
                for j in range(4):
                    mm = pe.matmul(ps[:, 6, 2 * j:2 * j + 2], arow[0:4, j // 2, (j % 2) * P:(j % 2 + 1) * P],
                                   sel4[:, :], start=True, stop=True)
                mm.then_inc(sem(f"{name}_sel"), 1)

            def swiglu(f, name, ready):
                B0 = B_FF[f]

                def up(i, b_g, at, first):
                    for part in range(2):
                        pe.wait_ge(*when("w_split", b_g + part + 1))
                        for j in range(2):
                            if not first:
                                pe.wait_ge(*when(f"{name}_silu" if part == 0 else f"{name}_mul", 2 * i + j - 1))
                            mm = gemm([ps[:, 2 * part + j, :]], lambda k: k * 256 + j * P, at + part, KT, a_rhs, X_ONLY,
                                      on_tile(ready) if first and part + j == 0 else None)
                            done(mm, f"{name}_up", j == 1)
                        if part == 0:
                            ada_select(name, i + 1)

                def down(i, b_d, at, slot):
                    pe.wait_ge(*when("w_split", b_d + 1))
                    pe.wait_ge(*when(f"{name}_h", 2 * i + 2))
                    for m in range(KT):
                        pe.wait_ge(*when(f"{name}_dfree", 8 * i + m + 7))
                        mm = gemm([ps[:, 4 + m % 2, :]], lambda k: k * D + m * P, at, 2, h_rhs(slot), X_ONLY)
                        done(mm, f"{name}_down", m == KT - 1)

                for e in range(2):
                    ada(B0 + e, (B0 + e) % 2, e)
                up(0, B0 + 2, B0 + 2, True)
                with pe.Fori(0, (FF_IT - 1) // 2) as p:
                    for half in range(2):
                        i = 2 * p + half
                        at = B0 + 4 + 5 * half
                        b = 10 * p + at
                        pe.wait_ge(*when(f"{name}_ada", i + 1))
                        for e in range(2):
                            ada(b + e, (at + e) % 2, e)
                        up(i + 1, b + 2, at + 2, False)
                        down(i, b + 4, at + 4, half)
                i = FF_IT - 1
                b = B0 + 4 + 5 * i
                pe.wait_ge(*when(f"{name}_ada", i + 1))
                for e in range(2):
                    ada(b + e, (b + e) % 2, e)
                ada_select(name, i + 2)
                down(i, b + 2, b + 2, i % 2)

            rms("n2", 5)
            pe.wait_ge(*when("c4", 3))
            swiglu(0, "ff0", "n2_out")
            rms("n3", 0)
            pe.wait_ge(*when("w_split", B_POOL + 1))
            for g in range(4):
                pe.wait_ge(*when("pool_in", g + 1))
                for m in range(2):
                    j = 2 * g + m
                    if j >= 4:
                        pe.wait_ge(*when("pool_evac", j - 3))
                    mm = gemm([ps[:, 4 + j % 4, :]], lambda k: k * D + g * 256 + m * P, B_POOL, 2,
                              lambda k, part, c0, n: a_rhs(2 * g + k, part, c0, n), X_ONLY)
                    done(mm, "pool_done", j == 7)
            rms("n4", 0)
            swiglu(1, "ff1", "n4_out")
            rms("n5", 0)

            for j in range(3):
                b = B_KV + j // 2
                if j != 1:
                    pe.wait_ge(*when("w_split", b + 1))
                if j == 2:
                    pe.wait_ge(*when("kvA_evac", 1))
                dst = [ps[:, 4 + 2 * (j % 2) + c, 0:n] for c, (_, n) in enumerate(X_CTX)]
                mm = gemm(dst, lambda k: k * 256 + (j % 2) * P, b, KT, a_rhs, X_CTX, on_tile("n5_out") if j == 0 else None)
                done(mm, "kvA_done", j >= 1)
            pe.wait_ge(*when("kvA_evac", 3))
            for t in range(NTT):
                mm = pe.transpose(psf[:, 4 * 512 + t * P:4 * 512 + (t + 1) * P], vT[:, t * P:(t + 1) * P], ident[:, :])
            mm.then_inc(sem("vA_done"), 1)

            def window_scores(u, tile, half, n):
                rows = slice(DH * half, DH * half + DH)
                q = qA[rows, tile, n * P:(n + 1) * P]
                mid = 2 * (u % 2) * 512 + 512
                first, last = window(n)
                if last > first:
                    a = mid - (last - first) * P
                    ends = [k for k in (first, last - 1) if k != n]
                    pe.matmul(psf[:, a:mid], q, kcur[rows, first * P:last * P], start=True, stop=False, skip_group_check=True)
                    for k in ends:
                        at = a + (k - first) * P
                        pe.matmul(psf[:, at:at + P], ident[:, :], maskl if k < n else maskr, start=False,
                                  stop=(k == ends[-1]), skip_group_check=True)
                return pe.matmul(psf[:, mid:mid + C], q, kcur[rows, T:TT], start=True, stop=True)

            def window_turn(u, n, unit):
                pe.wait_ge(*when("pA", unit + 1))
                pe.wait_ge(*when("ptA", unit + 1))
                for t in range(len(keys(n))):
                    mm = pe.transpose(psf[:, 4 * 512 + t * P:4 * 512 + (t + 1) * P], probA[:, u % 2, t * P:(t + 1) * P],
                                      ident[:, :])
                mm.then_inc(sem("turnA"), 1)

            def window_values(n, unit, nth):
                pe.wait_ge(*when("ptA", unit + 2))
                pe.wait_ge(*when("oA", nth + 1))
                ks = keys(n)
                for t, k in enumerate(ks):
                    mm = pe.matmul(ps[0:DH, 6, :], vcur[:, k, :], ptA[:, t, :], start=(t == 0), stop=(t == len(ks) - 1))
                mm.then_inc(sem("oA_done"), 1)

            pe.sem_inc(sem("turnA"), 2)
            pe.sem_inc(sem("oA_done"), 1)
            with pe.Fori(0, 2) as g:
                for e in range(2):
                    blk = 2 * g + e
                    pe.wait_ge(*when("w_split", blk + B_WQA + 1))
                    pe.wait_ge(*when("oA", 6 * blk + 1))
                    for m in range(2):
                        for c, (c0, n) in enumerate(X_CTX):
                            pe.wait_ge(*when(f"qA_free{c}", 2 * blk + m + 1))
                            mm = gemm([ps[:, 6 + c, 0:n]], lambda k: k * 256 + m * P, B_WQA + e, KT, a_rhs, [(c0, n)])
                            done(mm, "qA_done", m == 1 and c == 1)
                    pe.wait_ge(*when("qA", 2 * blk + 3))
                    pe.wait_ge(*when("qA_free1", 2 * blk + 3))
                    pe.wait_ge(*when("kvcur", 2 * g + 2))
                    units = [(n, h) for n in range(NTT) for h in range(4)]
                    for u, (n, h) in enumerate(units):
                        unit = 24 * blk + u
                        pe.wait_ge(*when("sA_free", unit + 1))
                        window_scores(u, h // 2, h % 2, n).then_inc(sem("sA"), 1)
                        if u >= 1:
                            window_turn(u - 1, units[u - 1][0], unit - 1)
                        if u >= 2 and units[u - 2][1] == 3:
                            window_values(units[u - 2][0], unit - 2, 6 * blk + units[u - 2][0])
                    window_turn(23, NTT - 1, 24 * blk + 23)
                    window_values(NTT - 1, 24 * blk + 23, 6 * blk + NTT - 1)
            dense("woA", B_WOA, 8, X_CTX, "OA_split", banks=2)
            layernorm("l1", X_CTX, 4, "woA_evac", 0)

            def mlp(l, name, cols, ready):
                B0 = B_ML[l]

                def up(i, b_u, at, first):
                    pe.wait_ge(*when("w_split", b_u + 1))
                    for j in range(2):
                        if not first:
                            pe.wait_ge(*when(f"{name}_relu", 2 * i + j - 1))
                        dst = [ps[:, 2 * j + c, 0:n] for c, (_, n) in enumerate(cols)]
                        mm = gemm(dst, lambda k: k * 256 + j * P, at, KT, a_rhs, cols,
                                  on_tile(ready) if first and j == 0 else None)
                        done(mm, f"{name}_up", j == 1)

                def down(i, b_d, at, slot):
                    pe.wait_ge(*when("w_split", b_d + 1))
                    pe.wait_ge(*when(f"{name}_h", 2 * i + 2))
                    for m in range(KT):
                        pe.wait_ge(*when(f"{name}_dfree", 8 * i + m + 7))
                        dst = [ps[:, 4 + 2 * (m % 2) + c, 0:n] for c, (_, n) in enumerate(cols)]
                        mm = gemm(dst, lambda k: k * D + m * P, at, 2, h_rhs(slot), cols)
                        done(mm, f"{name}_down", m == KT - 1)

                up(0, B0, B0, True)
                with pe.Fori(0, (ML_IT - 2) // 2) as p:
                    for half in range(2):
                        i = 2 * p + half
                        at = B0 + 1 + 2 * half
                        up(i + 1, 4 * p + at, at, False)
                        down(i, 4 * p + at + 1, at + 1, half)
                i = ML_IT - 2
                up(i + 1, B0 + 1 + 2 * i, B0 + 1 + 2 * i, False)
                down(i, B0 + 2 + 2 * i, B0 + 2 + 2 * i, i % 2)
                down(i + 1, B0 + 3 + 2 * i, B0 + 3 + 2 * i, (i + 1) % 2)

            mlp(0, "ml0", X_CTX, "l1_out")
            layernorm("l2", X_CTX, 0, "ml0_dfree", 8 * ML_IT)

            def diff_turn(u, unit):
                pe.wait_ge(*when("pB", unit + 1))
                pe.wait_ge(*when("aT", unit + 1))
                for t in range(NTT):
                    mm = pe.transpose(psf[:, 4 * 512 + t * P:4 * 512 + (t + 1) * P], tmp[:, 2 * (u % 2), t * P:(t + 1) * P],
                                      ident[:, :])
                mm.then_inc(sem("turnB"), 1)

            def diff_values(hh, unit, nth):
                pe.wait_ge(*when("aT", unit + 1))
                pe.wait_ge(*when("oB", nth + 1))
                for t in range(NTT):
                    mm = pe.matmul(ps[:, 6, :], vB[:, t, hh * P:(hh + 1) * P], aT[:, t, :],
                                   start=(t == 0), stop=(t == NTT - 1))
                mm.then_inc(sem("oB_done"), 1)

            on = on_tile("l2_out")
            for k in range(KT):
                on(k)
            pe.sem_inc(sem("turnB"), 2)
            pe.sem_inc(sem("oB_done"), 1)
            with pe.Fori(0, 2) as p:
                for e in range(2):
                    st = 2 * p + e
                    at = B_QKV + 3 * e
                    b = 6 * p + at
                    pe.wait_ge(*when("oB", 2 * st + 1))
                    job = 0
                    for which in range(2):
                        pe.wait_ge(*when("w_split", b + which + 1))
                        for m in range(2):
                            for c, (c0, n) in enumerate(X_CTX[:1 + which]):
                                pe.wait_ge(*when(f"qkB_free{job % 2}", 3 * st + job // 2 + 1))
                                mm = gemm([ps[:, 6 + job % 2, 0:n]], lambda k: k * 256 + m * P, at + which, KT, a_rhs, [(c0, n)])
                                done(mm, "qkB_done", m == 1 and c == which)
                                job += 1
                    pe.wait_ge(*when("w_split", b + 3))
                    pe.wait_ge(*when("aT", 8 * st + 1))
                    for t in range(NTT):
                        pe.wait_ge(*when("vB", 6 * st + t + 1))
                        for k in range(KT):
                            for a, w in ((Ahi, whi), (Alo, whi), (Ahi, wlo)):
                                mm = pe.matmul(ps[:, 4 + t % 2, 0:256], a[:, k, t * P:(t + 1) * P],
                                               w[:, (at + 2) % 2, k * 256:(k + 1) * 256],
                                               start=(k == 0 and a is Ahi and w is whi), stop=(k == KT - 1 and w is wlo))
                        done(mm, "vB_done", t == NTT - 1)
                    pe.wait_ge(*when("qkB", 4 * st + 5))
                    pe.wait_ge(*when("qkB_free1", 3 * st + 4))
                    pe.wait_ge(*when("vB", 6 * st + 8))
                    for u in range(9):
                        if u < 8:
                            hh, n = u // 4, u % 4
                            for t in range(2):
                                rows = slice(DH * t, DH * t + DH)
                                pe.wait_ge(*when("sB_free", 16 * st + 2 * u + t + 1))
                                for half in range(2):
                                    a = 2 * t * 512 + P + half * 384
                                    mm = pe.matmul(psf[:, a:a + 384], qB[rows, hh, n * P:(n + 1) * P],
                                                   kB[rows, hh, half * 384:half * 384 + 384], start=True, stop=True)
                                mm.then_inc(sem("sB"), 1)
                        if u >= 1:
                            diff_turn(u - 1, 8 * st + u - 1)
                        if u == 4 or u == 8:
                            diff_values(u // 4 - 1, 8 * st + u, 2 * st + u // 4 - 1)
            for h in range(8):
                pe.wait_ge(*when("oB_sq", h + 1))
                if h >= 4:
                    pe.wait_ge(*when("oB_std", h - 3))
                pe.matmul(ps[:, h % 4, :], ones[:, :], tmp[:, h % 4, 0:T], start=True, stop=True).then_inc(sem("oB_ms"), 1)
            dense("woB", B_WOB, 8, X_ONLY, "OB_split")
            layernorm("l3", X_ONLY, 4, "woB_evac", 0)
            mlp(1, "ml1", X_ONLY, "l3_out")
            layernorm("l4", X_ONLY, 0, "ml1_dfree", 8 * ML_IT)

        @block.scalar
        def _(act):
            def copy(dst, src, scale=1.0):
                return act.activation(dst, src, ACT.Copy, scale=scale)

            def norm_squares(name, src, ready, before, each, width):
                for k in range(KT):
                    if ready:
                        act.wait_ge(*when(ready, before + each * (k + 1)))
                    if k >= 4:
                        act.wait_ge(*when(f"{name}_sum", k - 3))
                    act.activation(tmp[:, k % 4, 0:width], src[:, k, 0:width], ACT.Square).then_inc(sem(f"{name}_sq"), 1)

            def norm_std(name, bank, cols, eps):
                act.wait_ge(*when(f"{name}_sum", KT))
                for c, (c0, n) in enumerate(cols):
                    act.activation(std[:, c0:c0 + n], ps[:, bank + c, 0:n], ACT.Sqrt, scale=1.0 / D,
                                   bias=epsr[:, eps:eps + 1]).then_inc(sem(f"{name}_std"), 1)

            def split_hi(name, src, ready, each, width):
                for k in range(KT):
                    act.wait_ge(*when(ready, each * (k + 1)))
                    copy(Ahi[:, k, 0:width], src(k)).then_inc(sem(f"{name}_hi"), 1)

            def normed(k):
                return tmp[:, k % 4, 0:T]

            def rms(name, bank, ready, before, split=True):
                norm_squares(name, X, ready, before, 1, T)
                norm_std(name, bank, X_ONLY, 0)
                if split:
                    split_hi(name, normed, f"{name}_y", 1, T)

            def layernorm(name, cols, bank, last=False):
                width = sum(n for _, n in cols)
                norm_squares(name, X, f"{name}_d", 0, len(cols), width)
                norm_std(name, bank, cols, 1)
                if not last:
                    split_hi(name, lambda k: modin[:, k % 2, 0:width], f"{name}_m", len(cols), width)

            act.wait_ge(*when("small", 16 * N_SMALL))
            act.wait_ge(*when("setup", 4))
            act.wait_ge(*when("lam", 2))
            act.activation(lamt[:, 2:4], lamt[:, 0:2], ACT.Exp).then_inc(sem("lam"), 1)
            rms("n1", 0, None, 0)

            act.wait_ge(*when("csm_done", 1))
            for c in range(2):
                copy(csm[:, :, c * P:(c + 1) * P], ps[:, 4 + c, :].rearrange("p (h e) -> p h e", h=HEADS_A)).then_inc(sem("csm"), 1)
            for t, j in enumerate((2, 3, 6, 7)):
                if j % 2:
                    act.wait_ge(*when("w_used", B_WIN + j // 2 + 1))
                else:
                    act.wait_ge(*when("win_done", j // 2 + 1))
                act.activation(tmp[:, t, 0:T], ps[:, j % 4, :], ACT.Sigmoid).then_inc(sem("sig"), 1)
            for h in range(HEADS_A):
                j = 8 + h
                if j % 2:
                    act.wait_ge(*when("w_used", B_WIN + j // 2 + 1))
                else:
                    act.wait_ge(*when("win_done", j // 2 + 1))
                copy(pf[:, h, :], ps[:, h, :]).then_inc(sem("pf"), 1)

            def fourier_mid(h):
                act.wait_ge(*when("z_done", h + 1))
                if h >= 2:
                    act.wait_ge(*when("y_done", h - 1))
                zb = (4 + 2 * (h % 2)) * 512
                copy(zz[:, h % 2, :], psf[:, zb:zb + 1024]).then_inc(sem("z"), 1)

            def fourier_out(h):
                act.wait_ge(*when("y_done", h + 1))
                copy(Ahi[:, h, 0:T], ps[:, h, :]).then_inc(sem("mix_hi"), 1)

            fourier_mid(0)
            fourier_mid(1)
            for h in range(2, HEADS_A):
                fourier_mid(h)
                fourier_out(h - 2)
            fourier_out(2)
            fourier_out(3)
            act.activation(csil[:, :, :], v("c", 0, 2 * KT).rearrange("p (k s) -> p k s", s=2), ACT.Silu).then_inc(sem("csil"), 1)
            act.wait_ge(*when("csil", 1))
            act.wait_ge(*when("c4", 1))
            copy(c4[:, :, 0:2], csil[:, :, :]).then_inc(sem("c4"), 1)
            for h in range(4):
                act.wait_ge(*when("cd", h + 1))
                act.activation(tmp[:, h, 0:T], conv[:, h, :], ACT.Square).then_inc(sem("csq"), 1)
            for h in range(4):
                act.wait_ge(*when("cvar", h + 1))
                act.activation(pf[:, h, :], ps[:, h, :], ACT.Sqrt, scale=1.0 / P, bias=epsr[:, 1:2]).then_inc(sem("cstd"), 1)
            for h in range(4):
                act.wait_ge(*when("cy", h + 1))
                act.activation(tmp[:, h, 0:T], conv[:, h, :], ACT.Silu, bias=v("conv_ln_b", h)).then_inc(sem("csilu"), 1)
            for h in range(4):
                act.wait_ge(*when("csilu", h + 1))
                copy(Ahi[:, 4 + h, 0:T], tmp[:, h, 0:T]).then_inc(sem("mix_hi"), 1)

            def swiglu(f, name):
                B0 = B_FF[f]

                def rows(first, b_a):
                    for e in range(2):
                        act.wait_ge(*when("w_used", b_a + e + 1))
                        copy(arow[:, e, :], ps[0:4, 6 + e, 0:256]).then_inc(sem(f"{name}_arow"), 1)

                def step(i, b_g, slot, first):
                    for j in range(2):
                        if j:
                            act.wait_ge(*when("w_used", b_g + 1))
                        else:
                            act.wait_ge(*when(f"{name}_up", 2 * i + 1))
                        if not first:
                            act.wait_ge(*when(f"{name}_mul", 2 * i + j - 1))
                        act.activation(tmp[:, 2 + j, 0:T], ps[:, j, :], ACT.Silu).then_inc(sem(f"{name}_silu"), 1)
                    for j in range(2):
                        act.wait_ge(*when(f"{name}_mul", 2 * i + j + 1))
                        copy(hhi[:, slot, j, 0:T], tmp[:, j, 0:T]).then_inc(sem(f"{name}_hi"), 1)

                rows(True, B0)
                step(0, B0 + 2, 0, True)
                with act.Fori(0, (FF_IT - 1) // 2) as p:
                    for half in range(2):
                        b = 10 * p + B0 + 4 + 5 * half
                        rows(False, b)
                        step(2 * p + half + 1, b + 2, (half + 1) % 2, False)
                rows(False, B0 + 4 + 5 * (FF_IT - 1))

            rms("n2", 5, "wout_evac", 0)
            act.dma_start(icnt.rearrange("p a b -> p (a b)"), ins["icnt"]).then_inc(sem("icnt"), 16)
            swiglu(0, "ff0")
            rms("n3", 0, "ff0_dfree", 8 * FF_IT, split=False)
            for k in range(KT):
                act.wait_ge(*when("pool_y", k // 2 + 1))
                copy(Ahi[:, k, 0:T], tmp[:, k % 4, 0:T]).then_inc(sem("pool_hi"), 1)
            rms("n4", 0, "pool_evac", 0)
            for name, dst in (("cosq", cosq), ("sinq", sinq), ("maskl", maskl), ("maskr", maskr)):
                act.dma_start(dst, ins[name]).then_inc(sem("tables"), 16)
            swiglu(1, "ff1")
            rms("n5", 0, "ff1_dfree", 8 * FF_IT, split=False)
            split_hi("n5", lambda k: modin[:, k % 2, :], "n5_m", 2, TT)

            def swap_halves(src, scale):
                for q in range(4):
                    mm = copy(swap[32 * q:32 * q + 32, :], src[32 * (q ^ 1):32 * (q ^ 1) + 32, :], scale)
                return mm

            for j in range(2):
                if j:
                    act.wait_ge(*when("w_used", B_KV + 1))
                    act.wait_ge(*when("kvA_evac", 1))
                else:
                    act.wait_ge(*when("kvA_done", 1))
                bank = 4 + 2 * j
                copy(kd[:, j, T:TT], ps[:, bank + 1, 0:C])
                swap_halves(ps[:, bank, :], 1.0).then_inc(sem("kvA_swap"), 1)
            act.wait_ge(*when("w_used", B_KV + 2))
            copy(vT[:, 0:T], ps[:, 4, :])
            copy(vT[:, T:TT], ps[:, 5, 0:C]).then_inc(sem("kvA_evac"), 1)

            act.sem_inc(sem("qA_free1"), 1)
            act.sem_inc(sem("ptA"), 1)
            act.sem_inc(sem("sA_free"), 2)

            def sink(g, e, h):
                a = _cols["sink"][0] + 4 * e + h
                return vec[:, bass.ds(8 * g + a, 1)]

            with act.Fori(0, 2) as g:
                for e in range(2):
                    blk = 2 * g + e
                    for m in range(2):
                        if m:
                            act.wait_ge(*when("qA_done", 3 * blk + 3))
                        else:
                            act.wait_ge(*when("qA_done", 3 * blk + 1))
                        act.wait_ge(*when("qA", 2 * blk + m + 1))
                        swap_halves(ps[:, 6, :], SCALE).then_inc(sem("swA"), 1)
                        if m:
                            act.wait_ge(*when("w_used", blk + B_WQA + 1))
                        else:
                            act.wait_ge(*when("qA_done", 3 * blk + 2))
                        copy(qA[:, m, T:TT], ps[:, 7, 0:C], SCALE).then_inc(sem("qA_free1"), 1)

                    def take_turned(u, n, h):
                        unit = 24 * blk + u
                        nk = len(keys(n))
                        act.wait_ge(*when("turnA", unit + 3))
                        act.wait_ge(*when("oA_done", 6 * blk + n + 1))
                        copy(ptA[:, 0:nk, h * P:(h + 1) * P],
                             psf[:, 4 * 512:4 * 512 + nk * P].rearrange("p (t q) -> p t q", t=nk)).then_inc(sem("ptA"), 1)

                    units = [(n, h) for n in range(NTT) for h in range(4)]
                    for u, (n, h) in enumerate(units):
                        unit = 24 * blk + u
                        s = u % 2
                        W = len(keys(n)) * P
                        a = 2 * s * 512 + 512 + C - W
                        act.wait_ge(*when("nmA", unit + 1))
                        act.wait_ge(*when("turnA", unit + 1))
                        act.activation(probA[:, s, 0:W], psf[:, a:a + W], ACT.Exp, bias=sm[:, s, 1:2],
                                       accum_out=sm[:, s, 2:3]).then_inc(sem("sA_free"), 1)
                        act.activation(sm[:, s, 3:4], sink(g, e, h), ACT.Exp, bias=sm[:, s, 1:2]).then_inc(sem("esA"), 1)
                        if u >= 1:
                            take_turned(u - 1, *units[u - 1])
                    take_turned(23, *units[23])
            for k in range(KT):
                if k == 0:
                    act.wait_ge(*when("oA", 25))
                copy(Ahi[:, k, :], O[:, k, :]).then_inc(sem("OA_hi"), 1)
            layernorm("l1", X_CTX, 6)

            def mlp(l, name, cols):
                B0 = B_ML[l]
                width = sum(n for _, n in cols)

                def step(i, b_u, slot, first):
                    for j in range(2):
                        if j:
                            act.wait_ge(*when("w_used", b_u + 1))
                        else:
                            act.wait_ge(*when(f"{name}_up", i + 1))
                        if not first:
                            act.wait_ge(*when(f"{name}_mul", 2 * i + j - 1))
                        for c, (c0, n) in enumerate(cols):
                            mm = act.activation(tmp[:, 2 + j, c0:c0 + n], ps[:, 2 * j + c, 0:n], ACT.Relu)
                        mm.then_inc(sem(f"{name}_relu"), 1)
                    for j in range(2):
                        act.wait_ge(*when(f"{name}_mul", 2 * i + j + 1))
                        copy(hhi[:, slot, j, 0:width], tmp[:, j, 0:width]).then_inc(sem(f"{name}_hi"), 1)

                step(0, B0, 0, True)
                with act.Fori(0, (ML_IT - 2) // 2) as p:
                    for half in range(2):
                        step(2 * p + half + 1, 4 * p + B0 + 1 + 2 * half, (half + 1) % 2, False)
                i = ML_IT - 1
                step(i, B0 + 2 * i - 1, i % 2, False)

            mlp(0, "ml0", X_CTX)
            layernorm("l2", X_CTX, 2)

            act.sem_inc(sem("aT"), 1)
            act.sem_inc(sem("vB"), 2)
            act.sem_inc(sem("sB_free"), 2)
            with act.Fori(0, 2) as p:
                for e in range(2):
                    st = 2 * p + e
                    b = 6 * p + B_QKV + 3 * e

                    def swapped(src, scale, nth):
                        act.wait_ge(*when("qkB", 4 * st + nth + 1))
                        swap_halves(src, scale).then_inc(sem("swB"), 1)

                    act.wait_ge(*when("qkB_done", 4 * st + 1))
                    swapped(ps[:, 6, :], SCALE, 0)
                    act.wait_ge(*when("w_used", b + 1))
                    swapped(ps[:, 7, :], SCALE, 1)
                    for m in range(2):
                        act.wait_ge(*when("qkB_done", 4 * st + 2 + 2 * m))
                        swapped(ps[:, 6, :], 1.0, 2 + m)
                        if m:
                            act.wait_ge(*when("w_used", b + 2))
                        else:
                            act.wait_ge(*when("qkB_done", 4 * st + 3))
                        copy(kB[:, m, T:TT], ps[:, 7, 0:C]).then_inc(sem("qkB_free1"), 1)
                    for t in range(NTT):
                        if t < NTT - 1:
                            act.wait_ge(*when("vB_done", 5 * st + t + 1))
                        else:
                            act.wait_ge(*when("w_used", b + 3))
                        copy(vB[:, t, :], ps[:, 4 + t % 2, 0:256]).then_inc(sem("vB"), 1)
                    for u in range(9):
                        unit = 8 * st + u
                        s = u % 2
                        if u < 8:
                            act.wait_ge(*when("turnB", unit + 1))
                            for t in range(2):
                                a = 2 * t * 512 + P
                                act.wait_ge(*when("nmB", 16 * st + 2 * u + t + 1))
                                act.activation(tmp[:, 2 * s + t, :], psf[:, a:a + TT], ACT.Exp, bias=sm[:, s, t:t + 1],
                                               accum_out=sm[:, s, 2 + t:3 + t]).then_inc(sem("sB_free"), 1)
                        if u >= 1:
                            n = (u - 1) % 4
                            act.wait_ge(*when("turnB", unit + 2))
                            act.wait_ge(*when("oB_done", 2 * st + (u - 1) // 4 + 1))
                            copy(aT[:, :, n * P:(n + 1) * P],
                                 psf[:, 4 * 512:4 * 512 + TT].rearrange("p (t q) -> p t q", t=NTT)).then_inc(sem("aT"), 1)
            for i in range(12):
                if i < 8:
                    act.wait_ge(*when("oB_t", 2 * i + 2))
                    act.activation(tmp[:, i % 4, 0:T], tmp[:, i % 4, 0:T], ACT.Square).then_inc(sem("oB_sq"), 1)
                if 0 <= i - 2 < 8:
                    h = i - 2
                    act.wait_ge(*when("oB_flag", h + 1))
                    if h >= 2:
                        act.wait_ge(*when("oB_r", 3 * h - 4))
                    act.activation(aT[:, h % 2, :], ps[:, h % 4, :], ACT.Sqrt, scale=1.0 / P,
                                   bias=epsr[:, 2:3]).then_inc(sem("oB_std"), 1)
                if i >= 4:
                    h = i - 4
                    act.wait_ge(*when("oB_r", 3 * h + 3))
                    copy(Ahi[:, h, 0:T], O[:, h, 0:T]).then_inc(sem("OB_hi"), 1)
            layernorm("l3", X_ONLY, 6)
            mlp(1, "ml1", X_ONLY)
            layernorm("l4", X_ONLY, 2, last=True)

        @block.vector
        def _(dve):
            def split_lo(out_sem, hi_sem, k, src, width):
                dve.wait_ge(*when(hi_sem, k + 1))
                dve.tensor_tensor(Alo[:, k, 0:width], src, Ahi[:, k, 0:width], ALU.subtract).then_inc(sem(out_sem), 1)

            def norm_rstd(name, n_std, width):
                dve.wait_ge(*when(f"{name}_std", n_std))
                dve.reciprocal(rstd[:, 0:width], std[:, 0:width]).then_inc(sem(f"{name}_rstd"), 1)
                dve.wait_ge(*when(f"{name}_rstd", 1))

            def scaled(name, k, g, dst, width=T):
                return dve.scalar_tensor_tensor(out=dst, in0=X[:, k, 0:width], scalar=v(g[0], g[1] + k),
                                                in1=rstd[:, 0:width], op0=ALU.mult, op1=ALU.mult)

            def rms(name, g):
                norm_rstd(name, 1, T)
                for k in range(KT + 1):
                    if k < KT:
                        scaled(name, k, g, tmp[:, k % 4, 0:T]).then_inc(sem(f"{name}_y"), 1)
                    if k >= 1:
                        split_lo(f"{name}_out", f"{name}_hi", k - 1, tmp[:, (k - 1) % 4, 0:T], T)

            def modulate(name, k, use, src, cols, shared=None):
                for c, (c0, n) in enumerate(cols):
                    dve.tensor_scalar(modin[:, k % 2, c0:c0 + n], src[:, c0:c0 + n], s1[:, use, k, c:c + 1],
                                      s2[:, use, k, c:c + 1], ALU.mult, ALU.add).then_inc(sem(f"{name}_m"), 1)

            def layernorm(name, cols, bank, g, bias, use):
                width = sum(n for _, n in cols)
                dve.wait_ge(*when(f"{name}_mu", 1))
                for k in range(KT):
                    for c, (c0, n) in enumerate(cols):
                        dve.scalar_tensor_tensor(out=X[:, k, c0:c0 + n], in0=ps[:, bank + c, 0:n], scalar=-1.0 / D,
                                                 in1=X[:, k, c0:c0 + n], op0=ALU.mult, op1=ALU.add).then_inc(sem(f"{name}_d"), 1)
                dve.wait_ge(*when(f"{name}_d", len(cols) * KT))
                norm_rstd(name, len(cols), width)
                for k in range(KT + 1):
                    if k < KT:
                        t = tmp[:, k % 4, 0:width]
                        scaled(name, k, g, t, width).then_inc(sem(f"{name}_y"), 1)
                        dve.wait_ge(*when(f"{name}_y", k + 1))
                        dve.tensor_scalar(X[:, k, 0:width], t, v(bias[0], bias[1] + k), ALPHA if use is not None else 1.0,
                                          ALU.add, ALU.mult).then_inc(sem(f"{name}_res"), 1)
                        if use is not None:
                            modulate(name, k, use, t, cols)
                    if k >= 1 and use is not None:
                        split_lo(f"{name}_out", f"{name}_hi", k - 1, modin[:, (k - 1) % 2, 0:width], width)

            dve.memset(ones[:, :], 1.0).then_inc(sem("setup"), 1)
            for i, e in enumerate((RMS_EPS, LN_EPS, LN_EPS * SUB_SCALE * SUB_SCALE)):
                dve.memset(epsr[:, i:i + 1], e).then_inc(sem("setup"), 1)
            dve.memset(upad, 0.0).then_inc(sem("upad"), 1)
            dve.memset(c4[:, :, :].bitcast(F32), 0.0).then_inc(sem("c4"), 1)
            dve.wait_ge(*when("small", 16 * N_SMALL))
            pairs = v("lq1", 0, 4 * DH).rearrange("p (i s d) -> p i s d", i=2, s=2)
            products = rstd[:, 0:2 * DH].rearrange("p (i d) -> p i d", i=2)
            dve.tensor_tensor(products, pairs[:, :, 0], pairs[:, :, 1], ALU.mult).then_inc(sem("lam"), 1)
            dve.wait_ge(*when("lam", 1))
            dve.tensor_reduce(lamt[:, 0:2], products, AX_X, ALU.add).then_inc(sem("lam"), 1)
            dve.wait_ge(*when("lam", 3))
            dve.tensor_tensor(lamt[:, 4:5], lamt[:, 2:3], lamt[:, 3:4], ALU.subtract).then_inc(sem("lam"), 1)
            dve.wait_ge(*when("lam", 4))
            dve.tensor_scalar(lamt[:, 5:6], lamt[:, 4:5], LAM_INIT, -1.0, ALU.add, ALU.mult).then_inc(sem("lam"), 1)
            dve.tensor_scalar(lamt[:, 6:7], v("subln_g", 0), 1.0 - LAM_INIT, SUB_SCALE, ALU.mult, ALU.mult).then_inc(sem("lam"), 1)
            rms("n1", ("mix_g", 0))

            dve.wait_ge(*when("upad", 1))
            for t, j in enumerate((0, 1, 4, 5)):
                dve.wait_ge(*when("sig", t + 1))
                dve.tensor_tensor(upad[:, t, PADC:PADC + T], ps[:, j % 4, :], tmp[:, t, 0:T], ALU.mult).then_inc(sem("u"), 1)
            dve.wait_ge(*when("u", 4))
            w = _cols["conv_w"][0]
            for t in range(4):
                dve.tensor_scalar(conv[:, t, :], upad[:, t, 0:T], vec[:, w + t * TAPS:w + t * TAPS + 1], v("conv_b", t),
                                  ALU.mult, ALU.add).then_inc(sem("tap"), 1)
            with dve.Fori(1, TAPS - 1) as tap:
                for t in range(4):
                    dve.wait_ge(*when("tap", 4 * tap + t - 3))
                    dve.scalar_tensor_tensor(out=conv[:, t, :], in0=upad[:, t, bass.ds(tap, T)],
                                             scalar=vec[:, bass.ds(tap + (w + t * TAPS), 1)], in1=conv[:, t, :],
                                             op0=ALU.mult, op1=ALU.add).then_inc(sem("tap"), 1)
            for t in range(4):
                last = w + t * TAPS + TAPS - 1
                dve.wait_ge(*when("tap", 4 * (TAPS - 1) + t - 3))
                dve.scalar_tensor_tensor(out=conv[:, t, :], in0=upad[:, t, TAPS - 1:TAPS - 1 + T], scalar=vec[:, last:last + 1],
                                         in1=conv[:, t, :], op0=ALU.mult, op1=ALU.add).then_inc(sem("conv"), 1)
            for h in range(HEADS_A):
                split_lo("mix_out", "mix_hi", h, ps[:, h, :], T)
            dve.wait_ge(*when("c4", 2))
            dve.tensor_tensor(c4[:, :, 2:4], csil[:, :, :], c4[:, :, 0:2], ALU.subtract).then_inc(sem("c4"), 1)
            for h in range(4):
                dve.wait_ge(*when("cmu", h + 1))
                dve.scalar_tensor_tensor(out=conv[:, h, :], in0=ps[:, 4 + h, :], scalar=-1.0 / P, in1=conv[:, h, :],
                                         op0=ALU.mult, op1=ALU.add).then_inc(sem("cd"), 1)
            for h in range(4):
                dve.wait_ge(*when("cstd", h + 1))
                dve.reciprocal(pf[:, h, :], pf[:, h, :]).then_inc(sem("crstd"), 1)
                dve.wait_ge(*when("crstd", h + 1))
                dve.wait_ge(*when("cd", h + 1))
                dve.scalar_tensor_tensor(out=conv[:, h, :], in0=conv[:, h, :], scalar=v("conv_ln_g", h), in1=pf[:, h, :],
                                         op0=ALU.mult, op1=ALU.mult).then_inc(sem("cy"), 1)
            for h in range(4):
                split_lo("mix_out", "mix_hi", 4 + h, tmp[:, h, 0:T], T)
            for j in range(8):
                if j % 2:
                    dve.wait_ge(*when("w_used", B_WOUT + j // 2 + 1))
                else:
                    dve.wait_ge(*when("wout_done", j // 2 + 1))
                dve.tensor_tensor(X[:, j, 0:T], ps[:, j % 4, :], X[:, j, 0:T], ALU.add).then_inc(sem("wout_evac"), 1)

            def swiglu(f, name):
                B0 = B_FF[f]
                dve.sem_inc(sem(f"{name}_dfree"), 8)

                def mods(pair):
                    dve.wait_ge(*when(f"{name}_sel", pair + 1))
                    a = _cols["b_ada"][0] + f * 2 * N_MOD * KT
                    dve.tensor_tensor(modT[:, f, bass.ds(4 * pair, 4), :].rearrange("p k s -> p (k s)"), ps[:, 6, 0:8],
                                      vec[:, bass.ds(8 * pair + a, 8)], ALU.add).then_inc(sem(f"{name}_ada"), 1)

                def hidden(i, b_u, slot, first=False):
                    for j in range(2):
                        if j:
                            dve.wait_ge(*when("w_used", b_u + 1))
                        else:
                            dve.wait_ge(*when(f"{name}_up", 2 * i + 2))
                        dve.wait_ge(*when(f"{name}_silu", 2 * i + j + 1))
                        if not first:
                            dve.wait_ge(*when(f"{name}_h", 2 * i + j - 1))
                        dve.tensor_tensor(tmp[:, j, 0:T], ps[:, 2 + j, :], tmp[:, 2 + j, 0:T], ALU.mult).then_inc(sem(f"{name}_mul"), 1)
                    for j in range(2):
                        dve.wait_ge(*when(f"{name}_hi", 2 * i + j + 1))
                        dve.tensor_tensor(hlo[:, slot, j, 0:T], tmp[:, j, 0:T], hhi[:, slot, j, 0:T],
                                          ALU.subtract).then_inc(sem(f"{name}_h"), 1)

                def add_down(i, b_d):
                    for m in range(KT):
                        if m == KT - 1:
                            dve.wait_ge(*when("w_used", b_d + 1))
                        else:
                            dve.wait_ge(*when(f"{name}_down", 7 * i + m + 1))
                        dve.wait_ge(*when(f"{name}_dfree", 8 * i + m + 1))
                        dve.tensor_tensor(X[:, m, 0:T], ps[:, 4 + m % 2, :], X[:, m, 0:T], ALU.add).then_inc(sem(f"{name}_dfree"), 1)

                mods(0)
                hidden(0, B0 + 3, 0, True)
                with dve.Fori(0, (FF_IT - 1) // 2) as p:
                    for half in range(2):
                        i = 2 * p + half
                        b = 10 * p + B0 + 4 + 5 * half
                        mods(i + 1)
                        hidden(i + 1, b + 3, (half + 1) % 2)
                        add_down(i, b + 4)
                mods(FF_IT)
                add_down(FF_IT - 1, B0 + FF_BLOCKS - 1)

            rms("n2", ("ffn_g", 0))
            swiglu(0, "ff0")

            for a in (0, PADP + T):
                dve.memset(hp[:, :, a:a + PADP], 0.0).then_inc(sem("hp"), 1)
            norm_rstd("n3", 1, T)
            for k in range(KT):
                scaled("n3", k, ("mix_g", KT), hp[:, k, PADP:PADP + T]).then_inc(sem("hp"), 1)
            dve.wait_ge(*when("icnt", 16))
            n_win = 0
            for g in range(5):
                if g < 4:
                    dve.wait_ge(*when("hp", 2 + 2 * g + 2))
                    if g:
                        dve.wait_ge(*when("pool_y", g))
                    src, width = hp[:, 2 * g:2 * g + 2, :], HPAD
                    for d in range(g + 1):
                        dst = (pa, pb)[d % 2]
                        width -= 1 << d
                        if d:
                            dve.wait_ge(*when("win", n_win))
                        dve.tensor_tensor(dst[:, :, 0:width], src[:, :, 0:width], src[:, :, 1 << d:(1 << d) + width],
                                          ALU.add).then_inc(sem("win"), 1)
                        n_win += 1
                        src = dst
                    start = PADP - (1 << g)
                    other = (pb, pa)[g % 2]
                    dve.wait_ge(*when("win", n_win))
                    for m in range(2):
                        dve.tensor_tensor(other[:, m, 0:T], src[:, m, start:start + T], icnt[:, g, :], ALU.mult).then_inc(sem("win"), 1)
                    n_win += 2
                    dve.wait_ge(*when("win", n_win))
                    if g >= 2:
                        dve.wait_ge(*when("pool_in", g - 1))
                    dve.tensor_tensor(tmp[:, 2 * (g % 2):2 * (g % 2) + 2, 0:T], other[:, :, 0:T],
                                      hp[:, 2 * g:2 * g + 2, PADP:PADP + T], ALU.subtract).then_inc(sem("pool_y"), 1)
                if g >= 1:
                    for k in (2 * g - 2, 2 * g - 1):
                        dve.wait_ge(*when("pool_hi", k + 1))
                        ins_ = dve.tensor_tensor(Alo[:, k, 0:T], tmp[:, k % 4, 0:T], Ahi[:, k, 0:T], ALU.subtract)
                    ins_.then_inc(sem("pool_in"), 1)
            for j in range(8):
                if j == 7:
                    dve.wait_ge(*when("w_used", B_POOL + 1))
                else:
                    dve.wait_ge(*when("pool_done", j + 1))
                dve.scalar_tensor_tensor(out=X[:, j, 0:T], in0=ps[:, 4 + j % 4, :], scalar=v("pool_scale", j), in1=X[:, j, 0:T],
                                         op0=ALU.mult, op1=ALU.add).then_inc(sem("pool_evac"), 1)
            rms("n4", ("ffn_g", KT))
            swiglu(1, "ff1")

            dve.wait_ge(*when("ff0_ada", ADA_PAIRS))
            dve.wait_ge(*when("ff1_ada", ADA_PAIRS))
            n_mod = 0
            for use, (layer, shift, bias) in enumerate([(0, 0, None), (0, 3, ("ln1_b", 0)), (1, 0, ("ln2_b", 0)), (1, 3, ("ln1_b", KT))]):
                sh = modT[:, layer, shift * KT:(shift + 1) * KT, :]
                sc = modT[:, layer, (shift + 1) * KT:(shift + 2) * KT, :]
                dve.tensor_scalar(s1[:, use, :, :], sc, 1.0, None, ALU.add).then_inc(sem("mods"), 1)
                n_mod += 1
                if bias is None:
                    dve.tensor_copy(s2[:, use, :, :], sh).then_inc(sem("mods"), 1)
                    n_mod += 1
                    continue
                dve.wait_ge(*when("mods", n_mod))
                for src in range(2):
                    dve.tensor_tensor(s2[:, use, :, src], s1[:, use, :, src], v(bias[0], bias[1], KT), ALU.mult).then_inc(sem("mods"), 1)
                n_mod += 2
                dve.wait_ge(*when("mods", n_mod))
                dve.tensor_tensor(s2[:, use, :, :], s2[:, use, :, :], sh, ALU.add).then_inc(sem("mods"), 1)
                n_mod += 1
            dve.wait_ge(*when("mods", n_mod))
            norm_rstd("n5", 1, T)
            for k in range(KT + 1):
                if k < KT:
                    t = tmp[:, k % 4, 0:T]
                    scaled("n5", k, ("final_g", 0), t).then_inc(sem("n5_y"), 1)
                    dve.wait_ge(*when("n5_y", k + 1))
                    dve.tensor_scalar(X[:, k, 0:T], t, ALPHA, None, ALU.mult).then_inc(sem("n5_res"), 1)
                    dve.tensor_scalar(modin[:, k % 2, 0:T], t, s1[:, 0, k, 0:1], s2[:, 0, k, 0:1], ALU.mult, ALU.add).then_inc(sem("n5_m"), 1)
                    dve.tensor_scalar(modin[:, k % 2, T:TT], X[:, k, T:TT], s1[:, 0, k, 1:2], s2[:, 0, k, 1:2],
                                      ALU.mult, ALU.add).then_inc(sem("n5_m"), 1)
                    dve.tensor_scalar(X[:, k, T:TT], X[:, k, T:TT], ALPHA, None, ALU.mult).then_inc(sem("n5_res"), 1)
                if k >= 1:
                    split_lo("n5_out", "n5_hi", k - 1, modin[:, (k - 1) % 2, :], TT)

            dve.wait_ge(*when("tables", 64))

            def rotate(dst, src, scale, plain_sem, rot_sem, out_sem):
                dve.scalar_tensor_tensor(out=dst, in0=src, scalar=scale, in1=cosq, op0=ALU.mult,
                                         op1=ALU.mult).then_inc(sem(plain_sem[0]), 1)
                dve.tensor_tensor(swap, swap, sinq, ALU.mult).then_inc(sem(rot_sem[0]), 1)
                dve.wait_ge(*when(plain_sem[0], plain_sem[1]))
                dve.wait_ge(*when(rot_sem[0], rot_sem[1]))
                dve.tensor_tensor(dst, dst, swap, ALU.add).then_inc(sem(out_sem), 1)

            for j in range(2):
                dve.wait_ge(*when("kvA_swap", j + 1))
                rotate(kd[:, j, 0:T], ps[:, 4 + 2 * j, :], 1.0, ("kvA_cos", j + 1), ("kvA_sin", j + 1), "kvA_evac")
            dve.wait_ge(*when("vA_done", 1))
            dve.tensor_copy(vA.rearrange("p t d -> p (t d)"), psf[:, 4 * 512:4 * 512 + TT]).then_inc(sem("vA"), 1)
            dve.wait_ge(*when("vA", 1))
            dve.wait_ge(*when("kvA_evac", 3))
            dve.sem_inc(sem("qA_free0"), 1)
            dve.sem_inc(sem("qA"), 1)
            dve.sem_inc(sem("oA"), 1)
            with dve.Fori(0, 2) as g:
                dve.wait_ge(*when("oA_done", 12 * g + 1))
                dve.tensor_copy(kcur, kd[:, bass.ds(g, 1), :].rearrange("p a t -> p (a t)")).then_inc(sem("kvcur"), 1)
                dve.tensor_copy(vcur, vA[:, :, bass.ds(DH * g, DH)]).then_inc(sem("kvcur"), 1)
                for e in range(2):
                    blk = 2 * g + e
                    for m in range(2):
                        dve.wait_ge(*when("swA", 2 * blk + m + 1))
                        rotate(qA[:, m, 0:T], ps[:, 6, :], SCALE, ("qA_free0", 2 * blk + m + 2), ("sinA", 2 * blk + m + 1), "qA")

                    def finish(u, n):
                        unit = 24 * blk + u
                        s = u % 2
                        dve.wait_ge(*when("esA", unit + 1))
                        dve.wait_ge(*when("sA_free", unit + 3))
                        dve.tensor_tensor(sm[:, s, 4:5], sm[:, s, 2:3], sm[:, s, 3:4], ALU.add).then_inc(sem("denA"), 1)
                        dve.wait_ge(*when("denA", 2 * unit + 1))
                        dve.reciprocal(sm[:, s, 5:6], sm[:, s, 4:5]).then_inc(sem("denA"), 1)
                        dve.wait_ge(*when("denA", 2 * unit + 2))
                        W = len(keys(n)) * P
                        dve.tensor_scalar(probA[:, s, 0:W], probA[:, s, 0:W], sm[:, s, 5:6], None, ALU.mult).then_inc(sem("pA"), 1)

                    def take_values(n):
                        dve.wait_ge(*when("oA_done", 6 * blk + n + 2))
                        four = ps[0:DH, 6, :].rearrange("p (t h q) -> p h t q", t=2, h=2)
                        for h in range(2):
                            mm = dve.tensor_copy(O[DH * h:DH * h + DH, bass.ds(4 * g + 2 * e, 2), n * P:(n + 1) * P], four[:, h])
                        mm.then_inc(sem("oA"), 1)

                    units = [(n, h) for n in range(NTT) for h in range(4)]
                    for u, (n, h) in enumerate(units):
                        unit = 24 * blk + u
                        s = u % 2
                        W = len(keys(n)) * P
                        a = 2 * s * 512 + 512 + C - W
                        sink = vec[:, bass.ds(8 * g + (_cols["sink"][0] + 4 * e + h), 1)]
                        dve.wait_ge(*when("sA", unit + 1))
                        dve.tensor_reduce(sm[:, s, 0:1], psf[:, a:a + W], AX_X, ALU.max).then_inc(sem("mxA"), 1)
                        dve.wait_ge(*when("mxA", unit + 1))
                        dve.tensor_scalar(sm[:, s, 1:2], sm[:, s, 0:1], sink, -1.0, ALU.max, ALU.mult).then_inc(sem("nmA"), 1)
                        if u >= 1:
                            finish(u - 1, units[u - 1][0])
                        if u >= 2 and units[u - 2][1] == 3:
                            take_values(units[u - 2][0])
                    finish(23, NTT - 1)
                    take_values(NTT - 1)
            for k in range(KT):
                split_lo("OA_split", "OA_hi", k, O[:, k, :], TT)
            for j in range(8):
                if j % 2:
                    dve.wait_ge(*when("w_used", B_WOA + j // 2 + 1))
                else:
                    dve.wait_ge(*when("woA_done", j // 2 + 1))
                for c, (c0, n) in enumerate(X_CTX):
                    mm = dve.scalar_tensor_tensor(out=X[:, j, c0:c0 + n], in0=ps[:, 2 * (j % 2) + c, 0:n],
                                                  scalar=mod(0, 2, j, c), in1=X[:, j, c0:c0 + n], op0=ALU.mult, op1=ALU.add)
                mm.then_inc(sem("woA_evac"), 1)
            layernorm("l1", X_CTX, 4, ("ln1_g", 0), ("ln1_b", 0), 1)

            def mlp(l, name, cols):
                B0 = B_ML[l]
                width = sum(n for _, n in cols)
                dve.sem_inc(sem(f"{name}_dfree"), 8)

                def hidden(i, slot, first=False):
                    for j in range(2):
                        dve.wait_ge(*when(f"{name}_relu", 2 * i + j + 1))
                        if not first:
                            dve.wait_ge(*when(f"{name}_h", 2 * i + j - 1))
                        r = tmp[:, 2 + j, 0:width]
                        dve.tensor_tensor(tmp[:, j, 0:width], r, r, ALU.mult).then_inc(sem(f"{name}_mul"), 1)
                    for j in range(2):
                        dve.wait_ge(*when(f"{name}_hi", 2 * i + j + 1))
                        dve.tensor_tensor(hlo[:, slot, j, 0:width], tmp[:, j, 0:width], hhi[:, slot, j, 0:width],
                                          ALU.subtract).then_inc(sem(f"{name}_h"), 1)

                def add_down(i, b_d):
                    for m in range(KT):
                        if m == KT - 1:
                            dve.wait_ge(*when("w_used", b_d + 1))
                        else:
                            dve.wait_ge(*when(f"{name}_down", 7 * i + m + 1))
                        dve.wait_ge(*when(f"{name}_dfree", 8 * i + m + 1))
                        for c, (c0, n) in enumerate(cols):
                            mm = dve.scalar_tensor_tensor(out=X[:, m, c0:c0 + n], in0=ps[:, 4 + 2 * (m % 2) + c, 0:n],
                                                          scalar=mod(l, 5, m, c), in1=X[:, m, c0:c0 + n],
                                                          op0=ALU.mult, op1=ALU.add)
                        mm.then_inc(sem(f"{name}_dfree"), 1)

                dve.wait_ge(*when("l1_res" if l == 0 else "l3_res", KT))
                hidden(0, 0, True)
                with dve.Fori(0, (ML_IT - 2) // 2) as p:
                    for half in range(2):
                        i = 2 * p + half
                        hidden(i + 1, (half + 1) % 2)
                        add_down(i, 4 * p + B0 + 2 + 2 * half)
                i = ML_IT - 2
                hidden(i + 1, (i + 1) % 2)
                add_down(i, B0 + 2 + 2 * i)
                add_down(i + 1, B0 + 3 + 2 * i)

            mlp(0, "ml0", X_CTX)
            layernorm("l2", X_CTX, 0, ("ln2_g", 0), ("ln2_b", 0), 2)

            dve.sem_inc(sem("qkB_free0"), 1)
            dve.sem_inc(sem("qkB_free1"), 1)
            dve.sem_inc(sem("qkB"), 1)
            dve.sem_inc(sem("oB"), 1)
            with dve.Fori(0, 2) as p:
                for e in range(2):
                    st = 2 * p + e
                    for r, (dst, bank, scale, at) in enumerate([(qB[:, 0, :], 6, SCALE, 2), (qB[:, 1, :], 7, SCALE, 2),
                                                               (kB[:, 0, 0:T], 6, 1.0, 3), (kB[:, 1, 0:T], 6, 1.0, 4)]):
                        dve.wait_ge(*when("swB", 4 * st + r + 1))
                        rotate(dst, ps[:, bank, :], scale, (f"qkB_free{bank - 6}", 3 * st + at), ("sinB", 4 * st + r + 1), "qkB")
                    for u in range(9):
                        if u < 8:
                            for t in range(2):
                                a = 2 * t * 512 + P
                                dve.wait_ge(*when("sB", 16 * st + 2 * u + t + 1))
                                dve.tensor_reduce(sm[:, u % 2, t:t + 1], psf[:, a:a + TT], AX_X, ALU.max,
                                                  negate=True).then_inc(sem("nmB"), 1)
                        if u >= 1:
                            unit = 8 * st + u - 1
                            s = (u - 1) % 2
                            p0, p1 = tmp[:, 2 * s, :], tmp[:, 2 * s + 1, :]
                            dve.wait_ge(*when("sB_free", 2 * unit + 4))
                            dve.reciprocal(sm[:, s, 4:6], sm[:, s, 2:4]).then_inc(sem("denB"), 1)
                            dve.wait_ge(*when("denB", 3 * unit + 1))
                            dve.tensor_tensor(sm[:, s, 6:7], sm[:, s, 5:6], lamt[:, 5:6], ALU.mult).then_inc(sem("denB"), 1)
                            dve.tensor_scalar(p0, p0, sm[:, s, 4:5], None, ALU.mult).then_inc(sem("denB"), 1)
                            dve.wait_ge(*when("denB", 3 * unit + 3))
                            dve.scalar_tensor_tensor(out=p0, in0=p1, scalar=sm[:, s, 6:7], in1=p0, op0=ALU.mult,
                                                     op1=ALU.add).then_inc(sem("pB"), 1)
                        if u == 4 or u == 8:
                            head = 2 * st + u // 4 - 1
                            dve.wait_ge(*when("oB_done", head + 2))
                            dve.tensor_copy(O[:, bass.ds(head, 1), 0:T].rearrange("p a t -> p (a t)"), ps[:, 6, :]).then_inc(sem("oB"), 1)
            for i in range(12):
                if i < 8:
                    if i == 0:
                        dve.wait_ge(*when("oB", 9))
                    if i >= 4:
                        dve.wait_ge(*when("oB_ms", i - 3))
                    dve.tensor_scalar(tmp[:, i % 4, 0:T], O[:, i, 0:T], SUB_SCALE, SUB_CLAMP, ALU.mult, ALU.min).then_inc(sem("oB_t"), 1)
                    dve.wait_ge(*when("oB_t", 2 * i + 1))
                    dve.tensor_scalar(tmp[:, i % 4, 0:T], tmp[:, i % 4, 0:T], -SUB_CLAMP, None, ALU.max).then_inc(sem("oB_t"), 1)
                if 0 <= i - 2 < 8:
                    h = i - 2
                    dve.wait_ge(*when("oB_ms", h + 1))
                    dve.tensor_scalar(aT[:, 2 + h % 2, :], ps[:, h % 4, :], SUB_OVER, None, ALU.is_lt).then_inc(sem("oB_flag"), 1)
                if 0 <= i - 3 < 8:
                    h = i - 3
                    dve.wait_ge(*when("oB_std", h + 1))
                    dve.reciprocal(aT[:, 4 + h % 2, :], aT[:, h % 2, :]).then_inc(sem("oB_r"), 1)
                    dve.wait_ge(*when("oB_r", 3 * h + 1))
                    dve.wait_ge(*when("oB_flag", h + 1))
                    dve.tensor_tensor(aT[:, 4 + h % 2, :], aT[:, 4 + h % 2, :], aT[:, 2 + h % 2, :], ALU.mult).then_inc(sem("oB_r"), 1)
                    dve.wait_ge(*when("oB_r", 3 * h + 2))
                    dve.scalar_tensor_tensor(out=O[:, h, 0:T], in0=O[:, h, 0:T], scalar=lamt[:, 6:7], in1=aT[:, 4 + h % 2, :],
                                             op0=ALU.mult, op1=ALU.mult).then_inc(sem("oB_r"), 1)
                if i >= 4:
                    split_lo("OB_split", "OB_hi", i - 4, O[:, i - 4, 0:T], T)
            for j in range(8):
                if j % 2:
                    dve.wait_ge(*when("w_used", B_WOB + j // 2 + 1))
                else:
                    dve.wait_ge(*when("woB_done", j // 2 + 1))
                dve.scalar_tensor_tensor(out=X[:, j, 0:T], in0=ps[:, j % 4, :], scalar=mod(1, 2, j, 0), in1=X[:, j, 0:T],
                                         op0=ALU.mult, op1=ALU.add).then_inc(sem("woB_evac"), 1)
            layernorm("l3", X_ONLY, 4, ("ln1_g", KT), ("ln1_b", KT), 3)
            mlp(1, "ml1", X_ONLY)
            layernorm("l4", X_ONLY, 0, ("ln2_g", KT), ("ln2_b", KT), None)


SMALL = [("xT", (P, KT, T)), ("vec", (P, N_VEC)), ("ident", (P, P)), ("sel4", (4, 2)), ("ctxT", (P, KT, C)),
         ("csd", (P, 2 * P)), ("fmap", (P, HEADS_A * P)), ("dft", (P, 2 * QT * T))]
LATER = [("icnt", (P, 4 * T)), ("cosq", (P, T)), ("sinq", (P, T)), ("maskl", (P, P)), ("maskr", (P, P))]


def constants():
    f = np.float32
    out = {"ident": np.eye(P, dtype=f), "sel4": np.array([[1, 0], [0, 1], [1, 0], [0, 1]], f)}
    n = np.arange(P)
    ang = 2 * np.pi * (np.outer(n, n) % P) / P
    out["csd"] = (np.concatenate([np.cos(ang), np.sin(ang)], 1) / math.sqrt(T * P)).astype(f)
    n = np.arange(T)
    ang = 2 * np.pi * (np.outer(n, n) % T) / T
    both = np.stack([np.cos(ang), -np.sin(ang)])
    out["dft"] = both.reshape(2, QT, P, T).transpose(2, 0, 1, 3).reshape(P, -1).astype(f)
    pos = np.arange(T)
    cnt = [np.clip(pos - w // 2 + w, 0, T) - np.clip(pos - w // 2, 0, T) for w in (2, 4, 8, 16)]
    out["icnt"] = np.broadcast_to((1.0 / np.array(cnt)).astype(f).reshape(1, -1), (P, 4 * T))
    freqs = DH // 4
    inv = f(10000.0) ** (-np.arange(freqs, dtype=f) / f(freqs))
    row = np.repeat(np.arange(T // 64, dtype=f), 64)
    col = np.tile(np.arange(64, dtype=f), T // 64)
    ang = np.concatenate([row[:, None] * inv, col[:, None] * inv], 1).astype(f).T
    out["cosq"] = np.tile(np.cos(ang), (4, 1)).astype(f)
    out["sinq"] = np.tile(np.concatenate([-np.sin(ang), np.sin(ang)]), (2, 1)).astype(f)
    q, k = np.arange(P)[:, None], np.arange(P)[None, :]
    out["maskl"] = np.where(k >= q, 0, NEG).astype(f)
    out["maskr"] = np.where(k <= q, 0, NEG).astype(f)
    return out


def by_inputs(w):
    return [w[:, m:m + 256].reshape(KT, P, 256).transpose(1, 0, 2).reshape(P, BLK) for m in range(0, w.shape[1], 256)]


def by_hidden(w):
    return [w[m:m + 256].reshape(2, P, D).transpose(1, 0, 2).reshape(P, BLK) for m in range(0, w.shape[0], 256)]


def stream(a):
    blocks = []
    win = by_inputs(a["w_in_ab"][0])
    blocks += [win[2], win[4], win[3], win[5], win[0], win[1]]
    blocks += by_inputs(a["w_out_ab"][0])
    for f in range(2):
        ada = by_inputs(a["w_ada_2"][f])
        gate, up, down = by_inputs(a["ffn_w_gate"][f]), by_inputs(a["ffn_w_up"][f]), by_hidden(a["ffn_w_down"][f])
        blocks += ada[0:2] + [gate[0], up[0]]
        for i in range(FF_IT - 1):
            blocks += ada[2 * i + 2:2 * i + 4] + [gate[i + 1], up[i + 1], down[i]]
        blocks += ada[2 * FF_IT:2 * FF_IT + 2] + [down[FF_IT - 1]]
        if f == 0:
            blocks.append(a["pool_map"][0].reshape(4, 2, P, 256).transpose(2, 1, 0, 3).reshape(P, BLK))
    wk, wv = a["a_wk_2"][0], a["a_wv_2"][0]
    blocks += by_inputs(np.concatenate([wk[:, 0:DH], wk[:, 0:DH], wk[:, DH:], wk[:, DH:]], 1))
    blocks += by_inputs(np.concatenate([wv, np.zeros_like(wv)], 1))
    blocks += by_inputs(a["a_wq_2"][0]) + by_inputs(a["a_wo_2"][0])
    for l in range(2):
        w1, w2 = by_inputs(a["mlp_w1_2"][l]), by_hidden(a["mlp_w2_2"][l])
        blocks += [w1[0]]
        for i in range(ML_IT - 1):
            blocks += [w1[i + 1], w2[i]]
        blocks += [w2[ML_IT - 1]]
        if l == 0:
            for q, k, w in zip(by_inputs(a["b_wq_2"][0]), by_inputs(a["b_wk_2"][0]), by_inputs(a["b_wv_2"][0])):
                blocks += [q, k, w]
            blocks += by_inputs(a["b_wo_2"][0])
    assert len(blocks) == N_BLOCKS
    return np.stack(blocks)


def features(x):
    x = np.asarray(x)
    return np.ascontiguousarray(np.moveaxis(x.reshape(*x.shape[:-1], -1, P), -1, 0)).reshape(P, -1)


def vectors(a):
    every = lambda x: np.broadcast_to(np.asarray(x).reshape(1, -1), (P, np.asarray(x).size))
    parts = {
        "mix_g": features(a["norm_mix_g"]), "ffn_g": features(a["norm_ffn_g"]),
        "conv_w": features(a["conv_w"][0]).reshape(P, TAPS, 4).transpose(0, 2, 1).reshape(P, -1),
        "conv_b": features(a["conv_b"][0]), "conv_ln_g": features(a["conv_ln_g"][0]),
        "conv_ln_b": features(a["conv_ln_b"][0]), "pool_scale": features(a["pool_scale"][0]),
        "final_g": features(a["final_g"]), "b_ada": np.repeat(features(a["b_ada_2"]), 2, axis=1),
        "ln1_g": features(a["ln1_g_2"]), "ln1_b": features(a["ln1_b_2"]), "ln2_g": features(a["ln2_g_2"]),
        "ln2_b": features(a["ln2_b_2"]), "sink": every(a["a_sink_2"][0]), "subln_g": np.asarray(a["b_subln_g_2"][0])[:, None],
        "lq1": every(a["b_lq1_2"]), "lk1": every(a["b_lk1_2"]), "lq2": every(a["b_lq2_2"]), "lk2": every(a["b_lk2_2"]),
        "c": np.stack([features(a["c_2"][0]), features(a["c_ctx_2"])], 2).reshape(P, -1),
    }
    return np.ascontiguousarray(np.concatenate([parts[n] for n in _cols], 1))


def kernel(**inputs):
    import concourse.bacc as bacc
    from concourse.bass_utils import run_bass_kernel_spmd

    a = {n: np.asarray(x) for n, x in inputs.items()}
    arrays = {n: np.ascontiguousarray(x) for n, x in constants().items()}
    arrays["stream"] = stream(a)
    arrays["vec"] = vectors(a)
    arrays["xT"] = np.ascontiguousarray(a["x"][0].reshape(T, KT, P).transpose(2, 1, 0))
    arrays["ctxT"] = np.ascontiguousarray(a["ctx_2"][0].reshape(C, KT, P).transpose(2, 1, 0))
    arrays["fmap"] = np.ascontiguousarray(a["fnet_map"][0].transpose(1, 0, 2).reshape(P, HEADS_A * P))
    nc = bacc.Bacc("TRN2", target_bir_lowering=False, num_devices=1)
    ins = {n: nc.dram_tensor(f"in_{n}", x.shape, F32, kind="ExternalInput").ap() for n, x in arrays.items()}
    out = nc.dram_tensor("out_xT", (P, KT, T), F32, kind="ExternalOutput").ap()
    build(nc, ins, out)
    got = run_bass_kernel_spmd(nc, [{f"in_{n}": x for n, x in arrays.items()}], core_ids=[0]).results[0]["out_xT"]
    return np.ascontiguousarray(got.transpose(2, 1, 0)).reshape(1, T, D)
```

```python
import math
from contextlib import ExitStack

import numpy as np

import concourse.bass as bass
import concourse.mybir as mybir

F32 = mybir.dt.float32
F32R = mybir.dt.float32r
BF16 = mybir.dt.bfloat16
ALU = mybir.AluOpType
ACT = mybir.ActivationFunctionType
AX_X = mybir.AxisListType.X

P = 128
D = 1024
KT = D // P
T = 512
C = 256
TT = T + C
BLK = 2048
RING = 3
QT = T // P
NTT = TT // P
DH = 64
HEADS_A = 4
TAPS = 31
PADC = TAPS // 2
UP = T + 2 * PADC
PADP = 8
HPAD = T + 2 * PADP
D_FF = 2816
FF_IT = D_FF // 256
D_FF2 = 4096
ML_IT = D_FF2 // 256
N_MOD = 6
ADA_PAIRS = N_MOD * D // 512
RMS_EPS = 1e-6
LN_EPS = 1e-5
N_SMALL = 3
ALPHA = 4.0 ** 0.25
LAM_INIT = 0.8 - 0.6 * math.exp(-0.3)
SCALE = DH ** -0.5
NEG = -1e30
SUB_SCALE = 2.0 ** -40
SUB_CLAMP = 2.0 ** 30
SUB_OVER = 2.0 ** 48

UNITS = [(e, n, h) for e in range(2) for n in range(NTT) for h in range(4)]
N_UNITS = len(UNITS)

X_ONLY = [(0, T)]
X_CTX = [(0, T), (T, C)]

B_WIN = 0
B_WOUT = B_WIN + 6
FF_BLOCKS = 5 * FF_IT + 2
B_FF = [B_WOUT + 4, B_WOUT + 4 + FF_BLOCKS + 1]
B_POOL = B_FF[0] + FF_BLOCKS
B_KV = B_FF[1] + FF_BLOCKS
B_WQA = B_KV + 2
B_WOA = B_WQA + 4
ML_BLOCKS = 2 * ML_IT
B_ML0 = B_WOA + 4
B_QKV = B_ML0 + ML_BLOCKS
B_WOB = B_QKV + 12
B_ML1 = B_WOB + 4
N_BLOCKS = B_ML1 + ML_BLOCKS
B_ML = [B_ML0, B_ML1]

_cols = {}
_n = 0
for _name, _w in [
    ("mix_g", 2 * KT), ("ffn_g", 2 * KT), ("conv_w", 4 * TAPS), ("conv_b", 4), ("conv_ln_g", 4), ("conv_ln_b", 4),
    ("pool_scale", KT), ("final_g", KT), ("b_ada", 2 * 48 * 2), ("ln1_g", 2 * KT), ("ln1_b", 2 * KT),
    ("ln2_g", 2 * KT), ("ln2_b", 2 * KT), ("sink", 16), ("subln_g", 1), ("lq1", 64), ("lk1", 64), ("lq2", 64),
    ("lk2", 64), ("c", KT * 2),
]:
    _cols[_name] = (_n, _n + _w)
    _n += _w
N_VEC = _n


def build(nc, ins, out):
    ctx = ExitStack()
    with ctx:
        def sb(name, shape, dt=F32):
            return ctx.enter_context(nc.sbuf_tensor(name, shape, dt))

        shared = {}

        def share(signal, phases):
            before = 0
            for phase, n in phases.items():
                shared[f"{phase}_{signal}"] = (signal, before)
                before += n

        rms_split, with_ctx = ["n1", "n2", "n4"], ["l1", "l2"]
        norms = ["n1", "n2", "n3", "n4", "n5", "l1", "l2", "l3", "l4"]
        tiles = {n: KT for n in norms}
        share("sq", tiles)
        share("sum", tiles)
        share("std", {n: 2 if n in with_ctx else 1 for n in norms})
        share("rstd", {n: 1 for n in norms})
        share("y", {n: KT for n in norms if n != "n3"})
        for signal in ("hi", "out"):
            share(signal, {n: KT for n in norms if n not in ("n3", "l4")})
        share("m", {"n5": 2 * KT, "l1": 2 * KT, "l2": 2 * KT, "l3": KT})
        share("mu", {n: 1 for n in norms[5:]})
        share("d", {"l1": 2 * KT, "l2": 2 * KT, "l3": KT, "l4": KT})
        share("res", {"n5": 2 * KT, "l1": KT, "l2": KT, "l3": KT, "l4": KT})
        for kind, steps in (("ff", FF_IT), ("ml", ML_IT)):
            pair = (kind + "0", kind + "1")
            for signal in ("silu" if kind == "ff" else "relu", "mul", "hi", "h"):
                for n, phase in enumerate(pair):
                    shared[f"{phase}_{signal}"] = (f"{kind}_{signal}", 2 * steps * n)
            for n, phase in enumerate(pair):
                shared[f"{phase}_up"] = (f"{kind}_up", (2 if kind == "ff" else 1) * steps * n)
                shared[f"{phase}_down"] = (f"{kind}_down", (KT - 1) * steps * n)
                shared[f"{phase}_dfree"] = (f"{kind}_dfree", (KT * steps + 8) * n)
        for n in range(2):
            shared[f"ff{n}_ada"] = ("ada", ADA_PAIRS * n)
            shared[f"ff{n}_sel"] = ("ada_sel", ADA_PAIRS * n)
            shared[f"ff{n}_arow"] = ("ada_row", 2 * ADA_PAIRS * n)
        sems = {}

        def sem(name):
            name = shared.get(name, (name, 0))[0]
            if name not in sems:
                sems[name] = ctx.enter_context(nc.semaphore(name))
            return sems[name]

        def when(name, count):
            return sem(name), count + shared.get(name, (name, 0))[1]

        X = sb("X", [P, KT, TT])
        Ahi = sb("Ahi", [P, KT, TT], F32R)
        Alo = sb("Alo", [P, KT, TT], F32R)
        whi = sb("whi", [P, RING, BLK], F32R)
        raw = sb("raw", [P, RING, BLK])
        wlo = nc.alloc_sbuf_tensor_at("wlo", [P, RING, BLK], F32R, offset=nc.sbuf_base - 4 * RING * BLK)
        tmp = sb("tmp", [P, 4, TT])
        std = sb("std", [P, TT])
        rstd = sb("rstd", [P, TT])
        vec = sb("vec", [P, N_VEC])
        ident = sb("ident", [P, P])
        ones = sb("ones", [P, P])
        epsr = sb("epsr", [P, 3])
        modT = sb("modT", [P, 2, N_MOD * KT, 2])
        s1 = sb("s1", [P, 4, KT, 2])
        s2 = sb("s2", [P, 4, KT, 2])
        csil = sb("csil", [P, KT, 2])
        sel4 = sb("sel4", [4, 2])
        lamt = sb("lamt", [P, 8])
        sm = sb("sm", [P, 4, 8])
        maskb = sb("maskb", [P, 3, P], BF16)
        ARENA = 16128
        arena = sb("arena", [P, ARENA])
        arena_at = nc.sbuf_base - 4 * ARENA

        def carve(at, *shape):
            n = int(np.prod(shape))
            assert at + n <= ARENA, (at, shape)
            a = arena[:, at:at + n]
            if len(shape) == 2:
                a = a.rearrange("p (a b) -> p a b", a=shape[0])
            if len(shape) == 3:
                a = a.rearrange("p (a b c) -> p a b c", a=shape[0], b=shape[1])
            return a, at + n

        hhi = nc.alloc_sbuf_tensor_at("hhi", [P, 3, 2, TT], F32R, offset=arena_at)
        hlo = nc.alloc_sbuf_tensor_at("hlo", [P, 3, 2, TT], F32R, offset=arena_at + 4 * 6 * TT)
        H_END = 12 * TT
        c4 = nc.alloc_sbuf_tensor_at("c4", [P, KT, P], F32R, offset=arena_at + 4 * (ARENA - KT * P))
        modin, MODIN_END = carve(H_END, 2, TT)
        dft, at = carve(0, 2, QT, T)
        upad, at = carve(at, 4, UP)
        conv, at = carve(at, 4, T)
        pf, at = carve(at, 4, T)
        zz, at = carve(at, 2, QT * 256)
        csd, at = carve(at, 256)
        fmap, at = carve(at, 4 * P)
        csm, at = carve(at, 4, 256)
        assert at <= ARENA - KT * P
        hp, at = carve(0, KT, HPAD)
        pa, at = carve(at, 2, HPAD)
        pb, at = carve(at, 2, HPAD)
        assert at <= H_END
        icnt, at = carve(MODIN_END, 4, T)
        arow, at = carve(at, 2, 256)
        arow = arow[0:4]
        assert at <= ARENA - KT * P
        O, O_END = carve(0, KT, TT)
        cosq, at = carve(MODIN_END, T)
        sinq, at = carve(at, T)
        masks, base = carve(at, 2, P)
        swap = modin[:, :, 0:T]
        vT = tmp[:, 1, :]
        kcur = tmp[:, 1, :]
        probA = [tmp[:, i, 0:640] for i in (2, 3, 0)]
        ptA, at = carve(O_END, 5, T)
        vcur, at = carve(at, NTT, DH)
        assert at <= H_END
        kd, at = carve(base, 2, TT)
        vA, at = carve(at, NTT, P)
        qcur0, at = carve(at, 2, TT)
        qcur = (qcur0, modin)
        probB = [(tmp[:, 0, :], tmp[:, 1, :]), (tmp[:, 2, :], tmp[:, 3, :]), (std[:, :], rstd[:, :])]
        aT, at = carve(O_END, NTT, T)
        assert at <= H_END
        qB, at = carve(base, 2, T)
        kB, at = carve(at, 2, TT)
        vB, at = carve(at, NTT, 256)
        ps = ctx.enter_context(nc.psum_tensor("ps", [P, 8, 512], F32))
        psf = ps[:, :, :].rearrange("p b n -> p (b n)")

        def window(n):
            return (max(0, n - 1), min(QT, n + 2)) if n < QT else (0, 0)

        def keys(n):
            return [*range(*window(n)), *range(QT, NTT)]

        def v(name, i, n=1):
            a = _cols[name][0] + i
            return vec[:, a:a + n]

        def mod(layer, which, k, src):
            return modT[:, layer, which * KT + k, src:src + 1]

        def wl(w, b, off):
            return w[:, b % RING, off:off + P]

        block = ctx.enter_context(nc.Block())

        @block.sync
        def _(sp):
            def load_small(name, dst):
                sp.dma_start(dst, ins[name]).then_inc(sem("small"), 16)

            def load_block(b, slot):
                sp.dma_start(raw[:, slot, :], ins["stream"][b]).then_inc(sem(f"raw{slot}"), 16)

            for h in range(2):
                sp.dma_start(X[:, 4 * h:4 * h + 4, 0:T], ins["xT"][:, 4 * h:4 * h + 4, :]).then_inc(sem(f"x{h}"), 16)
            sp.dma_start(vec[:, :], ins["vec"]).then_inc(sem("vec"), 16)
            for b in range(RING):
                load_block(b, b)
            load_small("sel4", sel4[:, :])
            load_small("csd", csd)
            load_small("fmap", fmap)
            sp.dma_start(dft.rearrange("p a b c -> p (a b c)"), ins["dft"]).then_inc(sem("dft"), 16)
            sp.dma_start(ident[:, :], ins["ident"]).then_inc(sem("tables"), 16)
            sp.dma_start(X[:, :, T:TT], ins["ctxT"]).then_inc(sem("tables"), 16)
            with sp.Fori(1, N_BLOCKS // RING) as i:
                for s in range(RING):
                    sp.wait_ge(*when("w_used", RING * i + (s + 1 - RING)))
                    load_block(RING * i + s, s)
            for b in range(N_BLOCKS // RING * RING, N_BLOCKS):
                sp.wait_ge(*when("w_used", b + 1 - RING))
                load_block(b, b % RING)

            for h in range(2):
                sp.wait_ge(*when("l4_res", 4 * h + 4))
                sp.dma_start(out[:, 4 * h:4 * h + 4, :], X[:, 4 * h:4 * h + 4, 0:T]).then_inc(sem("stored"), 16)
            sp.wait_ge(*when("stored", 32))

        @block.gpsimd
        def _(pool):
            def split(s, loaded, nth):
                pool.wait_ge(*when(f"raw{s}", loaded))
                pool.sem_inc(sem("w_turn"), 1)
                pool.tensor_scalar(whi[:, s, :], raw[:, s, :], 1.0, 1.0, ALU.mult, ALU.mult).then_inc(sem("w_hi"), 1)
                pool.wait_ge(*when("w_hi", nth))
                pool.tensor_tensor(wlo[:, s, :], raw[:, s, :], whi[:, s, :], ALU.subtract).then_inc(sem("w_split"), 1)

            with pool.Fori(0, N_BLOCKS // RING) as i:
                for s in range(RING):
                    split(s, 16 * i + 16, RING * i + s + 1)
            for b in range(N_BLOCKS // RING * RING, N_BLOCKS):
                split(b % RING, 16 * (b // RING) + 16, b + 1)

        @block.tensor
        def _(pe):
            def gemm(dst, lhs_off, b, kn, rhs, cols, rhs_ready=None):
                mm = None
                for k in range(kn):
                    if rhs_ready:
                        rhs_ready(k)
                    for w, part in ((whi, 0), (whi, 1), (wlo, 0)):
                        for c, (c0, n) in enumerate(cols):
                            mm = pe.matmul(dst[c], wl(w, b, lhs_off(k)), rhs(k, part, c0, n),
                                           start=(k == 0 and w is whi and part == 0),
                                           stop=(k == kn - 1 and w is wlo))
                return mm

            def a_rhs(k, part, c0, n):
                return (Ahi, Alo)[part][:, k, c0:c0 + n]

            def h_rhs(slot):
                return lambda k, part, c0, n: (hhi, hlo)[part][:, slot, k, c0:c0 + n]

            def on_tile(name):
                return lambda k: pe.wait_ge(*when(name, k + 1))

            def column_sums(name, bank, cols, src, src_ready):
                for k in range(KT):
                    pe.wait_ge(*when(src_ready, k + 1))
                    for c, (c0, n) in enumerate(cols):
                        mm = pe.matmul(ps[:, bank + c, 0:n], ones[:, :], src(k)[:, c0:c0 + n],
                                       start=(k == 0), stop=(k == KT - 1))
                    mm.then_inc(sem(name), 1)

            def squares(k):
                return tmp[:, k % 4, :]

            def rms(name, bank):
                column_sums(f"{name}_sum", bank, X_ONLY, squares, f"{name}_sq")

            def layernorm(name, cols, bank, x_ready, x_before):
                for k in range(KT):
                    pe.wait_ge(*when(x_ready, x_before + k + 1))
                    for c, (c0, n) in enumerate(cols):
                        mm = pe.matmul(ps[:, bank + c, 0:n], ones[:, :], X[:, k, c0:c0 + n],
                                       start=(k == 0), stop=(k == KT - 1))
                mm.then_inc(sem(f"{name}_mu"), 1)
                column_sums(f"{name}_sum", bank + 2, cols, squares, f"{name}_sq")

            def done(mm, name, ends_block):
                mm.then_inc(sem("w_used" if ends_block else name), 1)

            def dense(name, b0, n_jobs, cols, ready, banks=4):
                for j in range(n_jobs):
                    b = b0 + j // 2
                    if j % 2 == 0:
                        pe.wait_ge(*when("w_split", b + 1))
                    if j >= banks:
                        pe.wait_ge(*when(f"{name}_evac", j - banks + 1))
                    dst = [ps[:, (j % banks) * len(cols) + c, 0:n] for c, (_, n) in enumerate(cols)]
                    mm = gemm(dst, lambda k: k * 256 + (j % 2) * P, b, KT, a_rhs, cols, on_tile(ready) if j == 0 and ready else None)
                    done(mm, f"{name}_done", j % 2 == 1)

            pe.wait_ge(*when("setup", 1))
            rms("n1", 0)
            for j in range(12):
                if j == 8:
                    pe.wait_ge(*when("small", 16 * N_SMALL))
                    for c in range(2):
                        mm = pe.matmul(ps[:, 4 + c, :], csd[:, c * P:(c + 1) * P], fmap, start=True, stop=True)
                    mm.then_inc(sem("csm_done"), 1)
                if j % 2 == 0:
                    pe.wait_ge(*when("w_split", B_WIN + j // 2 + 1))
                if j == 0:
                    pe.wait_ge(*when("n1_std", 1))
                if j >= 4:
                    pe.wait_ge(*when("u", (1, 2, 2, 2, 3, 4, 4, 4)[j - 4]))
                mm = gemm([ps[:, j % 4, :]], lambda k: k * 256 + (j % 2) * P, B_WIN + j // 2, KT, a_rhs, X_ONLY,
                          on_tile("n1_out") if j == 0 else None)
                done(mm, "win_done", j % 2 == 1)
            for h in range(HEADS_A):
                pe.wait_ge(*when("pf", h + 1))
                if h == 0:
                    pe.wait_ge(*when("csm", 2))
                else:
                    if h >= 2:
                        pe.wait_ge(*when("z", h - 1))
                zb = (4 + 2 * (h % 2)) * 512
                for t in range(QT):
                    mm = pe.matmul(psf[:, zb + t * 256:zb + (t + 1) * 256], pf[:, h, t * P:(t + 1) * P], csm[:, h, :],
                                   start=True, stop=True)
                mm.then_inc(sem("z_done"), 1)
            for h in range(HEADS_A):
                pe.wait_ge(*when("z", h + 1))
                if h == 0:
                    pe.wait_ge(*when("dft", 16))
                for t in range(QT):
                    for c in range(2):
                        mm = pe.matmul(ps[:, h, :], zz[:, h % 2, t * 256 + c * P:t * 256 + (c + 1) * P], dft[:, c, t, :],
                                       start=(t == 0 and c == 0), stop=(t == QT - 1 and c == 1))
                mm.then_inc(sem("y_done"), 1)
            for h in range(4):
                pe.wait_ge(*when("conv", h + 1))
                pe.matmul(ps[:, 4 + h, :], ones[:, :], conv[:, h, :], start=True, stop=True).then_inc(sem("cmu"), 1)
            for h in range(4):
                pe.wait_ge(*when("csq", h + 1))
                if h == 0:
                    pe.wait_ge(*when("mix_out", 4))
                pe.matmul(ps[:, h, :], ones[:, :], tmp[:, h, 0:T], start=True, stop=True).then_inc(sem("cvar"), 1)
            pe.wait_ge(*when("cstd", 4))
            dense("wout", B_WOUT, 8, X_ONLY, "mix_out")

            def ada(b, slot, e):
                pe.wait_ge(*when("w_split", b + 1))
                for k in range(KT):
                    for w in (whi, wlo):
                        mm = pe.matmul(ps[:, 6 + e, 0:256], c4[:, k, :], w[:, slot, k * 256:(k + 1) * 256],
                                       start=(k == 0 and w is whi), stop=(k == KT - 1 and w is wlo))
                mm.then_inc(sem("w_used"), 1)

            def ada_select(name, pairs):
                pe.wait_ge(*when(f"{name}_arow", 2 * pairs))
                for j in range(4):
                    mm = pe.matmul(ps[:, 6, 2 * j:2 * j + 2], arow[0:4, j // 2, (j % 2) * P:(j % 2 + 1) * P],
                                   sel4[:, :], start=True, stop=True)
                mm.then_inc(sem(f"{name}_sel"), 1)

            def swiglu(f, name, ready):
                B0 = B_FF[f]

                def up(i, b, at, first):
                    for part in range(2):
                        ada(b + 2 * part, (at + 2 * part) % RING, part)
                        pe.wait_ge(*when("w_split", b + 2 * part + 2))
                        for j in range(2):
                            if not first:
                                pe.wait_ge(*when(f"{name}_silu" if part == 0 else f"{name}_mul", 2 * i + j - 1))
                            mm = gemm([ps[:, 2 * part + j, :]], lambda k: k * 256 + j * P, at + 2 * part + 1, KT, a_rhs, X_ONLY,
                                      on_tile(ready) if first and part + j == 0 else None)
                            done(mm, f"{name}_up", j == 1)
                    ada_select(name, i + 1)

                def down(i, b_d, at, slot):
                    pe.wait_ge(*when("w_split", b_d + 1))
                    pe.wait_ge(*when(f"{name}_h", 2 * i + 2))
                    for m in range(KT):
                        pe.wait_ge(*when(f"{name}_dfree", 8 * i + m + 7))
                        mm = gemm([ps[:, 4 + m % 2, :]], lambda k: k * D + m * P, at, 2, h_rhs(slot), X_ONLY)
                        done(mm, f"{name}_down", m == KT - 1)

                up(0, B0, B0, True)

                def step(i, b, at, s):
                    pe.wait_ge(*when(f"{name}_ada", i + 1))
                    up(i + 1, b, at, False)
                    down(i, b + 4, at + 4, s)

                with pe.Fori(0, FF_IT // 3) as p:
                    for s in range(3):
                        at = B0 + 4 + 5 * s
                        step(3 * p + s, 15 * p + at, at, s)
                for i in range(FF_IT // 3 * 3, FF_IT - 1):
                    b = B0 + 4 + 5 * i
                    step(i, b, b, i % 3)
                i = FF_IT - 1
                b = B0 + 4 + 5 * i
                pe.wait_ge(*when(f"{name}_ada", i + 1))
                for e in range(2):
                    ada(b + e, (b + e) % RING, e)
                ada_select(name, i + 2)
                down(i, b + 2, b + 2, i % 3)

            rms("n2", 5)
            pe.wait_ge(*when("c4", 3))
            swiglu(0, "ff0", "n2_out")
            rms("n3", 0)
            pe.wait_ge(*when("w_split", B_POOL + 1))
            for g in range(4):
                pe.wait_ge(*when("pool_in", g + 1))
                for m in range(2):
                    j = 2 * g + m
                    if j >= 4:
                        pe.wait_ge(*when("pool_evac", j - 3))
                    mm = gemm([ps[:, 4 + j % 4, :]], lambda k: k * D + g * 256 + m * P, B_POOL, 2,
                              lambda k, part, c0, n: a_rhs(2 * g + k, part, c0, n), X_ONLY)
                    done(mm, "pool_done", j == 7)
            rms("n4", 0)
            swiglu(1, "ff1", "n4_out")
            rms("n5", 0)

            for j in range(3):
                b = B_KV + j // 2
                if j != 1:
                    pe.wait_ge(*when("w_split", b + 1))
                if j == 2:
                    pe.wait_ge(*when("kvA_evac", 1))
                dst = [ps[:, 4 + 2 * (j % 2) + c, 0:n] for c, (_, n) in enumerate(X_CTX)]
                mm = gemm(dst, lambda k: k * 256 + (j % 2) * P, b, KT, a_rhs, X_CTX, on_tile("n5_out") if j == 0 else None)
                done(mm, "kvA_done", j >= 1)
            pe.wait_ge(*when("kvA_evac", 3))
            for t in range(NTT):
                mm = pe.transpose(psf[:, 4 * 512 + t * P:4 * 512 + (t + 1) * P], vT[:, t * P:(t + 1) * P], ident[:, :])
            mm.then_inc(sem("vA_done"), 1)

            dense("qA", B_WQA, 8, X_CTX, None, banks=2)

            def window_scores(u, q_tile, half, n):
                rows = slice(DH * half, DH * half + DH)
                q = q_tile[rows, n * P:(n + 1) * P]
                mid = 2 * (u % 2) * 512 + 512
                first, last = window(n)
                if last > first:
                    a = mid - (last - first) * P
                    ends = [k for k in (first, last - 1) if k != n]
                    pe.matmul(psf[:, a:mid], q, kcur[rows, first * P:last * P], start=True, stop=False, skip_group_check=True)
                    for k in ends:
                        at = a + (k - first) * P
                        pe.matmul(psf[:, at:at + P], maskb[:, 0, :], maskb[:, 1 if k < n else 2, :], start=False,
                                  stop=(k == ends[-1]), skip_group_check=True)
                return pe.matmul(psf[:, mid:mid + C], q, kcur[rows, T:TT], start=True, stop=True)

            def window_turn(u, n, unit):
                pe.wait_ge(*when("pA", unit + 1))
                pe.wait_ge(*when("ptA", unit + 1))
                for t in range(len(keys(n))):
                    mm = pe.transpose(psf[:, 4 * 512 + t * P:4 * 512 + (t + 1) * P], probA[u % 3][:, t * P:(t + 1) * P],
                                      ident[:, :])
                mm.then_inc(sem("turnA"), 1)

            def window_values(n, unit, nth):
                pe.wait_ge(*when("ptA", unit + 2))
                pe.wait_ge(*when("oA", nth + 1))
                ks = keys(n)
                for t, k in enumerate(ks):
                    mm = pe.matmul(ps[0:DH, 6, :], vcur[:, k, :], ptA[:, t, :], start=(t == 0), stop=(t == len(ks) - 1))
                mm.then_inc(sem("oA_done"), 1)

            pe.wait_ge(*when("maskb", 2))
            pe.sem_inc(sem("turnA"), 3)
            pe.sem_inc(sem("oA_done"), 1)
            with pe.Fori(0, 2) as g:
                pe.wait_ge(*when("kvcur", 2 * g + 2))
                for u in range(N_UNITS + 3):
                    unit = N_UNITS * g + u
                    if u < N_UNITS:
                        e, n, h = UNITS[u]
                        if n == 0 and h == 0:
                            pe.wait_ge(*when("qcur", 2 * g + e + 1))
                        pe.wait_ge(*when("sA_free", unit + 1))
                        window_scores(u, qcur[e][:, h // 2, :], h % 2, n).then_inc(sem("sA"), 1)
                    if 2 <= u < N_UNITS + 2:
                        window_turn(u - 2, UNITS[u - 2][1], unit - 2)
                    if u >= 3 and UNITS[u - 3][2] == 3:
                        window_values(UNITS[u - 3][1], unit - 3, N_UNITS // 4 * g + (u - 3) // 4)
            dense("woA", B_WOA, 8, X_CTX, "OA_split", banks=2)
            layernorm("l1", X_CTX, 4, "woA_evac", 0)

            def mlp(l, name, cols, ready):
                B0 = B_ML[l]

                def up(i, b_u, at, first):
                    pe.wait_ge(*when("w_split", b_u + 1))
                    for j in range(2):
                        if not first:
                            pe.wait_ge(*when(f"{name}_relu", 2 * i + j - 1))
                        dst = [ps[:, 2 * j + c, 0:n] for c, (_, n) in enumerate(cols)]
                        mm = gemm(dst, lambda k: k * 256 + j * P, at, KT, a_rhs, cols,
                                  on_tile(ready) if first and j == 0 else None)
                        done(mm, f"{name}_up", j == 1)

                def down(i, b_d, at, slot):
                    pe.wait_ge(*when("w_split", b_d + 1))
                    pe.wait_ge(*when(f"{name}_h", 2 * i + 2))
                    for m in range(KT):
                        pe.wait_ge(*when(f"{name}_dfree", 8 * i + m + 7))
                        dst = [ps[:, 4 + 2 * (m % 2) + c, 0:n] for c, (_, n) in enumerate(cols)]
                        mm = gemm(dst, lambda k: k * D + m * P, at, 2, h_rhs(slot), cols)
                        done(mm, f"{name}_down", m == KT - 1)

                up(0, B0, B0, True)
                with pe.Fori(0, (ML_IT - 1) // 3) as p:
                    for s in range(3):
                        i = 3 * p + s
                        at = B0 + 1 + 2 * s
                        up(i + 1, 6 * p + at, at, False)
                        down(i, 6 * p + at + 1, at + 1, s)
                i = ML_IT - 1
                down(i, B0 + 1 + 2 * i, B0 + 1 + 2 * i, i % 3)

            mlp(0, "ml0", X_CTX, "l1_out")
            layernorm("l2", X_CTX, 0, "ml0_dfree", 8 * ML_IT)

            def diff_turn(u, unit):
                pe.wait_ge(*when("pB", unit + 1))
                pe.wait_ge(*when("aT", unit + 1))
                for t in range(NTT):
                    mm = pe.transpose(psf[:, 4 * 512 + t * P:4 * 512 + (t + 1) * P], probB[u % 3][0][:, t * P:(t + 1) * P],
                                      ident[:, :])
                mm.then_inc(sem("turnB"), 1)

            def diff_values(hh, unit, nth):
                pe.wait_ge(*when("aT", unit + 2))
                pe.wait_ge(*when("oB", nth + 1))
                for t in range(NTT):
                    mm = pe.matmul(ps[:, 6, :], vB[:, t, hh * P:(hh + 1) * P], aT[:, t, :],
                                   start=(t == 0), stop=(t == NTT - 1))
                mm.then_inc(sem("oB_done"), 1)

            on = on_tile("l2_out")
            for k in range(KT):
                on(k)
            pe.sem_inc(sem("turnB"), 3)
            pe.sem_inc(sem("oB_done"), 1)
            with pe.Fori(0, 4) as st:
                pe.wait_ge(*when("oB", 2 * st + 1))
                job = 0
                for which in range(2):
                    pe.wait_ge(*when("w_split", 3 * st + (B_QKV + which + 1)))
                    for m in range(2):
                        for c, (c0, n) in enumerate(X_CTX[:1 + which]):
                            pe.wait_ge(*when(f"qkB_free{job % 2}", 3 * st + job // 2 + 1))
                            mm = gemm([ps[:, 6 + job % 2, 0:n]], lambda k: k * 256 + m * P, B_QKV + which, KT, a_rhs, [(c0, n)])
                            done(mm, "qkB_done", m == 1 and c == which)
                            job += 1
                pe.wait_ge(*when("w_split", 3 * st + (B_QKV + 3)))
                pe.wait_ge(*when("aT", 8 * st + 1))
                for t in range(NTT):
                    pe.wait_ge(*when("vB", 6 * st + t + 1))
                    for k in range(KT):
                        for a, w in ((Ahi, whi), (Alo, whi), (Ahi, wlo)):
                            mm = pe.matmul(ps[:, 4 + t % 2, 0:256], a[:, k, t * P:(t + 1) * P],
                                           w[:, (B_QKV + 2) % RING, k * 256:(k + 1) * 256],
                                           start=(k == 0 and a is Ahi and w is whi), stop=(k == KT - 1 and w is wlo))
                    done(mm, "vB_done", t == NTT - 1)
                pe.wait_ge(*when("qkB", 4 * st + 6))
                pe.wait_ge(*when("qkB_free1", 3 * st + 4))
                pe.wait_ge(*when("vB", 6 * st + 8))
                for u in range(11):
                    if u < 8:
                        hh, n = u // 4, u % 4
                        for t in range(2):
                            rows = slice(DH * t, DH * t + DH)
                            pe.wait_ge(*when("sB_free", 16 * st + 2 * u + t + 1))
                            for half in range(2):
                                a = 2 * t * 512 + P + half * 384
                                mm = pe.matmul(psf[:, a:a + 384], qB[rows, hh, n * P:(n + 1) * P],
                                               kB[rows, hh, half * 384:half * 384 + 384], start=True, stop=True)
                            mm.then_inc(sem("sB"), 1)
                    if 2 <= u < 10:
                        diff_turn(u - 2, 8 * st + u - 2)
                    if u >= 3 and u % 4 == 2:
                        diff_values((u - 3) // 4, 8 * st + u - 3, 2 * st + (u - 3) // 4)
            for h in range(8):
                pe.wait_ge(*when("oB_sq", h + 1))
                if h >= 4:
                    pe.wait_ge(*when("oB_std", h - 3))
                pe.matmul(ps[:, h % 4, :], ones[:, :], tmp[:, h % 4, 0:T], start=True, stop=True).then_inc(sem("oB_ms"), 1)
            dense("woB", B_WOB, 8, X_ONLY, "OB_split")
            layernorm("l3", X_ONLY, 4, "woB_evac", 0)
            mlp(1, "ml1", X_ONLY, "l3_out")
            layernorm("l4", X_ONLY, 0, "ml1_dfree", 8 * ML_IT)

        @block.scalar
        def _(act):
            def copy(dst, src, scale=1.0):
                return act.activation(dst, src, ACT.Copy, scale=scale)

            def norm_squares(name, src, ready, before, each, width):
                for k in range(KT):
                    if ready == "x":
                        act.wait_ge(*when(f"x{k // 4}", 16))
                    else:
                        act.wait_ge(*when(ready, before + each * (k + 1)))
                    if k >= 4:
                        act.wait_ge(*when(f"{name}_sum", k - 3))
                    act.activation(tmp[:, k % 4, 0:width], src[:, k, 0:width], ACT.Square).then_inc(sem(f"{name}_sq"), 1)

            def norm_std(name, bank, cols, eps):
                act.wait_ge(*when(f"{name}_sum", KT))
                for c, (c0, n) in enumerate(cols):
                    act.activation(std[:, c0:c0 + n], ps[:, bank + c, 0:n], ACT.Sqrt, scale=1.0 / D,
                                   bias=epsr[:, eps:eps + 1]).then_inc(sem(f"{name}_std"), 1)

            def split_hi(name, src, ready, each, width):
                for k in range(KT):
                    act.wait_ge(*when(ready, each * (k + 1)))
                    copy(Ahi[:, k, 0:width], src(k)).then_inc(sem(f"{name}_hi"), 1)

            def normed(k):
                return tmp[:, k % 4, 0:T]

            def rms(name, bank, ready, before, split=True):
                norm_squares(name, X, ready, before, 1, T)
                norm_std(name, bank, X_ONLY, 0)
                if split:
                    split_hi(name, normed, f"{name}_y", 1, T)

            def layernorm(name, cols, bank, last=False):
                width = sum(n for _, n in cols)
                norm_squares(name, X, f"{name}_d", 0, len(cols), width)
                norm_std(name, bank, cols, 1)
                if not last:
                    split_hi(name, lambda k: modin[:, k % 2, 0:width], f"{name}_m", len(cols), width)

            act.wait_ge(*when("setup", 4))
            rms("n1", 0, "x", 0)
            act.wait_ge(*when("lam", 2))
            act.activation(lamt[:, 2:4], lamt[:, 0:2], ACT.Exp).then_inc(sem("lam"), 1)

            for t, j in enumerate((2, 3, 6, 7)):
                if j % 2:
                    act.wait_ge(*when("w_used", B_WIN + j // 2 + 1))
                else:
                    act.wait_ge(*when("win_done", j // 2 + 1))
                act.activation(tmp[:, t, 0:T], ps[:, j % 4, :], ACT.Sigmoid).then_inc(sem("sig"), 1)
            act.wait_ge(*when("csm_done", 1))
            for c in range(2):
                copy(csm[:, :, c * P:(c + 1) * P], ps[:, 4 + c, :].rearrange("p (h e) -> p h e", h=HEADS_A)).then_inc(sem("csm"), 1)
            for h in range(HEADS_A):
                j = 8 + h
                if j % 2:
                    act.wait_ge(*when("w_used", B_WIN + j // 2 + 1))
                else:
                    act.wait_ge(*when("win_done", j // 2 + 1))
                copy(pf[:, h, :], ps[:, h, :]).then_inc(sem("pf"), 1)

            def fourier_mid(h):
                act.wait_ge(*when("z_done", h + 1))
                if h >= 2:
                    act.wait_ge(*when("y_done", h - 1))
                zb = (4 + 2 * (h % 2)) * 512
                copy(zz[:, h % 2, :], psf[:, zb:zb + 1024]).then_inc(sem("z"), 1)

            def fourier_out(h):
                act.wait_ge(*when("y_done", h + 1))
                copy(Ahi[:, h, 0:T], ps[:, h, :]).then_inc(sem("mix_hi"), 1)

            fourier_mid(0)
            fourier_mid(1)
            for h in range(2, HEADS_A):
                fourier_mid(h)
                fourier_out(h - 2)
            fourier_out(2)
            fourier_out(3)
            act.activation(csil[:, :, :], v("c", 0, 2 * KT).rearrange("p (k s) -> p k s", s=2), ACT.Silu).then_inc(sem("csil"), 1)
            act.wait_ge(*when("csil", 1))
            act.wait_ge(*when("c4", 1))
            copy(c4[:, :, 0:2], csil[:, :, :]).then_inc(sem("c4"), 1)
            for h in range(4):
                act.wait_ge(*when("cd", h + 1))
                act.activation(tmp[:, h, 0:T], conv[:, h, :], ACT.Square).then_inc(sem("csq"), 1)
            for h in range(4):
                act.wait_ge(*when("cvar", h + 1))
                act.activation(pf[:, h, :], ps[:, h, :], ACT.Sqrt, scale=1.0 / P, bias=epsr[:, 1:2]).then_inc(sem("cstd"), 1)
            for h in range(4):
                act.wait_ge(*when("cy", h + 1))
                act.activation(tmp[:, h, 0:T], conv[:, h, :], ACT.Silu, bias=v("conv_ln_b", h)).then_inc(sem("csilu"), 1)
            for h in range(4):
                act.wait_ge(*when("csilu", h + 1))
                copy(Ahi[:, 4 + h, 0:T], tmp[:, h, 0:T]).then_inc(sem("mix_hi"), 1)

            def swiglu(f, name):
                B0 = B_FF[f]

                def rows(b_a, gap):
                    for e in range(2):
                        act.wait_ge(*when("w_used", b_a + gap * e + 1))
                        copy(arow[:, e, :], ps[0:4, 6 + e, 0:256]).then_inc(sem(f"{name}_arow"), 1)

                def step(i, b, slot, first):
                    rows(b, 2)
                    for j in range(2):
                        if j:
                            act.wait_ge(*when("w_used", b + 2))
                        else:
                            act.wait_ge(*when(f"{name}_up", 2 * i + 1))
                        if not first:
                            act.wait_ge(*when(f"{name}_mul", 2 * i + j - 1))
                        act.activation(tmp[:, 2 + j, 0:T], ps[:, j, :], ACT.Silu).then_inc(sem(f"{name}_silu"), 1)
                    for j in range(2):
                        act.wait_ge(*when(f"{name}_mul", 2 * i + j + 1))
                        copy(hhi[:, slot, j, 0:T], tmp[:, j, 0:T]).then_inc(sem(f"{name}_hi"), 1)

                step(0, B0, 0, True)
                with act.Fori(0, FF_IT // 3) as p:
                    for s in range(3):
                        step(3 * p + s + 1, 15 * p + (B0 + 4 + 5 * s), (s + 1) % 3, False)
                for i in range(FF_IT // 3 * 3 + 1, FF_IT):
                    step(i, B0 + 5 * i - 1, i % 3, False)
                rows(B0 + 4 + 5 * (FF_IT - 1), 1)

            rms("n2", 5, "wout_evac", 0)
            act.dma_start(icnt.rearrange("p a b -> p (a b)"), ins["icnt"]).then_inc(sem("icnt"), 16)
            swiglu(0, "ff0")
            rms("n3", 0, "ff0_dfree", 8 * FF_IT, split=False)
            for k in range(KT):
                act.wait_ge(*when("pool_y", k // 2 + 1))
                copy(Ahi[:, k, 0:T], tmp[:, k % 4, 0:T]).then_inc(sem("pool_hi"), 1)
            rms("n4", 0, "pool_evac", 0)
            for name, dst in (("cosq", cosq), ("sinq", sinq), ("masks", masks.rearrange("p a k -> p (a k)"))):
                act.dma_start(dst, ins[name]).then_inc(sem("tables"), 16)
            swiglu(1, "ff1")
            rms("n5", 0, "ff1_dfree", 8 * FF_IT, split=False)
            split_hi("n5", lambda k: modin[:, k % 2, :], "n5_m", 2, TT)

            def swap_halves(slot, src, scale):
                for q in range(4):
                    mm = copy(swap[32 * q:32 * q + 32, slot, :], src[32 * (q ^ 1):32 * (q ^ 1) + 32, :], scale)
                return mm

            act.wait_ge(*when("tables", 16 * 5))
            copy(maskb[:, 0, :], ident[:, :]).then_inc(sem("maskb"), 1)
            copy(maskb[:, 1:3, :], masks).then_inc(sem("maskb"), 1)
            for j in range(2):
                if j:
                    act.wait_ge(*when("w_used", B_KV + 1))
                else:
                    act.wait_ge(*when("kvA_done", 1))
                bank = 4 + 2 * j
                copy(kd[:, j, T:TT], ps[:, bank + 1, 0:C])
                swap_halves(j, ps[:, bank, :], 1.0).then_inc(sem("kvA_swap"), 1)
            act.wait_ge(*when("w_used", B_KV + 2))
            act.wait_ge(*when("kvA_evac", 1))
            copy(vT[:, 0:T], ps[:, 4, :])
            copy(vT[:, T:TT], ps[:, 5, 0:C]).then_inc(sem("kvA_evac"), 1)
            for j in range(8):
                if j % 2:
                    act.wait_ge(*when("w_used", B_WQA + j // 2 + 1))
                else:
                    act.wait_ge(*when("qA_done", j // 2 + 1))
                bank = 2 * (j % 2)
                copy(O[:, j, T:TT], ps[:, bank + 1, 0:C], SCALE)
                if j < 2:
                    act.wait_ge(*when("kvA_evac", 3))
                else:
                    act.wait_ge(*when("qA_evac", j - 1))
                swap_halves(j % 2, ps[:, bank, :], SCALE).then_inc(sem("qA_swap"), 1)

            act.sem_inc(sem("ptA"), 1)
            act.sem_inc(sem("sA_free"), 2)
            with act.Fori(0, 2) as g:
                for u in range(N_UNITS + 2):
                    if u < N_UNITS:
                        e, n, h = UNITS[u]
                        unit = N_UNITS * g + u
                        W = len(keys(n)) * P
                        a = 2 * (u % 2) * 512 + 512 + C - W
                        c = sm[:, u % 4, :]
                        sink = vec[:, bass.ds(8 * g + (_cols["sink"][0] + 4 * e + h), 1)]
                        act.wait_ge(*when("nmA", unit + 1))
                        act.wait_ge(*when("turnA", unit + 1))
                        act.activation(probA[u % 3][:, 0:W], psf[:, a:a + W], ACT.Exp, bias=c[:, 1:2],
                                       accum_out=c[:, 2:3]).then_inc(sem("sA_free"), 1)
                        act.activation(c[:, 3:4], sink, ACT.Exp, bias=c[:, 1:2]).then_inc(sem("esA"), 1)
                    if u >= 2:
                        e, n, h = UNITS[u - 2]
                        nk = len(keys(n))
                        act.wait_ge(*when("turnA", N_UNITS * g + u - 2 + 4))
                        act.wait_ge(*when("oA_done", N_UNITS // 4 * g + (u - 2) // 4 + 1))
                        copy(ptA[:, 0:nk, h * P:(h + 1) * P],
                             psf[:, 4 * 512:4 * 512 + nk * P].rearrange("p (t q) -> p t q", t=nk)).then_inc(sem("ptA"), 1)
            for k in range(KT):
                if k == 0:
                    act.wait_ge(*when("oA", 25))
                copy(Ahi[:, k, :], O[:, k, :]).then_inc(sem("OA_hi"), 1)
            layernorm("l1", X_CTX, 6)

            def mlp(l, name, cols):
                B0 = B_ML[l]
                width = sum(n for _, n in cols)

                def step(i, b_u, slot, first):
                    for j in range(2):
                        if j:
                            act.wait_ge(*when("w_used", b_u + 1))
                        else:
                            act.wait_ge(*when(f"{name}_up", i + 1))
                        if not first:
                            act.wait_ge(*when(f"{name}_mul", 2 * i + j - 1))
                        for c, (c0, n) in enumerate(cols):
                            mm = act.activation(tmp[:, 2 + j, c0:c0 + n], ps[:, 2 * j + c, 0:n], ACT.Relu)
                        mm.then_inc(sem(f"{name}_relu"), 1)
                    for j in range(2):
                        act.wait_ge(*when(f"{name}_mul", 2 * i + j + 1))
                        copy(hhi[:, slot, j, 0:width], tmp[:, j, 0:width]).then_inc(sem(f"{name}_hi"), 1)

                step(0, B0, 0, True)
                with act.Fori(0, (ML_IT - 1) // 3) as p:
                    for s in range(3):
                        step(3 * p + s + 1, 6 * p + (B0 + 1 + 2 * s), (s + 1) % 3, False)

            mlp(0, "ml0", X_CTX)
            layernorm("l2", X_CTX, 2)

            act.sem_inc(sem("aT"), 1)
            act.sem_inc(sem("vB"), 2)
            act.sem_inc(sem("sB_free"), 2)
            with act.Fori(0, 4) as st:
                b = 3 * st + B_QKV

                def swapped(src, scale, nth):
                    act.wait_ge(*when("qkB", 4 * st + nth + 1))
                    swap_halves(nth % 2, src, scale).then_inc(sem("swB"), 1)

                act.wait_ge(*when("qkB_done", 4 * st + 1))
                swapped(ps[:, 6, :], SCALE, 0)
                act.wait_ge(*when("w_used", b + 1))
                swapped(ps[:, 7, :], SCALE, 1)
                for m in range(2):
                    act.wait_ge(*when("qkB_done", 4 * st + 2 + 2 * m))
                    swapped(ps[:, 6, :], 1.0, 2 + m)
                    if m:
                        act.wait_ge(*when("w_used", b + 2))
                    else:
                        act.wait_ge(*when("qkB_done", 4 * st + 3))
                    copy(kB[:, m, T:TT], ps[:, 7, 0:C]).then_inc(sem("qkB_free1"), 1)
                for t in range(NTT):
                    if t < NTT - 1:
                        act.wait_ge(*when("vB_done", 5 * st + t + 1))
                    else:
                        act.wait_ge(*when("w_used", b + 3))
                    copy(vB[:, t, :], ps[:, 4 + t % 2, 0:256]).then_inc(sem("vB"), 1)
                for u in range(10):
                    if u < 8:
                        act.wait_ge(*when("turnB", 8 * st + u + (2 if u < 2 else 1)))
                        for t in range(2):
                            a = 2 * t * 512 + P
                            c = sm[:, u % 4, :]
                            act.wait_ge(*when("nmB", 16 * st + 2 * u + t + 1))
                            act.activation(probB[u % 3][t], psf[:, a:a + TT], ACT.Exp, bias=c[:, t:t + 1],
                                           accum_out=c[:, 2 + t:3 + t]).then_inc(sem("sB_free"), 1)
                    if u >= 2:
                        n = (u - 2) % 4
                        act.wait_ge(*when("turnB", 8 * st + u - 2 + 4))
                        act.wait_ge(*when("oB_done", 2 * st + (u - 2) // 4 + 1))
                        copy(aT[:, :, n * P:(n + 1) * P],
                             psf[:, 4 * 512:4 * 512 + TT].rearrange("p (t q) -> p t q", t=NTT)).then_inc(sem("aT"), 1)
            for i in range(12):
                if i < 8:
                    act.wait_ge(*when("oB_t", 2 * i + 2))
                    act.activation(tmp[:, i % 4, 0:T], tmp[:, i % 4, 0:T], ACT.Square).then_inc(sem("oB_sq"), 1)
                if 0 <= i - 2 < 8:
                    h = i - 2
                    act.wait_ge(*when("oB_flag", h + 1))
                    if h >= 2:
                        act.wait_ge(*when("oB_r", 3 * h - 4))
                    act.activation(aT[:, h % 2, :], ps[:, h % 4, :], ACT.Sqrt, scale=1.0 / P,
                                   bias=epsr[:, 2:3]).then_inc(sem("oB_std"), 1)
                if i >= 4:
                    h = i - 4
                    act.wait_ge(*when("oB_r", 3 * h + 3))
                    copy(Ahi[:, h, 0:T], O[:, h, 0:T]).then_inc(sem("OB_hi"), 1)
            layernorm("l3", X_ONLY, 6)
            mlp(1, "ml1", X_ONLY)
            layernorm("l4", X_ONLY, 2, last=True)

        @block.vector
        def _(dve):
            def split_lo(out_sem, hi_sem, k, src, width):
                dve.wait_ge(*when(hi_sem, k + 1))
                dve.tensor_tensor(Alo[:, k, 0:width], src, Ahi[:, k, 0:width], ALU.subtract).then_inc(sem(out_sem), 1)

            def norm_rstd(name, n_std, width):
                dve.wait_ge(*when(f"{name}_std", n_std))
                dve.reciprocal(rstd[:, 0:width], std[:, 0:width]).then_inc(sem(f"{name}_rstd"), 1)
                dve.wait_ge(*when(f"{name}_rstd", 1))

            def scaled(name, k, g, dst, width=T):
                return dve.scalar_tensor_tensor(out=dst, in0=X[:, k, 0:width], scalar=v(g[0], g[1] + k),
                                                in1=rstd[:, 0:width], op0=ALU.mult, op1=ALU.mult)

            def rms(name, g):
                norm_rstd(name, 1, T)
                for k in range(KT + 1):
                    if k < KT:
                        scaled(name, k, g, tmp[:, k % 4, 0:T]).then_inc(sem(f"{name}_y"), 1)
                    if k >= 1:
                        split_lo(f"{name}_out", f"{name}_hi", k - 1, tmp[:, (k - 1) % 4, 0:T], T)

            def modulate(name, k, use, src, cols, shared=None):
                for c, (c0, n) in enumerate(cols):
                    dve.tensor_scalar(modin[:, k % 2, c0:c0 + n], src[:, c0:c0 + n], s1[:, use, k, c:c + 1],
                                      s2[:, use, k, c:c + 1], ALU.mult, ALU.add).then_inc(sem(f"{name}_m"), 1)

            def layernorm(name, cols, bank, g, bias, use):
                width = sum(n for _, n in cols)
                dve.wait_ge(*when(f"{name}_mu", 1))
                for k in range(KT):
                    for c, (c0, n) in enumerate(cols):
                        dve.scalar_tensor_tensor(out=X[:, k, c0:c0 + n], in0=ps[:, bank + c, 0:n], scalar=-1.0 / D,
                                                 in1=X[:, k, c0:c0 + n], op0=ALU.mult, op1=ALU.add).then_inc(sem(f"{name}_d"), 1)
                dve.wait_ge(*when(f"{name}_d", len(cols) * KT))
                norm_rstd(name, len(cols), width)
                for k in range(KT + 1):
                    if k < KT:
                        t = tmp[:, k % 4, 0:width]
                        scaled(name, k, g, t, width).then_inc(sem(f"{name}_y"), 1)
                        dve.wait_ge(*when(f"{name}_y", k + 1))
                        dve.tensor_scalar(X[:, k, 0:width], t, v(bias[0], bias[1] + k), ALPHA if use is not None else 1.0,
                                          ALU.add, ALU.mult).then_inc(sem(f"{name}_res"), 1)
                        if use is not None:
                            modulate(name, k, use, t, cols)
                    if k >= 1 and use is not None:
                        split_lo(f"{name}_out", f"{name}_hi", k - 1, modin[:, (k - 1) % 2, 0:width], width)

            dve.memset(ones[:, :], 1.0).then_inc(sem("setup"), 1)
            for i, e in enumerate((RMS_EPS, LN_EPS, LN_EPS * SUB_SCALE * SUB_SCALE)):
                dve.memset(epsr[:, i:i + 1], e).then_inc(sem("setup"), 1)
            dve.memset(upad, 0.0).then_inc(sem("upad"), 1)
            dve.memset(c4[:, :, :].bitcast(F32), 0.0).then_inc(sem("c4"), 1)
            dve.wait_ge(*when("vec", 16))
            pairs = v("lq1", 0, 4 * DH).rearrange("p (i s d) -> p i s d", i=2, s=2)
            products = rstd[:, T:T + 2 * DH].rearrange("p (i d) -> p i d", i=2)
            dve.tensor_tensor(products, pairs[:, :, 0], pairs[:, :, 1], ALU.mult).then_inc(sem("lam"), 1)
            dve.wait_ge(*when("lam", 1))
            dve.tensor_reduce(lamt[:, 0:2], products, AX_X, ALU.add).then_inc(sem("lam"), 1)
            rms("n1", ("mix_g", 0))
            dve.wait_ge(*when("lam", 3))
            dve.tensor_tensor(lamt[:, 4:5], lamt[:, 2:3], lamt[:, 3:4], ALU.subtract).then_inc(sem("lam"), 1)
            dve.wait_ge(*when("lam", 4))
            dve.tensor_scalar(lamt[:, 5:6], lamt[:, 4:5], LAM_INIT, -1.0, ALU.add, ALU.mult).then_inc(sem("lam"), 1)
            dve.tensor_scalar(lamt[:, 6:7], v("subln_g", 0), 1.0 - LAM_INIT, SUB_SCALE, ALU.mult, ALU.mult).then_inc(sem("lam"), 1)

            dve.wait_ge(*when("upad", 1))
            for t, j in enumerate((0, 1, 4, 5)):
                dve.wait_ge(*when("sig", t + 1))
                dve.tensor_tensor(upad[:, t, PADC:PADC + T], ps[:, j % 4, :], tmp[:, t, 0:T], ALU.mult).then_inc(sem("u"), 1)
            dve.wait_ge(*when("u", 4))
            w = _cols["conv_w"][0]
            for t in range(4):
                dve.tensor_scalar(conv[:, t, :], upad[:, t, 0:T], vec[:, w + t * TAPS:w + t * TAPS + 1], v("conv_b", t),
                                  ALU.mult, ALU.add).then_inc(sem("tap"), 1)
            with dve.Fori(1, TAPS - 1) as tap:
                for t in range(4):
                    dve.wait_ge(*when("tap", 4 * tap + t - 3))
                    dve.scalar_tensor_tensor(out=conv[:, t, :], in0=upad[:, t, bass.ds(tap, T)],
                                             scalar=vec[:, bass.ds(tap + (w + t * TAPS), 1)], in1=conv[:, t, :],
                                             op0=ALU.mult, op1=ALU.add).then_inc(sem("tap"), 1)
            for t in range(4):
                last = w + t * TAPS + TAPS - 1
                dve.wait_ge(*when("tap", 4 * (TAPS - 1) + t - 3))
                dve.scalar_tensor_tensor(out=conv[:, t, :], in0=upad[:, t, TAPS - 1:TAPS - 1 + T], scalar=vec[:, last:last + 1],
                                         in1=conv[:, t, :], op0=ALU.mult, op1=ALU.add).then_inc(sem("conv"), 1)
            for h in range(HEADS_A):
                split_lo("mix_out", "mix_hi", h, ps[:, h, :], T)
            dve.wait_ge(*when("c4", 2))
            dve.tensor_tensor(c4[:, :, 2:4], csil[:, :, :], c4[:, :, 0:2], ALU.subtract).then_inc(sem("c4"), 1)
            for h in range(4):
                dve.wait_ge(*when("cmu", h + 1))
                dve.scalar_tensor_tensor(out=conv[:, h, :], in0=ps[:, 4 + h, :], scalar=-1.0 / P, in1=conv[:, h, :],
                                         op0=ALU.mult, op1=ALU.add).then_inc(sem("cd"), 1)
            for h in range(4):
                dve.wait_ge(*when("cstd", h + 1))
                dve.reciprocal(pf[:, h, :], pf[:, h, :]).then_inc(sem("crstd"), 1)
                dve.wait_ge(*when("crstd", h + 1))
                dve.wait_ge(*when("cd", h + 1))
                dve.scalar_tensor_tensor(out=conv[:, h, :], in0=conv[:, h, :], scalar=v("conv_ln_g", h), in1=pf[:, h, :],
                                         op0=ALU.mult, op1=ALU.mult).then_inc(sem("cy"), 1)
            for h in range(4):
                split_lo("mix_out", "mix_hi", 4 + h, tmp[:, h, 0:T], T)
            for j in range(8):
                if j % 2:
                    dve.wait_ge(*when("w_used", B_WOUT + j // 2 + 1))
                else:
                    dve.wait_ge(*when("wout_done", j // 2 + 1))
                dve.tensor_tensor(X[:, j, 0:T], ps[:, j % 4, :], X[:, j, 0:T], ALU.add).then_inc(sem("wout_evac"), 1)

            def swiglu(f, name):
                B0 = B_FF[f]
                dve.sem_inc(sem(f"{name}_dfree"), 8)

                def mods(pair):
                    dve.wait_ge(*when(f"{name}_sel", pair + 1))
                    a = _cols["b_ada"][0] + f * 2 * N_MOD * KT
                    dve.tensor_tensor(modT[:, f, bass.ds(4 * pair, 4), :].rearrange("p k s -> p (k s)"), ps[:, 6, 0:8],
                                      vec[:, bass.ds(8 * pair + a, 8)], ALU.add).then_inc(sem(f"{name}_ada"), 1)

                def hidden(i, b_u, j, first=False):
                    if j:
                        dve.wait_ge(*when("w_used", b_u + 1))
                    else:
                        dve.wait_ge(*when(f"{name}_up", 2 * i + 2))
                    dve.wait_ge(*when(f"{name}_silu", 2 * i + j + 1))
                    if not first:
                        dve.wait_ge(*when(f"{name}_h", 2 * i + j - 1))
                    dve.tensor_tensor(tmp[:, j, 0:T], ps[:, 2 + j, :], tmp[:, 2 + j, 0:T], ALU.mult).then_inc(sem(f"{name}_mul"), 1)

                def hidden_lo(i, slot, j):
                    dve.wait_ge(*when(f"{name}_hi", 2 * i + j + 1))
                    dve.tensor_tensor(hlo[:, slot, j, 0:T], tmp[:, j, 0:T], hhi[:, slot, j, 0:T],
                                      ALU.subtract).then_inc(sem(f"{name}_h"), 1)

                def add_down(i, b_d, m):
                    if m == KT - 1:
                        dve.wait_ge(*when("w_used", b_d + 1))
                    else:
                        dve.wait_ge(*when(f"{name}_down", 7 * i + m + 1))
                    dve.wait_ge(*when(f"{name}_dfree", 8 * i + m + 1))
                    dve.tensor_tensor(X[:, m, 0:T], ps[:, 4 + m % 2, :], X[:, m, 0:T], ALU.add).then_inc(sem(f"{name}_dfree"), 1)

                def step(i, b, slot):
                    for j in range(2):
                        hidden(i + 1, b + 3, j)
                    mods(i + 1)
                    for m in range(KT):
                        add_down(i, b + 4, m)
                        if m < 2:
                            hidden_lo(i + 1, slot, m)

                for j in range(2):
                    hidden(0, B0 + 3, j, True)
                mods(0)
                for j in range(2):
                    hidden_lo(0, 0, j)
                with dve.Fori(0, FF_IT // 3) as p:
                    for s in range(3):
                        step(3 * p + s, 15 * p + (B0 + 4 + 5 * s), (s + 1) % 3)
                for i in range(FF_IT // 3 * 3, FF_IT - 1):
                    step(i, B0 + 4 + 5 * i, (i + 1) % 3)
                mods(FF_IT)
                for m in range(KT):
                    add_down(FF_IT - 1, B0 + FF_BLOCKS - 1, m)

            rms("n2", ("ffn_g", 0))
            swiglu(0, "ff0")

            for a in (0, PADP + T):
                dve.memset(hp[:, :, a:a + PADP], 0.0).then_inc(sem("hp"), 1)
            norm_rstd("n3", 1, T)
            for k in range(KT):
                scaled("n3", k, ("mix_g", KT), hp[:, k, PADP:PADP + T]).then_inc(sem("hp"), 1)
            dve.wait_ge(*when("icnt", 16))
            n_win = 0
            for g in range(5):
                if g < 4:
                    dve.wait_ge(*when("hp", 2 + 2 * g + 2))
                    if g:
                        dve.wait_ge(*when("pool_y", g))
                    src, width = hp[:, 2 * g:2 * g + 2, :], HPAD
                    for d in range(g + 1):
                        dst = (pa, pb)[d % 2]
                        width -= 1 << d
                        if d:
                            dve.wait_ge(*when("win", n_win))
                        dve.tensor_tensor(dst[:, :, 0:width], src[:, :, 0:width], src[:, :, 1 << d:(1 << d) + width],
                                          ALU.add).then_inc(sem("win"), 1)
                        n_win += 1
                        src = dst
                    start = PADP - (1 << g)
                    other = (pb, pa)[g % 2]
                    dve.wait_ge(*when("win", n_win))
                    for m in range(2):
                        dve.tensor_tensor(other[:, m, 0:T], src[:, m, start:start + T], icnt[:, g, :], ALU.mult).then_inc(sem("win"), 1)
                    n_win += 2
                    dve.wait_ge(*when("win", n_win))
                    if g >= 2:
                        dve.wait_ge(*when("pool_in", g - 1))
                    dve.tensor_tensor(tmp[:, 2 * (g % 2):2 * (g % 2) + 2, 0:T], other[:, :, 0:T],
                                      hp[:, 2 * g:2 * g + 2, PADP:PADP + T], ALU.subtract).then_inc(sem("pool_y"), 1)
                if g >= 1:
                    for k in (2 * g - 2, 2 * g - 1):
                        dve.wait_ge(*when("pool_hi", k + 1))
                        ins_ = dve.tensor_tensor(Alo[:, k, 0:T], tmp[:, k % 4, 0:T], Ahi[:, k, 0:T], ALU.subtract)
                    ins_.then_inc(sem("pool_in"), 1)
            for j in range(8):
                if j == 7:
                    dve.wait_ge(*when("w_used", B_POOL + 1))
                else:
                    dve.wait_ge(*when("pool_done", j + 1))
                dve.scalar_tensor_tensor(out=X[:, j, 0:T], in0=ps[:, 4 + j % 4, :], scalar=v("pool_scale", j), in1=X[:, j, 0:T],
                                         op0=ALU.mult, op1=ALU.add).then_inc(sem("pool_evac"), 1)
            rms("n4", ("ffn_g", KT))
            swiglu(1, "ff1")

            dve.wait_ge(*when("ff0_ada", ADA_PAIRS))
            dve.wait_ge(*when("ff1_ada", ADA_PAIRS))
            n_mod = 0
            for use, (layer, shift, bias) in enumerate([(0, 0, None), (0, 3, ("ln1_b", 0)), (1, 0, ("ln2_b", 0)), (1, 3, ("ln1_b", KT))]):
                sh = modT[:, layer, shift * KT:(shift + 1) * KT, :]
                sc = modT[:, layer, (shift + 1) * KT:(shift + 2) * KT, :]
                dve.tensor_scalar(s1[:, use, :, :], sc, 1.0, None, ALU.add).then_inc(sem("mods"), 1)
                n_mod += 1
                if bias is None:
                    dve.tensor_copy(s2[:, use, :, :], sh).then_inc(sem("mods"), 1)
                    n_mod += 1
                    continue
                dve.wait_ge(*when("mods", n_mod))
                for src in range(2):
                    dve.tensor_tensor(s2[:, use, :, src], s1[:, use, :, src], v(bias[0], bias[1], KT), ALU.mult).then_inc(sem("mods"), 1)
                n_mod += 2
                dve.wait_ge(*when("mods", n_mod))
                dve.tensor_tensor(s2[:, use, :, :], s2[:, use, :, :], sh, ALU.add).then_inc(sem("mods"), 1)
                n_mod += 1
            dve.wait_ge(*when("mods", n_mod))
            dve.wait_ge(*when("tables", 16 * 5))
            norm_rstd("n5", 1, T)
            for k in range(KT + 1):
                if k < KT:
                    t = tmp[:, k % 4, 0:T]
                    scaled("n5", k, ("final_g", 0), t).then_inc(sem("n5_y"), 1)
                    dve.wait_ge(*when("n5_y", k + 1))
                    dve.tensor_scalar(X[:, k, 0:T], t, ALPHA, None, ALU.mult).then_inc(sem("n5_res"), 1)
                    dve.tensor_scalar(modin[:, k % 2, 0:T], t, s1[:, 0, k, 0:1], s2[:, 0, k, 0:1], ALU.mult, ALU.add).then_inc(sem("n5_m"), 1)
                    dve.tensor_scalar(modin[:, k % 2, T:TT], X[:, k, T:TT], s1[:, 0, k, 1:2], s2[:, 0, k, 1:2],
                                      ALU.mult, ALU.add).then_inc(sem("n5_m"), 1)
                    dve.tensor_scalar(X[:, k, T:TT], X[:, k, T:TT], ALPHA, None, ALU.mult).then_inc(sem("n5_res"), 1)
                if k >= 1:
                    split_lo("n5_out", "n5_hi", k - 1, modin[:, (k - 1) % 2, :], TT)

            def rotate(dst, src, scale, slot, plain_sem, rot_sem, out_sem):
                dve.scalar_tensor_tensor(out=dst, in0=src, scalar=scale, in1=cosq, op0=ALU.mult,
                                         op1=ALU.mult).then_inc(sem(plain_sem[0]), 1)
                half = swap[:, slot, :]
                dve.tensor_tensor(half, half, sinq, ALU.mult).then_inc(sem(rot_sem[0]), 1)
                dve.wait_ge(*when(plain_sem[0], plain_sem[1]))
                dve.wait_ge(*when(rot_sem[0], rot_sem[1]))
                dve.tensor_tensor(dst, dst, half, ALU.add).then_inc(sem(out_sem), 1)

            def move(dst, src):
                return dve.tensor_scalar(dst, src, 1.0, None, ALU.mult)

            for j in range(2):
                dve.wait_ge(*when("kvA_swap", j + 1))
                rotate(kd[:, j, 0:T], ps[:, 4 + 2 * j, :], 1.0, j, ("kvA_cos", j + 1), ("kvA_sin", j + 1), "kvA_evac")
            dve.wait_ge(*when("vA_done", 1))
            dve.tensor_copy(vA.rearrange("p t d -> p (t d)"), psf[:, 4 * 512:4 * 512 + TT]).then_inc(sem("vA"), 1)
            for j in range(8):
                dve.wait_ge(*when("qA_swap", j + 1))
                rotate(O[:, j, 0:T], ps[:, 2 * (j % 2), :], SCALE, j % 2, ("qA_cos", j + 1), ("qA_sin", j + 1), "qA_evac")
            dve.wait_ge(*when("vA", 1))
            dve.wait_ge(*when("kvA_evac", 3))
            dve.wait_ge(*when("qA_evac", 8))
            dve.sem_inc(sem("oA"), 1)
            with dve.Fori(0, 2) as g:
                def take_queries(e):
                    move(qcur[e], O[:, bass.ds(4 * g + 2 * e, 2), :]).then_inc(sem("qcur"), 1)

                take_queries(0)
                dve.wait_ge(*when("oA_done", N_UNITS // 4 * g + 1))
                move(kcur, kd[:, bass.ds(g, 1), :].rearrange("p a t -> p (a t)")).then_inc(sem("kvcur"), 1)
                move(vcur, vA[:, :, bass.ds(DH * g, DH)]).then_inc(sem("kvcur"), 1)

                def finish(u):
                    unit = N_UNITS * g + u
                    c = sm[:, u % 4, :]
                    dve.wait_ge(*when("esA", unit + 1))
                    dve.wait_ge(*when("sA_free", unit + 3))
                    dve.tensor_tensor(c[:, 4:5], c[:, 2:3], c[:, 3:4], ALU.add).then_inc(sem("denA"), 1)
                    dve.wait_ge(*when("denA", 2 * unit + 1))
                    dve.reciprocal(c[:, 5:6], c[:, 4:5]).then_inc(sem("denA"), 1)
                    dve.wait_ge(*when("denA", 2 * unit + 2))
                    prob = probA[u % 3][:, 0:len(keys(UNITS[u][1])) * P]
                    dve.tensor_scalar(prob, prob, c[:, 5:6], None, ALU.mult).then_inc(sem("pA"), 1)

                def take_values(u):
                    e, n, _ = UNITS[u]
                    dve.wait_ge(*when("oA_done", N_UNITS // 4 * g + u // 4 + 2))
                    four = ps[0:DH, 6, :].rearrange("p (t h q) -> p h t q", t=2, h=2)
                    for h in range(2):
                        mm = move(O[DH * h:DH * h + DH, bass.ds(4 * g + 2 * e, 2), n * P:(n + 1) * P], four[:, h])
                    mm.then_inc(sem("oA"), 1)

                for u in range(N_UNITS + 4):
                    if u < N_UNITS:
                        e, n, h = UNITS[u]
                        unit = N_UNITS * g + u
                        W = len(keys(n)) * P
                        a = 2 * (u % 2) * 512 + 512 + C - W
                        c = sm[:, u % 4, :]
                        sink = vec[:, bass.ds(8 * g + (_cols["sink"][0] + 4 * e + h), 1)]
                        dve.wait_ge(*when("sA", unit + 1))
                        dve.tensor_reduce(c[:, 0:1], psf[:, a:a + W], AX_X, ALU.max).then_inc(sem("mxA"), 1)
                        dve.wait_ge(*when("mxA", unit + 1))
                        dve.tensor_scalar(c[:, 1:2], c[:, 0:1], sink, -1.0, ALU.max, ALU.mult).then_inc(sem("nmA"), 1)
                    if u == 4:
                        take_queries(1)
                    if 1 <= u < N_UNITS + 1:
                        finish(u - 1)
                    if u >= 4 and UNITS[u - 4][2] == 3:
                        take_values(u - 4)
            for k in range(KT):
                split_lo("OA_split", "OA_hi", k, O[:, k, :], TT)
            for j in range(8):
                if j % 2:
                    dve.wait_ge(*when("w_used", B_WOA + j // 2 + 1))
                else:
                    dve.wait_ge(*when("woA_done", j // 2 + 1))
                for c, (c0, n) in enumerate(X_CTX):
                    mm = dve.scalar_tensor_tensor(out=X[:, j, c0:c0 + n], in0=ps[:, 2 * (j % 2) + c, 0:n],
                                                  scalar=mod(0, 2, j, c), in1=X[:, j, c0:c0 + n], op0=ALU.mult, op1=ALU.add)
                mm.then_inc(sem("woA_evac"), 1)
            layernorm("l1", X_CTX, 4, ("ln1_g", 0), ("ln1_b", 0), 1)

            def mlp(l, name, cols):
                B0 = B_ML[l]
                width = sum(n for _, n in cols)
                dve.sem_inc(sem(f"{name}_dfree"), 8)

                def hidden(i, j, first=False):
                    dve.wait_ge(*when(f"{name}_relu", 2 * i + j + 1))
                    if not first:
                        dve.wait_ge(*when(f"{name}_h", 2 * i + j - 1))
                    r = tmp[:, 2 + j, 0:width]
                    dve.tensor_tensor(tmp[:, j, 0:width], r, r, ALU.mult).then_inc(sem(f"{name}_mul"), 1)

                def hidden_lo(i, slot, j):
                    dve.wait_ge(*when(f"{name}_hi", 2 * i + j + 1))
                    dve.tensor_tensor(hlo[:, slot, j, 0:width], tmp[:, j, 0:width], hhi[:, slot, j, 0:width],
                                      ALU.subtract).then_inc(sem(f"{name}_h"), 1)

                def add_down(i, b_d, m):
                    if m == KT - 1:
                        dve.wait_ge(*when("w_used", b_d + 1))
                    else:
                        dve.wait_ge(*when(f"{name}_down", 7 * i + m + 1))
                    dve.wait_ge(*when(f"{name}_dfree", 8 * i + m + 1))
                    for c, (c0, n) in enumerate(cols):
                        mm = dve.scalar_tensor_tensor(out=X[:, m, c0:c0 + n], in0=ps[:, 4 + 2 * (m % 2) + c, 0:n],
                                                      scalar=mod(l, 5, m, c), in1=X[:, m, c0:c0 + n],
                                                      op0=ALU.mult, op1=ALU.add)
                    mm.then_inc(sem(f"{name}_dfree"), 1)

                dve.wait_ge(*when("l1_res" if l == 0 else "l3_res", KT))
                for j in range(2):
                    hidden(0, j, True)
                for j in range(2):
                    hidden_lo(0, 0, j)
                with dve.Fori(0, (ML_IT - 1) // 3) as p:
                    for s in range(3):
                        i = 3 * p + s
                        for j in range(2):
                            hidden(i + 1, j)
                        for m in range(KT):
                            add_down(i, 6 * p + (B0 + 2 + 2 * s), m)
                            if m < 2:
                                hidden_lo(i + 1, (s + 1) % 3, m)
                for m in range(KT):
                    add_down(ML_IT - 1, B0 + ML_BLOCKS - 1, m)

            mlp(0, "ml0", X_CTX)
            layernorm("l2", X_CTX, 0, ("ln2_g", 0), ("ln2_b", 0), 2)

            dve.sem_inc(sem("qkB_free0"), 1)
            dve.sem_inc(sem("qkB_free1"), 1)
            dve.sem_inc(sem("qkB"), 2)
            dve.sem_inc(sem("oB"), 1)
            with dve.Fori(0, 4) as st:
                for r, (dst, bank, scale, free) in enumerate([(qB[:, 0, :], 6, SCALE, 2), (qB[:, 1, :], 7, SCALE, 2),
                                                             (kB[:, 0, 0:T], 6, 1.0, 3), (kB[:, 1, 0:T], 6, 1.0, 4)]):
                    dve.wait_ge(*when("swB", 4 * st + r + 1))
                    rotate(dst, ps[:, bank, :], scale, r % 2, (f"qkB_free{bank - 6}", 3 * st + free), ("sinB", 4 * st + r + 1), "qkB")

                def finish(u):
                    unit = 8 * st + u
                    c = sm[:, u % 4, :]
                    p0, p1 = probB[u % 3]
                    dve.wait_ge(*when("sB_free", 2 * unit + 4))
                    dve.reciprocal(c[:, 4:6], c[:, 2:4]).then_inc(sem("denB"), 1)
                    dve.wait_ge(*when("denB", 3 * unit + 1))
                    dve.tensor_tensor(c[:, 6:7], c[:, 5:6], lamt[:, 5:6], ALU.mult).then_inc(sem("denB"), 1)
                    dve.tensor_scalar(p0, p0, c[:, 4:5], None, ALU.mult).then_inc(sem("denB"), 1)
                    dve.wait_ge(*when("denB", 3 * unit + 3))
                    dve.scalar_tensor_tensor(out=p0, in0=p1, scalar=c[:, 6:7], in1=p0, op0=ALU.mult,
                                             op1=ALU.add).then_inc(sem("pB"), 1)

                def take_values(hh):
                    head = 2 * st + hh
                    dve.wait_ge(*when("oB_done", head + 2))
                    move(O[:, bass.ds(head, 1), 0:T].rearrange("p a t -> p (a t)"), ps[:, 6, :]).then_inc(sem("oB"), 1)

                for u in range(9):
                    if u < 8:
                        for t in range(2):
                            a = 2 * t * 512 + P
                            dve.wait_ge(*when("sB", 16 * st + 2 * u + t + 1))
                            dve.tensor_reduce(sm[:, u % 4, t:t + 1], psf[:, a:a + TT], AX_X, ALU.max,
                                              negate=True).then_inc(sem("nmB"), 1)
                    if u >= 1:
                        finish(u - 1)
                    if u == 7:
                        take_values(0)
                take_values(1)
            for i in range(12):
                if i < 8:
                    if i == 0:
                        dve.wait_ge(*when("oB", 9))
                    if i >= 4:
                        dve.wait_ge(*when("oB_ms", i - 3))
                    dve.tensor_scalar(tmp[:, i % 4, 0:T], O[:, i, 0:T], SUB_SCALE, SUB_CLAMP, ALU.mult, ALU.min).then_inc(sem("oB_t"), 1)
                    dve.wait_ge(*when("oB_t", 2 * i + 1))
                    dve.tensor_scalar(tmp[:, i % 4, 0:T], tmp[:, i % 4, 0:T], -SUB_CLAMP, None, ALU.max).then_inc(sem("oB_t"), 1)
                if 0 <= i - 2 < 8:
                    h = i - 2
                    dve.wait_ge(*when("oB_ms", h + 1))
                    dve.tensor_scalar(aT[:, 2 + h % 2, :], ps[:, h % 4, :], SUB_OVER, None, ALU.is_lt).then_inc(sem("oB_flag"), 1)
                if 0 <= i - 3 < 8:
                    h = i - 3
                    dve.wait_ge(*when("oB_std", h + 1))
                    dve.reciprocal(aT[:, 4 + h % 2, :], aT[:, h % 2, :]).then_inc(sem("oB_r"), 1)
                    dve.wait_ge(*when("oB_r", 3 * h + 1))
                    dve.wait_ge(*when("oB_flag", h + 1))
                    dve.tensor_tensor(aT[:, 4 + h % 2, :], aT[:, 4 + h % 2, :], aT[:, 2 + h % 2, :], ALU.mult).then_inc(sem("oB_r"), 1)
                    dve.wait_ge(*when("oB_r", 3 * h + 2))
                    dve.scalar_tensor_tensor(out=O[:, h, 0:T], in0=O[:, h, 0:T], scalar=lamt[:, 6:7], in1=aT[:, 4 + h % 2, :],
                                             op0=ALU.mult, op1=ALU.mult).then_inc(sem("oB_r"), 1)
                if i >= 4:
                    split_lo("OB_split", "OB_hi", i - 4, O[:, i - 4, 0:T], T)
            for j in range(8):
                if j % 2:
                    dve.wait_ge(*when("w_used", B_WOB + j // 2 + 1))
                else:
                    dve.wait_ge(*when("woB_done", j // 2 + 1))
                dve.scalar_tensor_tensor(out=X[:, j, 0:T], in0=ps[:, j % 4, :], scalar=mod(1, 2, j, 0), in1=X[:, j, 0:T],
                                         op0=ALU.mult, op1=ALU.add).then_inc(sem("woB_evac"), 1)
            layernorm("l3", X_ONLY, 4, ("ln1_g", KT), ("ln1_b", KT), 3)
            mlp(1, "ml1", X_ONLY)
            layernorm("l4", X_ONLY, 0, ("ln2_g", KT), ("ln2_b", KT), None)


def constants():
    f = np.float32
    out = {"ident": np.eye(P, dtype=f), "sel4": np.array([[1, 0], [0, 1], [1, 0], [0, 1]], f)}
    n = np.arange(P)
    ang = 2 * np.pi * (np.outer(n, n) % P) / P
    out["csd"] = (np.concatenate([np.cos(ang), np.sin(ang)], 1) / math.sqrt(T * P)).astype(f)
    n = np.arange(T)
    ang = 2 * np.pi * (np.outer(n, n) % T) / T
    both = np.stack([np.cos(ang), -np.sin(ang)])
    out["dft"] = both.reshape(2, QT, P, T).transpose(2, 0, 1, 3).reshape(P, -1).astype(f)
    pos = np.arange(T)
    cnt = [np.clip(pos - w // 2 + w, 0, T) - np.clip(pos - w // 2, 0, T) for w in (2, 4, 8, 16)]
    out["icnt"] = np.broadcast_to((1.0 / np.array(cnt)).astype(f).reshape(1, -1), (P, 4 * T))
    freqs = DH // 4
    inv = f(10000.0) ** (-np.arange(freqs, dtype=f) / f(freqs))
    row = np.repeat(np.arange(T // 64, dtype=f), 64)
    col = np.tile(np.arange(64, dtype=f), T // 64)
    ang = np.concatenate([row[:, None] * inv, col[:, None] * inv], 1).astype(f).T
    out["cosq"] = np.tile(np.cos(ang), (4, 1)).astype(f)
    out["sinq"] = np.tile(np.concatenate([-np.sin(ang), np.sin(ang)]), (2, 1)).astype(f)
    q, k = np.arange(P)[:, None], np.arange(P)[None, :]
    out["masks"] = np.concatenate([np.where(k >= q, 0, NEG), np.where(k <= q, 0, NEG)], 1).astype(f)
    return out


def by_inputs(w):
    return [w[:, m:m + 256].reshape(KT, P, 256).transpose(1, 0, 2).reshape(P, BLK) for m in range(0, w.shape[1], 256)]


def by_hidden(w):
    return [w[m:m + 256].reshape(2, P, D).transpose(1, 0, 2).reshape(P, BLK) for m in range(0, w.shape[0], 256)]


def stream(a):
    blocks = []
    win = by_inputs(a["w_in_ab"][0])
    blocks += [win[2], win[4], win[3], win[5], win[0], win[1]]
    blocks += by_inputs(a["w_out_ab"][0])
    for f in range(2):
        ada = by_inputs(a["w_ada_2"][f])
        gate, up, down = by_inputs(a["ffn_w_gate"][f]), by_inputs(a["ffn_w_up"][f]), by_hidden(a["ffn_w_down"][f])
        blocks += [ada[0], gate[0], ada[1], up[0]]
        for i in range(FF_IT - 1):
            blocks += [ada[2 * i + 2], gate[i + 1], ada[2 * i + 3], up[i + 1], down[i]]
        blocks += ada[2 * FF_IT:2 * FF_IT + 2] + [down[FF_IT - 1]]
        if f == 0:
            blocks.append(a["pool_map"][0].reshape(4, 2, P, 256).transpose(2, 1, 0, 3).reshape(P, BLK))
    wk, wv = a["a_wk_2"][0], a["a_wv_2"][0]
    blocks += by_inputs(np.concatenate([wk[:, 0:DH], wk[:, 0:DH], wk[:, DH:], wk[:, DH:]], 1))
    blocks += by_inputs(np.concatenate([wv, np.zeros_like(wv)], 1))
    blocks += by_inputs(a["a_wq_2"][0]) + by_inputs(a["a_wo_2"][0])
    for l in range(2):
        w1, w2 = by_inputs(a["mlp_w1_2"][l]), by_hidden(a["mlp_w2_2"][l])
        blocks += [w1[0]]
        for i in range(ML_IT - 1):
            blocks += [w1[i + 1], w2[i]]
        blocks += [w2[ML_IT - 1]]
        if l == 0:
            for q, k, w in zip(by_inputs(a["b_wq_2"][0]), by_inputs(a["b_wk_2"][0]), by_inputs(a["b_wv_2"][0])):
                blocks += [q, k, w]
            blocks += by_inputs(a["b_wo_2"][0])
    assert len(blocks) == N_BLOCKS
    return np.stack(blocks)


def features(x):
    x = np.asarray(x)
    return np.ascontiguousarray(np.moveaxis(x.reshape(*x.shape[:-1], -1, P), -1, 0)).reshape(P, -1)


def vectors(a):
    every = lambda x: np.broadcast_to(np.asarray(x).reshape(1, -1), (P, np.asarray(x).size))
    parts = {
        "mix_g": features(a["norm_mix_g"]), "ffn_g": features(a["norm_ffn_g"]),
        "conv_w": features(a["conv_w"][0]).reshape(P, TAPS, 4).transpose(0, 2, 1).reshape(P, -1),
        "conv_b": features(a["conv_b"][0]), "conv_ln_g": features(a["conv_ln_g"][0]),
        "conv_ln_b": features(a["conv_ln_b"][0]), "pool_scale": features(a["pool_scale"][0]),
        "final_g": features(a["final_g"]), "b_ada": np.repeat(features(a["b_ada_2"]), 2, axis=1),
        "ln1_g": features(a["ln1_g_2"]), "ln1_b": features(a["ln1_b_2"]), "ln2_g": features(a["ln2_g_2"]),
        "ln2_b": features(a["ln2_b_2"]), "sink": every(a["a_sink_2"][0]), "subln_g": np.asarray(a["b_subln_g_2"][0])[:, None],
        "lq1": every(a["b_lq1_2"]), "lk1": every(a["b_lk1_2"]), "lq2": every(a["b_lq2_2"]), "lk2": every(a["b_lk2_2"]),
        "c": np.stack([features(a["c_2"][0]), features(a["c_ctx_2"])], 2).reshape(P, -1),
    }
    return np.ascontiguousarray(np.concatenate([parts[n] for n in _cols], 1))


def kernel(**inputs):
    import concourse.bacc as bacc
    from concourse.bass_utils import run_bass_kernel_spmd

    a = {n: np.asarray(x) for n, x in inputs.items()}
    arrays = {n: np.ascontiguousarray(x) for n, x in constants().items()}
    arrays["stream"] = stream(a)
    arrays["vec"] = vectors(a)
    arrays["xT"] = np.ascontiguousarray(a["x"][0].reshape(T, KT, P).transpose(2, 1, 0))
    arrays["ctxT"] = np.ascontiguousarray(a["ctx_2"][0].reshape(C, KT, P).transpose(2, 1, 0))
    arrays["fmap"] = np.ascontiguousarray(a["fnet_map"][0].transpose(1, 0, 2).reshape(P, HEADS_A * P))
    nc = bacc.Bacc("TRN2", target_bir_lowering=False, num_devices=1)
    ins = {n: nc.dram_tensor(f"in_{n}", x.shape, F32, kind="ExternalInput").ap() for n, x in arrays.items()}
    out = nc.dram_tensor("out_xT", (P, KT, T), F32, kind="ExternalOutput").ap()
    build(nc, ins, out)
    got = run_bass_kernel_spmd(nc, [{f"in_{n}": x for n, x in arrays.items()}], core_ids=[0]).results[0]["out_xT"]
    return np.ascontiguousarray(got.transpose(2, 1, 0)).reshape(1, T, D)
```

```python
import math
from contextlib import ExitStack

import numpy as np

import concourse.bass as bass
import concourse.mybir as mybir

F32 = mybir.dt.float32
F32R = mybir.dt.float32r
BF16 = mybir.dt.bfloat16
ALU = mybir.AluOpType
ACT = mybir.ActivationFunctionType
AX_X = mybir.AxisListType.X

P = 128
D = 1024
KT = D // P
T = 512
C = 256
TT = T + C
BLK = 2048
HALF = BLK // 2
RING = 3
QT = T // P
NTT = TT // P
DH = 64
HEADS_A = 4
TAPS = 31
PADC = TAPS // 2
UP = T + 2 * PADC
PADP = 8
HPAD = T + 2 * PADP
D_FF = 2816
FF_IT = D_FF // 256
D_FF2 = 4096
ML_IT = D_FF2 // 256
N_MOD = 6
ADA_PAIRS = N_MOD * D // 512
RMS_EPS = 1e-6
LN_EPS = 1e-5
N_SMALL = 3
ALPHA = 4.0 ** 0.25
LAM_INIT = 0.8 - 0.6 * math.exp(-0.3)
SCALE = DH ** -0.5
NEG = -1e30
SUB_SCALE = 2.0 ** -40
SUB_CLAMP = 2.0 ** 30
SUB_OVER = 2.0 ** 48

Q_TILES = [*range(QT, NTT), *range(QT)]
UNITS = [(e, n, h) for e in range(2) for n in Q_TILES for h in range(4)]
N_UNITS = len(UNITS)
LEAD = 3
TAKE_AT = (15, 17, 19, 21)
V_FIRST = 2
TURNED_B = [[], [], [0], [1], [2], [3], [], [4], [5], [6, 7]]

X_ONLY = [(0, T)]
X_CTX = [(0, T), (T, C)]
PASSES = {"l1": [(0, 1)], "l2": [(0,), (1,)], "l3": [(0,)], "n5": [(0, 1)]}

B_WIN = 0
B_WOUT = B_WIN + 6
FF_BLOCKS = 5 * FF_IT + 2
B_FF = [B_WOUT + 4, B_WOUT + 4 + FF_BLOCKS + 1]
B_POOL = B_FF[0] + FF_BLOCKS
B_KV = B_FF[1] + FF_BLOCKS
B_WQA = B_KV + 2
B_WOA = B_WQA + 4
ML_BLOCKS = 2 * ML_IT
B_ML0 = B_WOA + 4
B_QKV = B_ML0 + ML_BLOCKS
B_WOB = B_QKV + 12
B_ML1 = B_WOB + 4
N_BLOCKS = B_ML1 + ML_BLOCKS
B_ML = [B_ML0, B_ML1]

_cols = {}
_n = 0
for _name, _w in [
    ("mix_g", 2 * KT), ("ffn_g", 2 * KT), ("conv_w", 4 * TAPS), ("conv_b", 4), ("conv_ln_g", 4), ("conv_ln_b", 4),
    ("pool_scale", KT), ("final_g", KT), ("b_ada", 2 * 48 * 2), ("ln1_g", 2 * KT), ("ln1_b", 2 * KT),
    ("ln2_g", 2 * KT), ("ln2_b", 2 * KT), ("sink", 16), ("subln_g", 1), ("lq1", 64), ("lk1", 64), ("lq2", 64),
    ("lk2", 64), ("c", KT * 2),
]:
    _cols[_name] = (_n, _n + _w)
    _n += _w
N_VEC = _n


def build(nc, ins, out):
    ctx = ExitStack()
    with ctx:
        def sb(name, shape, dt=F32):
            return ctx.enter_context(nc.sbuf_tensor(name, shape, dt))

        shared = {}

        def share(signal, phases):
            before = 0
            for phase, n in phases.items():
                shared[f"{phase}_{signal}"] = (signal, before)
                before += n

        with_ctx = ["l1", "l2"]
        norms = ["n1", "n2", "n3", "n4", "n5", "l1", "l2", "l3", "l4"]
        tiles = {n: KT for n in norms}
        share("sq", tiles)
        share("sum", tiles)
        share("std", {n: 2 if n in with_ctx else 1 for n in norms})
        share("rstd", {n: 1 for n in norms})
        share("y", {n: KT for n in norms if n not in ("n3", "n5")})
        for signal in ("hi", "out"):
            share(signal, {n: 2 * KT if n == "l2" else KT for n in norms if n not in ("n3", "l4")})
        share("m", {"n5": 2 * KT, "l1": 2 * KT, "l2": 2 * KT, "l3": KT})
        share("mu", {n: 1 for n in norms[5:]})
        share("d", {"l1": 2 * KT, "l2": 2 * KT, "l3": KT, "l4": KT})
        share("res", {"n5": KT, "l1": KT, "l2": KT, "l3": KT, "l4": KT})
        for kind, steps in (("ff", FF_IT), ("ml", ML_IT)):
            pair = (kind + "0", kind + "1")
            for signal in ("silu" if kind == "ff" else "relu", "mul", "hi", "h"):
                for n, phase in enumerate(pair):
                    shared[f"{phase}_{signal}"] = (f"{kind}_{signal}", 2 * steps * n)
            for n, phase in enumerate(pair):
                shared[f"{phase}_up"] = (f"{kind}_up", (2 if kind == "ff" else 1) * steps * n)
                shared[f"{phase}_down"] = (f"{kind}_down", (KT - 2) * steps * n)
                shared[f"{phase}_dfree"] = (f"{kind}_dfree", (KT * steps + 8) * n)
        for n in range(2):
            shared[f"ff{n}_ada"] = ("ada", ADA_PAIRS * n)
            shared[f"ff{n}_sel"] = ("ada_sel", ADA_PAIRS * n)
            shared[f"ff{n}_arow"] = ("ada_row", 2 * ADA_PAIRS * n)
        sems = {}

        def sem(name):
            name = shared.get(name, (name, 0))[0]
            if name not in sems:
                sems[name] = ctx.enter_context(nc.semaphore(name))
            return sems[name]

        def when(name, count):
            return sem(name), count + shared.get(name, (name, 0))[1]

        def block_used(b):
            return when("w_used", 2 * b + 2)

        X = sb("X", [P, KT, TT])
        Ahi = sb("Ahi", [P, KT, TT], F32R)
        Ahi_at = nc.sbuf_base - 4 * KT * TT
        Alo = sb("Alo", [P, KT, TT], F32R)
        whi = sb("whi", [P, RING, BLK], F32R)
        raw = sb("raw", [P, RING, BLK])
        wlo = nc.alloc_sbuf_tensor_at("wlo", [P, RING, BLK], F32R, offset=nc.sbuf_base - 4 * RING * BLK)
        tmp = sb("tmp", [P, 4, TT])
        std = sb("std", [P, TT])
        std_r = nc.alloc_sbuf_tensor_at("std_r", [P, TT], F32R, offset=nc.sbuf_base - 4 * TT)
        rstd = sb("rstd", [P, TT])
        rstd_r = nc.alloc_sbuf_tensor_at("rstd_r", [P, TT], F32R, offset=nc.sbuf_base - 4 * TT)
        vec = sb("vec", [P, N_VEC])
        ident = sb("ident", [P, P])
        ones = sb("ones", [P, P])
        epsr = sb("epsr", [P, 3])
        modT = sb("modT", [P, 2, N_MOD * KT, 2])
        s1 = sb("s1", [P, 4, KT, 2])
        s2 = sb("s2", [P, 4, KT, 2])
        rg = sb("rg", [P, 4, KT])
        rb = sb("rb", [P, 4, KT])
        csil = sb("csil", [P, KT, 2])
        sel4 = sb("sel4", [4, 2])
        lamt = sb("lamt", [P, 8])
        sm = sb("sm", [P, 8, 8])
        hnorm = sb("hnorm", [P, 2, 8 * QT])
        maskb = sb("maskb", [P, 3, P], BF16)
        ARENA = 16128
        arena = sb("arena", [P, ARENA])
        arena_at = nc.sbuf_base - 4 * ARENA

        def carve(at, *shape):
            n = int(np.prod(shape))
            assert at + n <= ARENA, (at, shape)
            a = arena[:, at:at + n]
            if len(shape) == 2:
                a = a.rearrange("p (a b) -> p a b", a=shape[0])
            if len(shape) == 3:
                a = a.rearrange("p (a b c) -> p a b c", a=shape[0], b=shape[1])
            return a, at + n

        hhi = nc.alloc_sbuf_tensor_at("hhi", [P, 3, 2, TT], F32R, offset=arena_at)
        hlo = nc.alloc_sbuf_tensor_at("hlo", [P, 3, 2, TT], F32R, offset=arena_at + 4 * 6 * TT)
        H_END = 12 * TT
        c4 = nc.alloc_sbuf_tensor_at("c4", [P, KT, P], F32R, offset=arena_at + 4 * (ARENA - KT * P))
        halves, HALVES_END = carve(H_END, 2, TT)
        dft, at = carve(0, 2, QT, T)
        upad, at = carve(at, 4, UP)
        conv, at = carve(at, 4, T)
        pf, at = carve(at, 4, T)
        zz, at = carve(at, 2, QT * 256)
        csd, at = carve(at, 256)
        fmap, at = carve(at, 4 * P)
        csm, at = carve(at, 4, 256)
        assert at <= ARENA - KT * P
        hp, at = carve(0, KT, HPAD)
        pa, at = carve(at, 2, HPAD)
        pb, at = carve(at, 2, HPAD)
        assert at <= H_END
        icnt, at = carve(HALVES_END, 4, T)
        arow, at = carve(at, 2, 256)
        arow = arow[0:4]
        assert at <= ARENA - KT * P
        O, O_END = carve(0, KT, TT)
        cosq, at = carve(HALVES_END, T)
        sinq, at = carve(at, T)
        masks, base = carve(at, 2, P)
        swapA = halves[:, :, 0:T]
        vT = tmp[:, 1, :]
        kh, kl = std_r, rstd_r
        probA = [tmp[:, i, 0:641] for i in (2, 3, 0, 1)]
        ptA0, at = carve(O_END, 5, T)
        vcur, at = carve(at, NTT, DH)
        assert at <= H_END
        kd, at = carve(base, 2, TT)
        vA, at = carve(at, NTT, P)
        q01 = nc.alloc_sbuf_tensor_at("q01", [P, 2, TT], F32R, offset=arena_at + 4 * H_END)
        q23 = nc.alloc_sbuf_tensor_at("q23", [P, 2, TT], F32R, offset=arena_at + 4 * at)
        assert at + 2 * TT <= ARENA
        ptA1 = nc.alloc_sbuf_tensor_at("ptA1", [P, 5, T], F32, offset=Ahi_at)
        ptA = [ptA0, ptA1]
        qs = [q23[:, 0, :], q23[:, 1, :], q01[:, 0, :], q01[:, 1, :], *(Ahi[:, 4 + h, :] for h in range(4))]
        rot = tmp[:, 0:2, :]
        swapB = tmp[:, 2:4, 0:T]
        probB = [tmp[:, 0, :], tmp[:, 2, :], std[:, :]]
        probB2 = [tmp[:, 1, :], tmp[:, 3, :]]
        aT, at = carve(O_END, NTT, T)
        assert at <= H_END
        vB, at = carve(H_END, NTT, 256)
        assert at == HALVES_END
        q0 = nc.alloc_sbuf_tensor_at("q0", [P, KT, TT], F32R, offset=arena_at)
        at = base - 2 * P
        k012 = nc.alloc_sbuf_tensor_at("k012", [P, 3, TT], F32R, offset=arena_at + 4 * at)
        q1 = nc.alloc_sbuf_tensor_at("q1", [P, KT, 256], F32R, offset=arena_at + 4 * (at + 3 * TT))
        assert at + 3 * TT + KT * 256 <= ARENA
        qB = (q0[:, :, T:TT], q1[:, :, :])
        kB = [[k012[:, 0, :], k012[:, 1, :]], [k012[:, 2, :], rstd_r[:, :]]]
        ps = ctx.enter_context(nc.psum_tensor("ps", [P, 8, 512], F32))
        psf = ps[:, :, :].rearrange("p b n -> p (b n)")

        def turn_at(u):
            return 4 * 512 if u < 7 else 0

        def window(n):
            return (max(0, n - 1), min(QT, n + 2)) if n < QT else (0, 0)

        def keys(n):
            return [*range(*window(n)), *range(QT, NTT)]

        def v(name, i, n=1):
            a = _cols[name][0] + i
            return vec[:, a:a + n]

        def mod(layer, which, k, src):
            return modT[:, layer, which * KT + k, src:src + 1]

        block = ctx.enter_context(nc.Block())

        @block.sync
        def _(sp):
            def load_small(name, dst):
                sp.dma_start(dst, ins[name]).then_inc(sem("small"), 16)

            def load(b, slot, half):
                sp.dma_start(raw[:, slot, half * HALF:(half + 1) * HALF],
                             ins["stream"][b, :, half * HALF:(half + 1) * HALF]).then_inc(sem(f"raw{slot}{half}"), 16)

            for h in range(2):
                sp.dma_start(X[:, 4 * h:4 * h + 4, 0:T], ins["xT"][:, 4 * h:4 * h + 4, :]).then_inc(sem(f"x{h}"), 16)
            sp.dma_start(vec[:, :], ins["vec"]).then_inc(sem("vec"), 16)
            for b in range(RING):
                for half in range(2):
                    load(b, b, half)
            load_small("sel4", sel4[:, :])
            load_small("csd", csd)
            load_small("fmap", fmap)
            sp.dma_start(dft.rearrange("p a b c -> p (a b c)"), ins["dft"]).then_inc(sem("dft"), 16)
            sp.dma_start(ident[:, :], ins["ident"]).then_inc(sem("tables"), 16)
            sp.dma_start(X[:, :, T:TT], ins["ctxT"]).then_inc(sem("tables"), 16)
            with sp.Fori(1, N_BLOCKS // RING) as i:
                for s in range(RING):
                    for half in range(2):
                        sp.wait_ge(*when("w_used", 2 * RING * i + (2 * (s - RING) + half + 1)))
                        load(RING * i + s, s, half)
            for b in range(N_BLOCKS // RING * RING, N_BLOCKS):
                for half in range(2):
                    sp.wait_ge(*when("w_used", 2 * (b - RING) + half + 1))
                    load(b, b % RING, half)

            for h in range(2):
                sp.wait_ge(*when("l4_res", 4 * h + 4))
                sp.dma_start(out[:, 4 * h:4 * h + 4, :], X[:, 4 * h:4 * h + 4, 0:T]).then_inc(sem("stored"), 16)
            sp.wait_ge(*when("stored", 32))

        @block.gpsimd
        def _(pool):
            def split(s, half, loaded, nth):
                part = slice(half * HALF, (half + 1) * HALF)
                pool.wait_ge(*when(f"raw{s}{half}", loaded))
                pool.sem_inc(sem("w_turn"), 1)
                pool.tensor_scalar(whi[:, s, part], raw[:, s, part], 1.0, 1.0, ALU.mult, ALU.mult).then_inc(sem("w_hi"), 1)
                pool.wait_ge(*when("w_hi", nth))
                pool.tensor_tensor(wlo[:, s, part], raw[:, s, part], whi[:, s, part], ALU.subtract).then_inc(sem("w_split"), 1)

            def split_rings(first, end):
                with pool.Fori(first, end) as i:
                    for s in range(RING):
                        for half in range(2):
                            split(s, half, 16 * i + 16, 2 * RING * i + (2 * s + half + 1))

            split_rings(0, -(-B_POOL // RING))
            pool.wait_ge(*when("w_split", 2 * RING * -(-B_POOL // RING)))
            for k in range(6):
                pool.wait_ge(*when("pool_hi", k + 1))
                pool.tensor_tensor(Alo[:, k, 0:T], tmp[:, k % 4, 0:T], Ahi[:, k, 0:T], ALU.subtract).then_inc(sem("pool_lo"), 1)
            split_rings(-(-B_POOL // RING), -(-B_WOA // RING))
            with pool.Fori(0, 2) as g:
                for u in range(N_UNITS):
                    e, n, h = UNITS[u]
                    pool.wait_ge(*when("denA", N_UNITS * g + u + 1))
                    pool.sem_inc(sem("pool_turn"), 1)
                    prob = probA[u % 4][:, 0:len(keys(n)) * P]
                    pool.tensor_scalar(prob, prob, sm[:, u % 8, 2:3], 1.0, ALU.mult, ALU.mult).then_inc(sem("pA"), 1)

            def norm_residual(name, use, cols):
                width = sum(n for _, n in cols)
                pool.wait_ge(*when(f"{name}_m", len(cols) * KT))
                for i in range(KT + 1):
                    if i < KT:
                        pool.tensor_tensor(X[:, i, 0:width], X[:, i, 0:width], rstd[:, 0:width], ALU.mult).then_inc(sem(f"{name}_y"), 1)
                    if i >= 1:
                        pool.wait_ge(*when(f"{name}_y", i))
                        pool.tensor_scalar(X[:, i - 1, 0:width], X[:, i - 1, 0:width], rg[:, use, i - 1:i], rb[:, use, i - 1:i], ALU.mult,
                                           ALU.add).then_inc(sem(f"{name}_res"), 1)

            split_rings(-(-B_WOA // RING), -(-(B_ML0 + 2) // RING))
            norm_residual("l1", 1, X_CTX)
            split_rings(-(-(B_ML0 + 2) // RING), -(-(B_QKV + 2) // RING))
            norm_residual("l2", 2, X_CTX)
            split_rings(-(-(B_QKV + 2) // RING), -(-(B_ML1 + 2) // RING))
            norm_residual("l3", 3, X_ONLY)
            split_rings(-(-(B_ML1 + 2) // RING), N_BLOCKS // RING)
            for b in range(N_BLOCKS // RING * RING, N_BLOCKS):
                for half in range(2):
                    split(b % RING, half, 16 * (b // RING) + 16, 2 * b + half + 1)

        @block.tensor
        def _(pe):
            def product(dst, cols, b, off, rhs, k, kn):
                mm = None
                for w, part in ((whi, 0), (whi, 1), (wlo, 0)):
                    for c, (c0, n) in enumerate(cols):
                        mm = pe.matmul(dst[c], w[:, b % RING, off:off + P], rhs(k, part, c0, n),
                                       start=(k == 0 and w is whi and part == 0), stop=(k == kn - 1 and w is wlo))
                return mm

            def a_rhs(k, part, c0, n):
                return (Ahi, Alo)[part][:, k, c0:c0 + n]

            def h_rhs(slot):
                return lambda k, part, c0, n: (hhi, hlo)[part][:, slot, k, c0:c0 + n]

            def columns(name, blocks, cols, dsts, ready=None):
                for k in range(KT):
                    if ready:
                        pe.wait_ge(*when(ready, k + 1))
                    for n, (b, at) in enumerate(blocks):
                        if k % 4 == 0:
                            pe.wait_ge(*when("w_split", 2 * b + (k // 4 + 1)))
                        for j in range(2):
                            mm = product(dsts[2 * n + j], cols, at, k * 256 + j * P, a_rhs, k, KT)
                            if j == 0 and k == KT - 1:
                                mm.then_inc(sem(name), 1)
                            if j == 1 and k == 3 and n == 0:
                                mm.then_inc(sem("w_used"), 1)
                            if j == 1 and k == KT - 1:
                                mm.then_inc(sem("w_used"), 2 if n else 1)

            def column_sums(name, bank, cols, src, src_ready):
                for k in range(KT):
                    pe.wait_ge(*when(src_ready, k + 1))
                    for c, (c0, n) in enumerate(cols):
                        mm = pe.matmul(ps[:, bank + c, 0:n], ones[:, :], src(k)[:, c0:c0 + n],
                                       start=(k == 0), stop=(k == KT - 1))
                    mm.then_inc(sem(name), 1)

            def squares(k):
                return tmp[:, k % 4, :]

            def rms(name, bank=0):
                column_sums(f"{name}_sum", bank, X_ONLY, squares, f"{name}_sq")

            def layernorm(name, cols, x_ready, x_before, bank=0):
                for k in range(KT):
                    pe.wait_ge(*when(x_ready, x_before + k + 1))
                    for c, (c0, n) in enumerate(cols):
                        mm = pe.matmul(ps[:, bank + c, 0:n], ones[:, :], X[:, k, c0:c0 + n],
                                       start=(k == 0), stop=(k == KT - 1))
                mm.then_inc(sem(f"{name}_mu"), 1)
                column_sums(f"{name}_sum", bank + 2, cols, squares, f"{name}_sq")

            def done(mm, name, ends_block):
                mm.then_inc(sem("w_used" if ends_block else name), 2 if ends_block else 1)

            def dense(name, b0, cols, ready, first_two=True):
                slots = 8 // len(cols)
                dst = [[ps[:, (j % slots) * len(cols) + c, 0:n] for c, (_, n) in enumerate(cols)] for j in range(8)]
                blocks = [(b0 + i, b0 + i) for i in range(4)]
                for i in ((0, 2, 3) if ready else range(4)):
                    both = bool(ready) and i == 0
                    if 2 * i + 2 > slots:
                        pe.wait_ge(*when(f"{name}_evac", 2 * i + 2 - slots))
                    columns(f"{name}_done", blocks[i:i + 1 + both], cols, dst[2 * i:], ready if both else None)

            pe.wait_ge(*when("setup", 1))
            rms("n1")
            pe.wait_ge(*when("n1_std", 1))
            win = [(B_WIN + i, B_WIN + i) for i in range(6)]
            banks = [[ps[:, j, :]] for j in range(8)]
            columns("win_done", win[0:2], X_ONLY, banks[0:4], "n1_out")
            columns("win_done", win[2:3], X_ONLY, banks[4:6])
            columns("win_done", win[3:4], X_ONLY, banks[6:8])
            pe.wait_ge(*when("u", 2))
            columns("win_done", win[4:5], X_ONLY, banks[0:2])
            columns("win_done", win[5:6], X_ONLY, banks[2:4])
            pe.wait_ge(*when("small", 16 * N_SMALL))
            pe.wait_ge(*when("u", 4))
            for c in range(2):
                mm = pe.matmul(ps[:, 4 + c, :], csd[:, c * P:(c + 1) * P], fmap, start=True, stop=True)
            mm.then_inc(sem("csm_done"), 1)
            for h in range(HEADS_A):
                pe.wait_ge(*when("pf", h + 1))
                if h == 0:
                    pe.wait_ge(*when("csm", 2))
                else:
                    if h >= 2:
                        pe.wait_ge(*when("z", h - 1))
                zb = (4 + 2 * (h % 2)) * 512
                for t in range(QT):
                    mm = pe.matmul(psf[:, zb + t * 256:zb + (t + 1) * 256], pf[:, h, t * P:(t + 1) * P], csm[:, h, :],
                                   start=True, stop=True)
                mm.then_inc(sem("z_done"), 1)
            for h in range(HEADS_A):
                pe.wait_ge(*when("z", h + 1))
                if h == 0:
                    pe.wait_ge(*when("dft", 16))
                for t in range(QT):
                    for c in range(2):
                        mm = pe.matmul(ps[:, h, :], zz[:, h % 2, t * 256 + c * P:t * 256 + (c + 1) * P], dft[:, c, t, :],
                                       start=(t == 0 and c == 0), stop=(t == QT - 1 and c == 1))
                mm.then_inc(sem("y_done"), 1)
            for h in range(4):
                pe.wait_ge(*when("conv", h + 1))
                pe.matmul(ps[:, 4 + h, :], ones[:, :], conv[:, h, :], start=True, stop=True).then_inc(sem("cmu"), 1)
            for h in range(4):
                pe.wait_ge(*when("csq", h + 1))
                if h == 0:
                    pe.wait_ge(*when("mix_out", 4))
                pe.matmul(ps[:, h, :], ones[:, :], tmp[:, h, 0:T], start=True, stop=True).then_inc(sem("cvar"), 1)
            pe.wait_ge(*when("cstd", 4))
            dense("wout", B_WOUT, X_ONLY, "mix_out")

            def ada(b, slot, e):
                for k in range(KT):
                    if k % 4 == 0:
                        pe.wait_ge(*when("w_split", 2 * b + (k // 4 + 1)))
                    for w in (whi, wlo):
                        mm = pe.matmul(ps[:, 6 + e, 0:256], c4[:, k, :], w[:, slot, k * 256:(k + 1) * 256],
                                       start=(k == 0 and w is whi), stop=(k == KT - 1 and w is wlo))
                    if k % 4 == 3:
                        mm.then_inc(sem("w_used"), 1)

            def ada_select(name, pairs):
                pe.wait_ge(*when(f"{name}_arow", 2 * pairs))
                for j in range(4):
                    mm = pe.matmul(ps[:, 6, 2 * j:2 * j + 2], arow[0:4, j // 2, (j % 2) * P:(j % 2 + 1) * P],
                                   sel4[:, :], start=True, stop=True)
                mm.then_inc(sem(f"{name}_sel"), 1)

            def down_job(name, i, b, at, m, rhs, cols, slots):
                if m % 4 == 0:
                    pe.wait_ge(*when("w_split", 2 * b + (m // 4 + 1)))
                pe.wait_ge(*when(f"{name}_dfree", 8 * i + (m + 9 - slots)))
                dst = [ps[:, 4 + len(cols) * (m % slots) + c, 0:n] for c, (_, n) in enumerate(cols)]
                for k in range(2):
                    mm = product(dst, cols, at, m // 4 * HALF + k * 512 + m % 4 * P, rhs, k, 2)
                mm.then_inc(sem("w_used" if m % 4 == 3 else f"{name}_down"), 1)

            def swiglu(f, name, ready):
                B0 = B_FF[f]

                def up(i, b, at):
                    for part in range(2):
                        ada(b + 2 * part, (at + 2 * part) % RING, part)
                        pe.wait_ge(*when(f"{name}_silu" if part == 0 else f"{name}_mul", 2 * i))
                        columns(f"{name}_up", [(b + 2 * part + 1, at + 2 * part + 1)], X_ONLY, banks[2 * part:2 * part + 2])
                    ada_select(name, i + 1)

                def down(i, b, at, slot):
                    pe.wait_ge(*when(f"{name}_h", 2 * i + 2))
                    for m in range(KT):
                        down_job(name, i, b, at, m, h_rhs(slot), X_ONLY, 2)

                for e in range(2):
                    ada(B0 + e, (B0 + e) % RING, e)
                columns(f"{name}_up", [(B0 + 2, B0 + 2), (B0 + 3, B0 + 3)], X_ONLY, banks[0:4], ready)
                ada_select(name, 1)

                def step(i, b, at, s):
                    pe.wait_ge(*when(f"{name}_ada", i + 1))
                    up(i + 1, b, at)
                    down(i, b + 4, at + 4, s)

                with pe.Fori(0, FF_IT // 3) as p:
                    for s in range(3):
                        at = B0 + 4 + 5 * s
                        step(3 * p + s, 15 * p + at, at, s)
                for i in range(FF_IT // 3 * 3, FF_IT - 1):
                    b = B0 + 4 + 5 * i
                    step(i, b, b, i % 3)
                i = FF_IT - 1
                b = B0 + 4 + 5 * i
                pe.wait_ge(*when(f"{name}_ada", i + 1))
                for e in range(2):
                    ada(b + e, (b + e) % RING, e)
                ada_select(name, i + 2)
                down(i, b + 2, b + 2, i % 3)

            rms("n2")
            pe.wait_ge(*when("c4", 3))
            swiglu(0, "ff0", "n2_out")
            rms("n3")
            for g in range(4):
                if g % 2 == 0:
                    pe.wait_ge(*when("w_split", 2 * B_POOL + g // 2 + 1))
                pe.wait_ge(*(when("pool_lo", 2 * g + 2) if g < 3 else when("pool_last", 2)))
                for m in range(2):
                    j = 2 * g + m
                    for k in range(2):
                        mm = product([ps[:, j, :]], X_ONLY, B_POOL, g // 2 * HALF + k * 512 + g % 2 * 256 + m * P,
                                     lambda k, part, c0, n: a_rhs(2 * g + k, part, c0, n), k, 2)
                    mm.then_inc(sem("w_used" if j % 4 == 3 else "pool_done"), 1)
            rms("n4")
            swiglu(1, "ff1", "n4_out")
            rms("n5")

            columns("kvA_done", [(B_KV, B_KV)], X_CTX, [[ps[:, 4, :], ps[:, 5, 0:C]], [ps[:, 6, :], ps[:, 7, 0:C]]], "n5_out")
            pe.wait_ge(*when("w_split", 2 * B_KV + 4))
            for k in range(KT):
                mm = product([ps[:, 0, :], ps[:, 1, 0:C]], X_CTX, B_KV + 1, k * 256, a_rhs, k, KT)
            mm.then_inc(sem("w_used"), 2)
            pe.wait_ge(*when("kvA_evac", 3))
            for t in range(NTT):
                mm = pe.transpose(psf[:, 4 * 512 + t * P:4 * 512 + (t + 1) * P], vT[:, t * P:(t + 1) * P], ident[:, :])
            mm.then_inc(sem("vA_done"), 1)

            pe.wait_ge(*when("vA", 1))
            dense("qA", B_WQA, X_CTX, None)

            def window_scores(u, g, e, h, n):
                q = qs[4 * e + h][:, n * P:(n + 1) * P]
                mid = 2 * (u % 2) * 512 + 512
                first, last = window(n)
                if last > first:
                    a = mid - (last - first) * P
                    ends = [k for k in (first, last - 1) if k != n]
                    for part in (kh, kl):
                        pe.matmul(psf[:, a:mid], q, part[:, first * P:last * P], start=(part is kh), stop=False,
                                  skip_group_check=True)
                    for k in ends:
                        at = a + (k - first) * P
                        pe.matmul(psf[:, at:at + P], maskb[:, 0, :], maskb[:, 1 if k < n else 2, :], start=False,
                                  stop=(k == ends[-1]), skip_group_check=True)
                for part in (kh, kl):
                    pe.matmul(psf[:, mid:mid + C], q, part[:, T:TT], start=(part is kh), stop=(part is kl))
                sink = vec[:, bass.ds(8 * g + (_cols["sink"][0] + 4 * e + h), 1)]
                return pe.matmul(psf[:, mid + C:mid + C + 1], ident[:, :], sink, start=True, stop=True)

            def turned(u, t):
                at = (4 + u % 2) * 512 + t * P if t < 4 else 7 * 512
                return psf[:, at:at + P]

            def window_turn(u, n, unit):
                pe.wait_ge(*when("pA", unit + 1))
                pe.wait_ge(*when("ptA", unit + 1))
                for t in range(len(keys(n))):
                    if t == 4:
                        pe.wait_ge(*when("ptA", unit + 2))
                    mm = pe.transpose(turned(u, t), probA[u % 4][:, t * P:(t + 1) * P], ident[:, :])
                mm.then_inc(sem("turnA"), 1)

            def window_values(four, part, g):
                ks = keys(UNITS[4 * four][1])
                nth = N_UNITS // 4 * g + four
                if part == 0:
                    pe.wait_ge(*when("ptA", 4 * nth + 6))
                    pe.wait_ge(*when("oA", nth + 1))
                    if four == 0:
                        pe.wait_ge(*when("vcur", g + 1))
                for t in range(len(ks)):
                    if t // 2 == part:
                        mm = pe.matmul(ps[0:DH, 6, :], vcur[:, ks[t], :], ptA[four % 2][:, t, :], start=(t == 0),
                                       stop=(t == len(ks) - 1), skip_group_check=True)
                        if t == len(ks) - 1:
                            mm.then_inc(sem("oA_done"), 1)

            pe.wait_ge(*when("maskb", 2))
            pe.sem_inc(sem("turnA"), 4)
            pe.sem_inc(sem("oA_done"), 2)
            with pe.Fori(0, 2) as g:
                pe.wait_ge(*when("ks", g + 1))
                for u in range(N_UNITS + LEAD + 3):
                    unit = N_UNITS * g + u
                    if u < N_UNITS:
                        e, n, h = UNITS[u]
                        if n == Q_TILES[0]:
                            pe.wait_ge(*when("qs", 8 * g + 4 * e + h + 1))
                        pe.wait_ge(*when("sA_free", unit + 1))
                        window_scores(u, g, e, h, n).then_inc(sem("sA"), 1)
                    if LEAD <= u < N_UNITS + LEAD:
                        window_turn(u - LEAD, UNITS[u - LEAD][1], unit - LEAD)
                    four, part = divmod(u - LEAD - 4, 4)
                    if four >= 0 and part < 3:
                        window_values(four, part, g)
            dense("woA", B_WOA, X_CTX, "OA_split")
            pe.wait_ge(*when("woA_evac", 5))
            layernorm("l1", X_CTX, "woA_evac", 0)

            def mlp(l, name, cols, ready):
                B0 = B_ML[l]

                slots = 4 // len(cols)
                dsts = [[ps[:, j * len(cols) + c, 0:n] for c, (_, n) in enumerate(cols)] for j in range(2)]

                def up(i, b, at, ready=None):
                    columns(f"{name}_up", [(b, at)], cols, dsts, ready)

                def down(i, b, at, slot):
                    pe.wait_ge(*when(f"{name}_h", 2 * i + 2))
                    for m in range(KT):
                        down_job(name, i, b, at, m, h_rhs(slot), cols, slots)

                up(0, B0, B0, ready)
                with pe.Fori(0, (ML_IT - 1) // 3) as p:
                    for s in range(3):
                        i = 3 * p + s
                        at = B0 + 1 + 2 * s
                        pe.wait_ge(*when(f"{name}_relu", 2 * i + 2))
                        up(i + 1, 6 * p + at, at)
                        down(i, 6 * p + at + 1, at + 1, s)
                i = ML_IT - 1
                down(i, B0 + 1 + 2 * i, B0 + 1 + 2 * i, i % 3)

            mlp(0, "ml0", X_CTX, "l1_out")
            layernorm("l2", X_CTX, "ml0_dfree", 8 * ML_IT)

            def diff_turn(u, unit):
                pe.wait_ge(*when("pB", unit + 1))
                if u < 7:
                    pe.wait_ge(*when("aT", unit + 1))
                for t in range(NTT):
                    mm = pe.transpose(psf[:, turn_at(u) + t * P:turn_at(u) + (t + 1) * P], probB[u % 3][:, t * P:(t + 1) * P],
                                      ident[:, :])
                mm.then_inc(sem("turnB"), 1)

            def diff_values(hh, unit, nth):
                pe.wait_ge(*when("aT", unit + 2))
                pe.wait_ge(*when("oB", nth + 1))
                for t in range(NTT):
                    mm = pe.matmul(ps[:, 6, :], vB[:, t, hh * P:(hh + 1) * P], aT[:, t, :],
                                   start=(t == 0), stop=(t == NTT - 1))
                mm.then_inc(sem("oB_done"), 1)

            pe.sem_inc(sem("turnB"), 3)
            pe.sem_inc(sem("oB_done"), 1)
            with pe.Fori(0, 4) as st:
                pe.wait_ge(*when("oB", 2 * st + 1))
                job = 0
                for which in range(2):
                    pe.wait_ge(*when("w_split", 6 * st + 2 * (B_QKV + which + 1)))
                    for m in range(2):
                        for c, (c0, n) in enumerate(X_CTX[:1 + which]):
                            pe.wait_ge(*when(f"qkB_free{job % 2}", 3 * st + job // 2 + 1))
                            for k in range(KT):
                                if job == 0:
                                    pe.wait_ge(*when("l2_out", k + 1))
                                if c == 1:
                                    pe.wait_ge(*when("l2_out", KT + k + 1))
                                mm = product([ps[:, 6 + job % 2, 0:n]], [(c0, n)], B_QKV + which, k * 256 + m * P, a_rhs, k, KT)
                            done(mm, "qkB_done", m == 1 and c == which)
                            job += 1
                def values_of(t):
                    pe.wait_ge(*when("vB", 6 * st + t + 1))
                    for k in range(KT):
                        for a, w in ((Ahi, whi), (Alo, whi), (Ahi, wlo)):
                            mm = pe.matmul(ps[:, 6 + t % 2, 0:256], a[:, k, t * P:(t + 1) * P],
                                           w[:, (B_QKV + 2) % RING, k * 256:(k + 1) * 256],
                                           start=(k == 0 and a is Ahi and w is whi), stop=(k == KT - 1 and w is wlo))
                    done(mm, "vB_done", t == NTT - 1)

                pe.wait_ge(*when("w_split", 6 * st + 2 * (B_QKV + 3)))
                for m in range(2):
                    pe.wait_ge(*when(f"qkB_free{m}", 3 * st + 4))
                for t in range(V_FIRST):
                    values_of(t)
                pe.wait_ge(*when("qkB_lo", 4 * st + 4))
                for u in range(10):
                    if u < 8:
                        hh, n = u // 4, u % 4
                        for t in range(2):
                            pe.wait_ge(*when("sB_free", 16 * st + 2 * u + t + 1))
                            for part in range(2):
                                q = qB[hh][:, part * 4 + t * 2 + n // 2, n % 2 * P:n % 2 * P + P]
                                for half in range(2):
                                    a = 2 * t * 512 + P + half * 384
                                    mm = pe.matmul(psf[:, a:a + 384], q, kB[hh][t][:, half * 384:half * 384 + 384],
                                                   start=(part == 0), stop=(part == 1))
                            mm.then_inc(sem("sB"), 1)
                    if V_FIRST + u < NTT:
                        values_of(V_FIRST + u)
                    if u == 7:
                        pe.wait_ge(*when("vB", 6 * st + 8))
                        diff_values(0, 8 * st + 3, 2 * st)
                    if 2 <= u < 10:
                        diff_turn(u - 2, 8 * st + u - 2)
                diff_values(1, 8 * st + 7, 2 * st + 1)
            for h in range(8):
                pe.wait_ge(*when("oB_sq", h + 1))
                for t in range(QT):
                    mm = pe.matmul(ps[:, 4, h * QT + t:h * QT + t + 1], tmp[:, h % 4, t * P:(t + 1) * P], ones[:, 0:1],
                                   start=True, stop=True)
                mm.then_inc(sem("oB_ms"), 1)
            pe.wait_ge(*when("oB_r", 2))
            for h in range(8):
                if h >= 4:
                    pe.wait_ge(*when("oB_n", h - 3))
                for t in range(QT):
                    mm = pe.matmul(ps[:, 4 + h % 4, t * P:(t + 1) * P],
                                   hnorm[:, 1, h * QT + t:h * QT + t + 1].to_broadcast([P, P]), ident[:, :], start=True, stop=True)
                mm.then_inc(sem("oB_b"), 1)
            dense("woB", B_WOB, X_ONLY, "OB_split")
            layernorm("l3", X_ONLY, "woB_evac", 0)
            mlp(1, "ml1", X_ONLY, "l3_out")
            layernorm("l4", X_ONLY, "ml1_dfree", 8 * ML_IT)

        @block.scalar
        def _(act):
            def copy(dst, src, scale=1.0):
                return act.activation(dst, src, ACT.Copy, scale=scale)

            def norm_squares(name, src, ready, before, each, width):
                for k in range(KT):
                    if ready == "x":
                        act.wait_ge(*when(f"x{k // 4}", 16))
                    else:
                        act.wait_ge(*when(ready, before + each * (k + 1)))
                    if k >= 4:
                        act.wait_ge(*when(f"{name}_sum", k - 3))
                    act.activation(tmp[:, k % 4, 0:width], src[:, k, 0:width], ACT.Square).then_inc(sem(f"{name}_sq"), 1)

            def norm_std(name, bank, cols, eps):
                act.wait_ge(*when(f"{name}_sum", KT))
                for c, (c0, n) in enumerate(cols):
                    act.activation(std[:, c0:c0 + n], ps[:, bank + c, 0:n], ACT.Sqrt, scale=1.0 / D,
                                   bias=epsr[:, eps:eps + 1]).then_inc(sem(f"{name}_std"), 1)

            def split_hi(name, src, ready, each, width):
                for k in range(KT):
                    act.wait_ge(*when(ready, each * (k + 1)))
                    copy(Ahi[:, k, 0:width], src(k)).then_inc(sem(f"{name}_hi"), 1)

            def normed(k):
                return tmp[:, k % 4, 0:T]

            def rms(name, bank, ready, before, split=True):
                norm_squares(name, X, ready, before, 1, T)
                norm_std(name, bank, X_ONLY, 0)
                if split:
                    split_hi(name, normed, f"{name}_y", 1, T)

            def split_hi_modulated(name, use, cols):
                for nth, part in enumerate(PASSES[name]):
                    for k in range(KT):
                        act.wait_ge(*when(f"{name}_m", len(part) * (nth * KT + k + 1)))
                        for c in part:
                            c0, n = cols[c]
                            mm = act.activation(Ahi[:, k, c0:c0 + n], tmp[:, k % 4, c0:c0 + n], ACT.Identity,
                                                bias=s2[:, use, k, c:c + 1])
                        mm.then_inc(sem(f"{name}_hi"), 1)

            def layernorm(name, cols, bank, use):
                width = sum(n for _, n in cols)
                norm_squares(name, X, f"{name}_d", 0, len(cols), width)
                norm_std(name, bank, cols, 1)
                if use is not None:
                    split_hi_modulated(name, use, cols)
                    return
                for k in range(KT):
                    act.wait_ge(*when(f"{name}_y", k + 1))
                    act.activation(X[:, k, 0:width], X[:, k, 0:width], ACT.Identity,
                                   bias=v("ln2_b", KT + k)).then_inc(sem(f"{name}_res"), 1)

            act.wait_ge(*when("setup", 4))
            rms("n1", 0, "x", 0)
            act.wait_ge(*when("lam", 2))
            act.activation(lamt[:, 2:4], lamt[:, 0:2], ACT.Exp).then_inc(sem("lam"), 1)

            for t, j in enumerate((2, 3, 6, 7)):
                if j % 2:
                    act.wait_ge(*block_used(B_WIN + j // 2))
                else:
                    act.wait_ge(*when("win_done", j // 2 + 1))
                act.activation(tmp[:, t, 0:T], ps[:, j, :], ACT.Sigmoid).then_inc(sem("sig"), 1)
            act.wait_ge(*when("csm_done", 1))
            for c in range(2):
                copy(csm[:, :, c * P:(c + 1) * P], ps[:, 4 + c, :].rearrange("p (h e) -> p h e", h=HEADS_A)).then_inc(sem("csm"), 1)
            for h in range(HEADS_A):
                j = 8 + h
                if j % 2:
                    act.wait_ge(*block_used(B_WIN + j // 2))
                else:
                    act.wait_ge(*when("win_done", j // 2 + 1))
                copy(pf[:, h, :], ps[:, h, :]).then_inc(sem("pf"), 1)

            def fourier_mid(h):
                act.wait_ge(*when("z_done", h + 1))
                if h >= 2:
                    act.wait_ge(*when("y_done", h - 1))
                zb = (4 + 2 * (h % 2)) * 512
                copy(zz[:, h % 2, :], psf[:, zb:zb + 1024]).then_inc(sem("z"), 1)

            def fourier_out(h):
                act.wait_ge(*when("y_done", h + 1))
                copy(Ahi[:, h, 0:T], ps[:, h, :]).then_inc(sem("mix_hi"), 1)

            fourier_mid(0)
            fourier_mid(1)
            for h in range(2, HEADS_A):
                fourier_mid(h)
                fourier_out(h - 2)
            fourier_out(2)
            fourier_out(3)
            act.activation(csil[:, :, :], v("c", 0, 2 * KT).rearrange("p (k s) -> p k s", s=2), ACT.Silu).then_inc(sem("csil"), 1)
            act.wait_ge(*when("csil", 1))
            act.wait_ge(*when("c4", 1))
            copy(c4[:, :, 0:2], csil[:, :, :]).then_inc(sem("c4"), 1)
            for h in range(4):
                act.wait_ge(*when("cd", h + 1))
                act.activation(tmp[:, h, 0:T], conv[:, h, :], ACT.Square).then_inc(sem("csq"), 1)
            for h in range(4):
                act.wait_ge(*when("cvar", h + 1))
                act.activation(pf[:, h, :], ps[:, h, :], ACT.Sqrt, scale=1.0 / P, bias=epsr[:, 1:2]).then_inc(sem("cstd"), 1)
            for h in range(4):
                act.wait_ge(*when("cy", h + 1))
                act.activation(tmp[:, h, 0:T], conv[:, h, :], ACT.Silu, bias=v("conv_ln_b", h)).then_inc(sem("csilu"), 1)
            for h in range(4):
                act.wait_ge(*when("csilu", h + 1))
                copy(Ahi[:, 4 + h, 0:T], tmp[:, h, 0:T]).then_inc(sem("mix_hi"), 1)

            def swiglu(f, name):
                B0 = B_FF[f]

                def rows(b_a, gap):
                    for e in range(2):
                        act.wait_ge(*block_used(b_a + gap * e))
                        copy(arow[:, e, :], ps[0:4, 6 + e, 0:256]).then_inc(sem(f"{name}_arow"), 1)

                def step(i, b, slot, first):
                    rows(b, 1 if first else 2)
                    for j in range(2):
                        if j:
                            act.wait_ge(*block_used(b + 2 if first else b + 1))
                        else:
                            act.wait_ge(*when(f"{name}_up", 2 * i + 1))
                        if not first:
                            act.wait_ge(*when(f"{name}_mul", 2 * i + j - 1))
                        act.activation(tmp[:, 2 + j, 0:T], ps[:, j, :], ACT.Silu).then_inc(sem(f"{name}_silu"), 1)
                    for j in range(2):
                        act.wait_ge(*when(f"{name}_mul", 2 * i + j + 1))
                        copy(hhi[:, slot, j, 0:T], tmp[:, j, 0:T]).then_inc(sem(f"{name}_hi"), 1)

                step(0, B0, 0, True)
                with act.Fori(0, FF_IT // 3) as p:
                    for s in range(3):
                        step(3 * p + s + 1, 15 * p + (B0 + 4 + 5 * s), (s + 1) % 3, False)
                for i in range(FF_IT // 3 * 3 + 1, FF_IT):
                    step(i, B0 + 5 * i - 1, i % 3, False)
                rows(B0 + 4 + 5 * (FF_IT - 1), 1)

            rms("n2", 0, "wout_evac", 0)
            act.dma_start(icnt.rearrange("p a b -> p (a b)"), ins["icnt"]).then_inc(sem("icnt"), 16)
            swiglu(0, "ff0")
            rms("n3", 0, "ff0_dfree", 8 * FF_IT, split=False)
            for k in range(KT):
                act.wait_ge(*when("pool_y", k // 2 + 1))
                copy(Ahi[:, k, 0:T], tmp[:, k % 4, 0:T]).then_inc(sem("pool_hi"), 1)
            act.wait_ge(*when("pool_lo", 6))
            rms("n4", 0, "pool_evac", 0)
            for name, dst in (("cosq", cosq), ("sinq", sinq), ("masks", masks.rearrange("p a k -> p (a k)"))):
                act.dma_start(dst, ins[name]).then_inc(sem("tables"), 16)
            swiglu(1, "ff1")
            rms("n5", 0, "ff1_dfree", 8 * FF_IT, split=False)
            split_hi_modulated("n5", 0, X_CTX)

            def swap_halves(swap, slot, src, scale):
                for q in range(4):
                    mm = copy(swap[32 * q:32 * q + 32, slot, :], src[32 * (q ^ 1):32 * (q ^ 1) + 32, :], scale)
                return mm

            act.wait_ge(*when("tables", 16 * 5))
            copy(maskb[:, 0, :], ident[:, :]).then_inc(sem("maskb"), 1)
            copy(maskb[:, 1:3, :], masks).then_inc(sem("maskb"), 1)
            for j in range(2):
                if j:
                    act.wait_ge(*block_used(B_KV))
                else:
                    act.wait_ge(*when("kvA_done", 1))
                bank = 4 + 2 * j
                copy(kd[:, j, T:TT], ps[:, bank + 1, 0:C])
                swap_halves(swapA, j, ps[:, bank, :], 1.0).then_inc(sem("kvA_swap"), 1)
            act.wait_ge(*block_used(B_KV + 1))
            copy(vT[:, 0:T], ps[:, 0, :])
            copy(vT[:, T:TT], ps[:, 1, 0:C]).then_inc(sem("kvA_evac"), 1)
            for j in range(8):
                if j % 2:
                    act.wait_ge(*block_used(B_WQA + j // 2))
                else:
                    act.wait_ge(*when("qA_done", j // 2 + 1))
                bank = 2 * (j % 4)
                copy(O[:, j, T:TT], ps[:, bank + 1, 0:C], SCALE)
                if j < 2:
                    act.wait_ge(*when("kvA_evac", 3))
                else:
                    act.wait_ge(*when("qA_evac", j - 1))
                swap_halves(swapA, j % 2, ps[:, bank, :], SCALE).then_inc(sem("qA_swap"), 1)

            act.sem_inc(sem("ptA"), 2)
            act.sem_inc(sem("sA_free"), 2)
            with act.Fori(0, 2) as g:
                def take_query(e, h):
                    half = slice(DH * (h % 2), DH * (h % 2) + DH)
                    copy(qs[4 * e + h][half], O[half, bass.ds(4 * g + (2 * e + h // 2), 1), :].rearrange("p a t -> p (a t)")).then_inc(sem("qs_hi"), 1)

                act.wait_ge(*when("kvA_evac", 2))
                copy(kh[:, :], kd[:, bass.ds(g, 1), :].rearrange("p a t -> p (a t)")).then_inc(sem("ks_hi"), 1)
                for h in range(4):
                    if h == 0:
                        act.wait_ge(*when("qA_evac", 4 * g + 1))
                    if h == 2:
                        act.wait_ge(*when("qA_evac", 8))
                    take_query(0, h)
                def take_turned(u):
                    e, n, h = UNITS[u]
                    nk = len(keys(n))
                    four = (4 + u % 2) * 512
                    act.wait_ge(*when("turnA", N_UNITS * g + u + 5))
                    act.wait_ge(*when("oA_done", N_UNITS // 4 * g + u // 4 + 1))
                    if nk > 4:
                        copy(ptA[u // 4 % 2][:, 4, h * P:(h + 1) * P], psf[:, 7 * 512:7 * 512 + P])
                        nk = 4
                    copy(ptA[u // 4 % 2][:, 0:nk, h * P:(h + 1) * P],
                         psf[:, four:four + nk * P].rearrange("p (t q) -> p t q", t=nk)).then_inc(sem("ptA"), 1)

                for u in range(N_UNITS + LEAD):
                    if u >= LEAD:
                        take_turned(u - LEAD)
                    if u < N_UNITS:
                        e, n, h = UNITS[u]
                        unit = N_UNITS * g + u
                        W = len(keys(n)) * P
                        a = 2 * (u % 2) * 512 + 512 + C - W
                        c = sm[:, u % 8, :]
                        act.wait_ge(*when("nmA", unit + 1))
                        act.wait_ge(*when("turnA", unit + 1))
                        act.activation(probA[u % 4][:, 0:W + 1], psf[:, a:a + W + 1], ACT.Exp, bias=c[:, 0:1],
                                       accum_out=c[:, 1:2]).then_inc(sem("sA_free"), 1)
                        if u in TAKE_AT:
                            take_query(1, TAKE_AT.index(u))
            for k in range(KT):
                if k == 0:
                    act.wait_ge(*when("oA", 25))
                copy(Ahi[:, k, :], O[:, k, :]).then_inc(sem("OA_hi"), 1)
            layernorm("l1", X_CTX, 2, 1)

            def mlp(l, name, cols):
                B0 = B_ML[l]
                width = sum(n for _, n in cols)

                def step(i, b_u, slot, first):
                    for j in range(2):
                        if j:
                            act.wait_ge(*block_used(b_u))
                        else:
                            act.wait_ge(*when(f"{name}_up", i + 1))
                        if not first:
                            act.wait_ge(*when(f"{name}_mul", 2 * i + j - 1))
                        for c, (c0, n) in enumerate(cols):
                            mm = act.activation(tmp[:, 2 + j, c0:c0 + n], ps[:, j * len(cols) + c, 0:n], ACT.Relu)
                        mm.then_inc(sem(f"{name}_relu"), 1)
                    for j in range(2):
                        act.wait_ge(*when(f"{name}_mul", 2 * i + j + 1))
                        copy(hhi[:, slot, j, 0:width], tmp[:, j, 0:width]).then_inc(sem(f"{name}_hi"), 1)

                step(0, B0, 0, True)
                with act.Fori(0, (ML_IT - 1) // 3) as p:
                    for s in range(3):
                        step(3 * p + s + 1, 6 * p + (B0 + 1 + 2 * s), (s + 1) % 3, False)

            mlp(0, "ml0", X_CTX)
            layernorm("l2", X_CTX, 2, 2)

            act.sem_inc(sem("aT"), 1)
            act.sem_inc(sem("vB"), 2)
            act.sem_inc(sem("sB_free"), 2)
            with act.Fori(0, 4) as st:
                b = 3 * st + B_QKV

                def swapped(src, scale, nth):
                    act.wait_ge(*when("qkB", 4 * st + nth + 1))
                    swap_halves(swapB, nth % 2, src, scale).then_inc(sem("swB"), 1)

                def query_hi(m):
                    act.wait_ge(*when("qkB", 4 * st + m + 3))
                    for t in range(2):
                        q_two = rot[DH * t:DH * t + DH, m, 0:T].rearrange("p (a n) -> p a n", a=2)
                        for half in range(2):
                            mm = copy(qB[m][DH * half:DH * half + DH, 2 * t:2 * t + 2, :], q_two)
                    mm.then_inc(sem("qkB_hi"), 1)

                def key_hi(m):
                    act.wait_ge(*when("qkB", 4 * st + m + 5))
                    act.wait_ge(*when("qkB_free1", 3 * st + m + 3))
                    if m == 1:
                        act.wait_ge(*when("l2_y", KT))
                    for t in range(2):
                        mm = copy(kB[m][t][DH * t:DH * t + DH], rot[DH * t:DH * t + DH, m, :])
                    mm.then_inc(sem("qkB_hi"), 1)

                def key_swap(m):
                    act.wait_ge(*when("qkB_done", 4 * st + 2 + 2 * m))
                    swapped(ps[:, 6, :], 1.0, 2 + m)
                    if m:
                        act.wait_ge(*block_used(b + 1))
                    else:
                        act.wait_ge(*when("qkB_done", 4 * st + 3))
                    copy(rot[:, m, T:TT], ps[:, 7, 0:C]).then_inc(sem("qkB_free1"), 1)

                act.wait_ge(*when("qkB_done", 4 * st + 1))
                swapped(ps[:, 6, :], SCALE, 0)
                act.wait_ge(*block_used(b))
                swapped(ps[:, 7, :], SCALE, 1)
                query_hi(0)
                key_swap(0)
                query_hi(1)
                key_swap(1)
                key_hi(0)
                key_hi(1)
                def take_heads_values(t):
                    if t < NTT - 1:
                        act.wait_ge(*when("vB_done", 5 * st + t + 1))
                    else:
                        act.wait_ge(*block_used(b + 2))
                    copy(vB[:, t, :], ps[:, 6 + t % 2, 0:256]).then_inc(sem("vB"), 1)

                for t in range(V_FIRST):
                    take_heads_values(t)
                for u in range(10):
                    if 1 <= u < 9:
                        act.wait_ge(*when("denB", 16 * st + 2 * u - 1))
                        p0 = probB[(u - 1) % 3]
                        copy(p0, p0, sm[:, (u - 1) % 4, 4:5]).then_inc(sem("p0B"), 1)
                    if u < 8:
                        act.wait_ge(*when("turnB", 8 * st + u + (2 if u < 2 else 1)))
                        for t in range(2):
                            a = 2 * t * 512 + P
                            c = sm[:, u % 4, :]
                            act.wait_ge(*when("nmB", 16 * st + 2 * u + t + 1))
                            act.activation((probB2[u % 2] if t else probB[u % 3]), psf[:, a:a + TT], ACT.Exp, bias=c[:, t:t + 1],
                                           accum_out=c[:, 2 + t:3 + t]).then_inc(sem("sB_free"), 1)
                    if V_FIRST + u < NTT:
                        take_heads_values(V_FIRST + u)
                    for v_u in TURNED_B[u]:
                        n = v_u % 4
                        act.wait_ge(*when("turnB", 8 * st + v_u + 4))
                        act.wait_ge(*when("oB_done", 2 * st + v_u // 4 + 1))
                        copy(aT[:, :, n * P:(n + 1) * P],
                             psf[:, turn_at(v_u):turn_at(v_u) + TT].rearrange("p (t q) -> p t q", t=NTT)).then_inc(sem("aT"), 1)
            for h in range(8):
                act.wait_ge(*when("oB_t", h + 1))
                act.activation(tmp[:, h % 4, 0:T], tmp[:, h % 4, 0:T], ACT.Square).then_inc(sem("oB_sq"), 1)
            act.wait_ge(*when("oB_flag", 1))
            act.activation(hnorm[:, 1, :], ps[:, 4, 0:8 * QT], ACT.Sqrt, scale=1.0 / P, bias=epsr[:, 2:3]).then_inc(sem("oB_std"), 1)
            for h in range(8):
                act.wait_ge(*when("oB_n", h + 1))
                copy(Ahi[:, h, 0:T], O[:, h, 0:T]).then_inc(sem("OB_hi"), 1)
            layernorm("l3", X_ONLY, 2, 3)
            mlp(1, "ml1", X_ONLY)
            layernorm("l4", X_ONLY, 2, None)

        @block.vector
        def _(dve):
            def split_lo(out_sem, hi_sem, k, src, width):
                dve.wait_ge(*when(hi_sem, k + 1))
                dve.tensor_tensor(Alo[:, k, 0:width], src, Ahi[:, k, 0:width], ALU.subtract).then_inc(sem(out_sem), 1)

            def norm_rstd(name, n_std, width):
                dve.wait_ge(*when(f"{name}_std", n_std))
                dve.reciprocal(rstd[:, 0:width], std[:, 0:width]).then_inc(sem(f"{name}_rstd"), 1)
                dve.wait_ge(*when(f"{name}_rstd", 1))

            def scaled(name, k, g, dst, width=T):
                return dve.scalar_tensor_tensor(out=dst, in0=X[:, k, 0:width], scalar=v(g[0], g[1] + k),
                                                in1=rstd[:, 0:width], op0=ALU.mult, op1=ALU.mult)

            def rms(name, g):
                norm_rstd(name, 1, T)
                for k in range(KT + 1):
                    if k < KT:
                        scaled(name, k, g, tmp[:, k % 4, 0:T]).then_inc(sem(f"{name}_y"), 1)
                    if k >= 1:
                        split_lo(f"{name}_out", f"{name}_hi", k - 1, tmp[:, (k - 1) % 4, 0:T], T)

            def modulated(name, nth, k, use, c, c0, n):
                if k >= 4 and c == PASSES[name][nth][0]:
                    dve.wait_ge(*when(f"{name}_out", nth * KT + k - 3))
                dve.scalar_tensor_tensor(out=tmp[:, k % 4, c0:c0 + n], in0=X[:, k, c0:c0 + n], scalar=s1[:, use, k, c:c + 1],
                                         in1=rstd[:, c0:c0 + n], op0=ALU.mult, op1=ALU.mult).then_inc(sem(f"{name}_m"), 1)

            def split_lo_modulated(name, nth, k, use, cols):
                dve.wait_ge(*when(f"{name}_hi", nth * KT + k + 1))
                for c in PASSES[name][nth]:
                    c0, n = cols[c]
                    mm = dve.scalar_tensor_tensor(out=Alo[:, k, c0:c0 + n], in0=tmp[:, k % 4, c0:c0 + n],
                                                  scalar=s2[:, use, k, c:c + 1], in1=Ahi[:, k, c0:c0 + n],
                                                  op0=ALU.add, op1=ALU.subtract)
                mm.then_inc(sem(f"{name}_out"), 1)

            def layernorm(name, cols, bank, use):
                width = sum(n for _, n in cols)
                dve.wait_ge(*when(f"{name}_mu", 1))
                for k in range(KT):
                    for c, (c0, n) in enumerate(cols):
                        dve.scalar_tensor_tensor(out=X[:, k, c0:c0 + n], in0=ps[:, bank + c, 0:n], scalar=-1.0 / D,
                                                 in1=X[:, k, c0:c0 + n], op0=ALU.mult, op1=ALU.add).then_inc(sem(f"{name}_d"), 1)
                dve.wait_ge(*when(f"{name}_d", len(cols) * KT))
                norm_rstd(name, len(cols), width)
                if use is not None:
                    for nth, part in enumerate(PASSES[name]):
                        for k in range(KT + 2):
                            if k < KT:
                                for c in part:
                                    modulated(name, nth, k, use, c, *cols[c])
                            if k >= 2:
                                split_lo_modulated(name, nth, k - 2, use, cols)
                    return
                for k in range(KT):
                    scaled(name, k, ("ln2_g", KT), X[:, k, 0:width], width).then_inc(sem(f"{name}_y"), 1)

            dve.memset(ones[:, :], 1.0).then_inc(sem("setup"), 1)
            for i, e in enumerate((RMS_EPS, LN_EPS, LN_EPS * SUB_SCALE * SUB_SCALE)):
                dve.memset(epsr[:, i:i + 1], e).then_inc(sem("setup"), 1)
            dve.memset(upad, 0.0).then_inc(sem("upad"), 1)
            dve.memset(c4[:, :, :].bitcast(F32), 0.0).then_inc(sem("c4"), 1)
            dve.wait_ge(*when("vec", 16))
            pairs = v("lq1", 0, 4 * DH).rearrange("p (i s d) -> p i s d", i=2, s=2)
            products = rstd[:, T:T + 2 * DH].rearrange("p (i d) -> p i d", i=2)
            dve.tensor_tensor(products, pairs[:, :, 0], pairs[:, :, 1], ALU.mult).then_inc(sem("lam"), 1)
            dve.wait_ge(*when("lam", 1))
            dve.tensor_reduce(lamt[:, 0:2], products, AX_X, ALU.add).then_inc(sem("lam"), 1)
            rms("n1", ("mix_g", 0))
            dve.wait_ge(*when("lam", 3))
            dve.tensor_tensor(lamt[:, 4:5], lamt[:, 2:3], lamt[:, 3:4], ALU.subtract).then_inc(sem("lam"), 1)
            dve.wait_ge(*when("lam", 4))
            dve.tensor_scalar(lamt[:, 5:6], lamt[:, 4:5], LAM_INIT, -1.0, ALU.add, ALU.mult).then_inc(sem("lam"), 1)
            dve.tensor_scalar(lamt[:, 6:7], v("subln_g", 0), 1.0 - LAM_INIT, SUB_SCALE, ALU.mult, ALU.mult).then_inc(sem("lam"), 1)

            dve.wait_ge(*when("upad", 1))
            w = _cols["conv_w"][0]
            for first in (0, 2):
                pair = (first, first + 1)
                for t in pair:
                    dve.wait_ge(*when("sig", t + 1))
                    dve.tensor_tensor(upad[:, t, PADC:PADC + T], ps[:, 2 * first + t % 2, :], tmp[:, t, 0:T],
                                      ALU.mult).then_inc(sem("u"), 1)
                dve.wait_ge(*when("u", first + 2))
                for t in pair:
                    dve.tensor_scalar(conv[:, t, :], upad[:, t, 0:T], vec[:, w + t * TAPS:w + t * TAPS + 1], v("conv_b", t),
                                      ALU.mult, ALU.add).then_inc(sem("tap"), 1)
                taps = first * (TAPS - 1)
                with dve.Fori(1, TAPS - 1) as tap:
                    for t in pair:
                        dve.wait_ge(*when("tap", 2 * tap + (taps + t - first - 1)))
                        dve.scalar_tensor_tensor(out=conv[:, t, :], in0=upad[:, t, bass.ds(tap, T)],
                                                 scalar=vec[:, bass.ds(tap + (w + t * TAPS), 1)], in1=conv[:, t, :],
                                                 op0=ALU.mult, op1=ALU.add).then_inc(sem("tap"), 1)
                for t in pair:
                    last = w + t * TAPS + TAPS - 1
                    dve.wait_ge(*when("tap", taps + 2 * (TAPS - 1) + t - first - 1))
                    dve.scalar_tensor_tensor(out=conv[:, t, :], in0=upad[:, t, TAPS - 1:TAPS - 1 + T], scalar=vec[:, last:last + 1],
                                             in1=conv[:, t, :], op0=ALU.mult, op1=ALU.add).then_inc(sem("conv"), 1)
            for h in range(HEADS_A):
                split_lo("mix_out", "mix_hi", h, ps[:, h, :], T)
            dve.wait_ge(*when("c4", 2))
            dve.tensor_tensor(c4[:, :, 2:4], csil[:, :, :], c4[:, :, 0:2], ALU.subtract).then_inc(sem("c4"), 1)
            for h in range(4):
                dve.wait_ge(*when("cmu", h + 1))
                dve.scalar_tensor_tensor(out=conv[:, h, :], in0=ps[:, 4 + h, :], scalar=-1.0 / P, in1=conv[:, h, :],
                                         op0=ALU.mult, op1=ALU.add).then_inc(sem("cd"), 1)
            for h in range(4):
                dve.wait_ge(*when("cstd", h + 1))
                dve.reciprocal(pf[:, h, :], pf[:, h, :]).then_inc(sem("crstd"), 1)
                dve.wait_ge(*when("crstd", h + 1))
                dve.wait_ge(*when("cd", h + 1))
                dve.scalar_tensor_tensor(out=conv[:, h, :], in0=conv[:, h, :], scalar=v("conv_ln_g", h), in1=pf[:, h, :],
                                         op0=ALU.mult, op1=ALU.mult).then_inc(sem("cy"), 1)
            for h in range(4):
                split_lo("mix_out", "mix_hi", 4 + h, tmp[:, h, 0:T], T)
            for j in range(8):
                if j % 2:
                    dve.wait_ge(*block_used(B_WOUT + j // 2))
                else:
                    dve.wait_ge(*when("wout_done", j // 2 + 1))
                dve.tensor_tensor(X[:, j, 0:T], ps[:, j, :], X[:, j, 0:T], ALU.add).then_inc(sem("wout_evac"), 1)

            def swiglu(f, name):
                B0 = B_FF[f]
                dve.sem_inc(sem(f"{name}_dfree"), 8)

                def mods(pair):
                    dve.wait_ge(*when(f"{name}_sel", pair + 1))
                    a = _cols["b_ada"][0] + f * 2 * N_MOD * KT
                    dve.tensor_tensor(modT[:, f, bass.ds(4 * pair, 4), :].rearrange("p k s -> p (k s)"), ps[:, 6, 0:8],
                                      vec[:, bass.ds(8 * pair + a, 8)], ALU.add).then_inc(sem(f"{name}_ada"), 1)

                def hidden(i, b_u, j, first=False):
                    if j:
                        dve.wait_ge(*block_used(b_u))
                    else:
                        dve.wait_ge(*when(f"{name}_up", 2 * i + 2))
                    dve.wait_ge(*when(f"{name}_silu", 2 * i + j + 1))
                    if not first:
                        dve.wait_ge(*when(f"{name}_h", 2 * i + j - 1))
                    dve.tensor_tensor(tmp[:, j, 0:T], ps[:, 2 + j, :], tmp[:, 2 + j, 0:T], ALU.mult).then_inc(sem(f"{name}_mul"), 1)

                def hidden_lo(i, slot, j):
                    dve.wait_ge(*when(f"{name}_hi", 2 * i + j + 1))
                    dve.tensor_tensor(hlo[:, slot, j, 0:T], tmp[:, j, 0:T], hhi[:, slot, j, 0:T],
                                      ALU.subtract).then_inc(sem(f"{name}_h"), 1)

                def add_down(i, b_d, m):
                    if m % 4 == 3:
                        dve.wait_ge(*when("w_used", 2 * b_d + (m // 4 + 1)))
                    else:
                        dve.wait_ge(*when(f"{name}_down", 6 * i + (m - m // 4 + 1)))
                    dve.wait_ge(*when(f"{name}_dfree", 8 * i + m + 1))
                    dve.tensor_tensor(X[:, m, 0:T], ps[:, 4 + m % 2, :], X[:, m, 0:T], ALU.add).then_inc(sem(f"{name}_dfree"), 1)

                def step(i, b, slot):
                    for j in range(2):
                        hidden(i + 1, b + 3, j)
                    mods(i + 1)
                    for m in range(KT):
                        add_down(i, b + 4, m)
                        if m < 2:
                            hidden_lo(i + 1, slot, m)

                for j in range(2):
                    hidden(0, B0 + 3, j, True)
                mods(0)
                for j in range(2):
                    hidden_lo(0, 0, j)
                with dve.Fori(0, FF_IT // 3) as p:
                    for s in range(3):
                        step(3 * p + s, 15 * p + (B0 + 4 + 5 * s), (s + 1) % 3)
                for i in range(FF_IT // 3 * 3, FF_IT - 1):
                    step(i, B0 + 4 + 5 * i, (i + 1) % 3)
                mods(FF_IT)
                for m in range(KT):
                    add_down(FF_IT - 1, B0 + FF_BLOCKS - 1, m)

            rms("n2", ("ffn_g", 0))
            swiglu(0, "ff0")

            for a in (0, PADP + T):
                dve.memset(hp[:, :, a:a + PADP], 0.0).then_inc(sem("hp"), 1)
            norm_rstd("n3", 1, T)
            dve.wait_ge(*when("icnt", 16))
            n_win = 0
            for g in range(4):
                for k in (2 * g, 2 * g + 1):
                    scaled("n3", k, ("mix_g", KT), hp[:, k, PADP:PADP + T]).then_inc(sem("hp"), 1)
                dve.wait_ge(*when("hp", 2 + 2 * g + 2))
                if g:
                    dve.wait_ge(*when("pool_y", g))
                src, width = hp[:, 2 * g:2 * g + 2, :], HPAD
                for d in range(g + 1):
                    dst = (pa, pb)[d % 2]
                    width -= 1 << d
                    if d:
                        dve.wait_ge(*when("win", n_win))
                    dve.tensor_tensor(dst[:, :, 0:width], src[:, :, 0:width], src[:, :, 1 << d:(1 << d) + width],
                                      ALU.add).then_inc(sem("win"), 1)
                    n_win += 1
                    src = dst
                start = PADP - (1 << g)
                other = (pb, pa)[g % 2]
                dve.wait_ge(*when("win", n_win))
                for m in range(2):
                    dve.tensor_tensor(other[:, m, 0:T], src[:, m, start:start + T], icnt[:, g, :], ALU.mult).then_inc(sem("win"), 1)
                n_win += 2
                dve.wait_ge(*when("win", n_win))
                if g >= 2:
                    dve.wait_ge(*when("pool_lo", 2 * g - 2))
                dve.tensor_tensor(tmp[:, 2 * (g % 2):2 * (g % 2) + 2, 0:T], other[:, :, 0:T],
                                  hp[:, 2 * g:2 * g + 2, PADP:PADP + T], ALU.subtract).then_inc(sem("pool_y"), 1)
            for k in (6, 7):
                dve.wait_ge(*when("pool_hi", k + 1))
                dve.tensor_tensor(Alo[:, k, 0:T], tmp[:, k % 4, 0:T], Ahi[:, k, 0:T], ALU.subtract).then_inc(sem("pool_last"), 1)
            for j in range(8):
                if j % 4 == 3:
                    dve.wait_ge(*when("w_used", 2 * B_POOL + j // 4 + 1))
                else:
                    dve.wait_ge(*when("pool_done", j - j // 4 + 1))
                dve.scalar_tensor_tensor(out=X[:, j, 0:T], in0=ps[:, j, :], scalar=v("pool_scale", j), in1=X[:, j, 0:T],
                                         op0=ALU.mult, op1=ALU.add).then_inc(sem("pool_evac"), 1)
            rms("n4", ("ffn_g", KT))
            swiglu(1, "ff1")

            dve.wait_ge(*when("ff0_ada", ADA_PAIRS))
            dve.wait_ge(*when("ff1_ada", ADA_PAIRS))
            uses = [(0, 0, ("final_g", 0), None), (0, 3, ("ln1_g", 0), ("ln1_b", 0)), (1, 0, ("ln2_g", 0), ("ln2_b", 0)),
                    (1, 3, ("ln1_g", KT), ("ln1_b", KT))]
            for use, (layer, shift, gain, bias) in enumerate(uses):
                sc = modT[:, layer, (shift + 1) * KT:(shift + 2) * KT, :]
                dve.tensor_scalar(s1[:, use, :, :], sc, 1.0, None, ALU.add).then_inc(sem("mods"), 1)
                dve.tensor_scalar(rg[:, use, :], v(*gain, KT), ALPHA, None, ALU.mult).then_inc(sem("mods"), 1)
                if bias:
                    dve.tensor_scalar(rb[:, use, :], v(*bias, KT), ALPHA, None, ALU.mult).then_inc(sem("mods"), 1)
                else:
                    dve.tensor_copy(s2[:, use, :, :], modT[:, layer, shift * KT:(shift + 1) * KT, :]).then_inc(sem("mods"), 1)
            dve.wait_ge(*when("mods", 12))
            for use, (layer, shift, gain, bias) in enumerate(uses[1:], 1):
                for src in range(2):
                    dve.tensor_tensor(s2[:, use, :, src], s1[:, use, :, src], v(*bias, KT), ALU.mult).then_inc(sem("mods"), 1)
            dve.wait_ge(*when("mods", 18))
            for use, (layer, shift, gain, bias) in enumerate(uses):
                if bias:
                    dve.tensor_tensor(s2[:, use, :, :], s2[:, use, :, :], modT[:, layer, shift * KT:(shift + 1) * KT, :],
                                      ALU.add).then_inc(sem("mods"), 1)
                for src in range(2 if bias else 1):
                    dve.tensor_tensor(s1[:, use, :, src], s1[:, use, :, src], v(*gain, KT), ALU.mult).then_inc(sem("mods"), 1)
            dve.wait_ge(*when("mods", 28))
            dve.wait_ge(*when("tables", 16 * 5))
            norm_rstd("n5", 1, T)
            for k in range(KT + 1):
                if k < KT:
                    modulated("n5", 0, k, 0, 0, 0, T)
                    dve.tensor_scalar(tmp[:, k % 4, T:TT], X[:, k, T:TT], s1[:, 0, k, 1:2], None, ALU.mult).then_inc(sem("n5_m"), 1)
                if k >= 1:
                    split_lo_modulated("n5", 0, k - 1, 0, X_CTX)
            dve.wait_ge(*when("n5_m", 2 * KT))
            for k in range(KT):
                dve.tensor_scalar(X[:, k, T:TT], X[:, k, T:TT], ALPHA, None, ALU.mult)
                dve.scalar_tensor_tensor(out=X[:, k, 0:T], in0=X[:, k, 0:T], scalar=rg[:, 0, k:k + 1], in1=rstd[:, 0:T],
                                         op0=ALU.mult, op1=ALU.mult).then_inc(sem("n5_res"), 1)

            def rotate(dst, src, scale, half, plain_sem, rot_sem, out_sem):
                dve.scalar_tensor_tensor(out=dst, in0=src, scalar=scale, in1=cosq, op0=ALU.mult,
                                         op1=ALU.mult).then_inc(sem(plain_sem[0]), 1)
                dve.tensor_tensor(half, half, sinq, ALU.mult).then_inc(sem(rot_sem[0]), 1)
                dve.wait_ge(*when(plain_sem[0], plain_sem[1]))
                dve.wait_ge(*when(rot_sem[0], rot_sem[1]))
                dve.tensor_tensor(dst, dst, half, ALU.add).then_inc(sem(out_sem), 1)

            def move(dst, src):
                return dve.tensor_scalar(dst, src, 1.0, None, ALU.mult)

            for j in range(2):
                dve.wait_ge(*when("kvA_swap", j + 1))
                rotate(kd[:, j, 0:T], ps[:, 4 + 2 * j, :], 1.0, swapA[:, j, :], ("kvA_cos", j + 1), ("kvA_sin", j + 1), "kvA_evac")
            dve.wait_ge(*when("vA_done", 1))
            dve.tensor_copy(vA.rearrange("p t d -> p (t d)"), psf[:, 4 * 512:4 * 512 + TT]).then_inc(sem("vA"), 1)
            for j in range(8):
                dve.wait_ge(*when("qA_swap", j + 1))
                rotate(O[:, j, 0:T], ps[:, 2 * (j % 4), :], SCALE, swapA[:, j % 2, :], ("qA_cos", j + 1), ("qA_sin", j + 1), "qA_evac")
            dve.wait_ge(*when("vA", 1))
            dve.wait_ge(*when("kvA_evac", 3))
            dve.wait_ge(*when("qA_evac", 8))
            dve.sem_inc(sem("oA"), 1)
            with dve.Fori(0, 2) as g:
                def take_query(e, h):
                    half = slice(DH * (h % 2), DH * (h % 2) + DH)
                    other = slice(DH - DH * (h % 2), 2 * DH - DH * (h % 2))
                    dve.wait_ge(*when("qs_hi", 8 * g + (4 * e + h + 1)))
                    dve.tensor_tensor(qs[4 * e + h][other], O[half, bass.ds(4 * g + (2 * e + h // 2), 1), :].rearrange("p a t -> p (a t)"),
                                       qs[4 * e + h][half], ALU.subtract).then_inc(sem("qs"), 1)

                dve.wait_ge(*when("ks_hi", g + 1))
                dve.tensor_tensor(kl[:, :], kd[:, bass.ds(g, 1), :].rearrange("p a t -> p (a t)"), kh[:, :],
                                  ALU.subtract).then_inc(sem("ks"), 1)
                for h in range(4):
                    take_query(0, h)
                dve.wait_ge(*when("oA_done", N_UNITS // 4 * g + 2))
                move(vcur, vA[:, :, bass.ds(DH * g, DH)]).then_inc(sem("vcur"), 1)

                def take_values(four):
                    e, n, _ = UNITS[4 * four]
                    dve.wait_ge(*when("oA_done", N_UNITS // 4 * g + four + 3))
                    values = ps[0:DH, 6, :].rearrange("p (t h q) -> p h t q", t=2, h=2)
                    for h in range(2):
                        mm = move(O[DH * h:DH * h + DH, bass.ds(4 * g + 2 * e, 2), n * P:(n + 1) * P], values[:, h])
                    mm.then_inc(sem("oA"), 1)

                for u in range(N_UNITS + LEAD + 4):
                    if u < N_UNITS:
                        e, n, h = UNITS[u]
                        unit = N_UNITS * g + u
                        W = len(keys(n)) * P
                        a = 2 * (u % 2) * 512 + 512 + C - W
                        dve.wait_ge(*when("sA", unit + 1))
                        dve.tensor_reduce(sm[:, u % 8, 0:1], psf[:, a:a + W + 1], AX_X, ALU.max,
                                          negate=True).then_inc(sem("nmA"), 1)
                        if u in TAKE_AT:
                            take_query(1, TAKE_AT.index(u))
                    if 1 <= u < N_UNITS + 1:
                        c = sm[:, (u - 1) % 8, :]
                        dve.wait_ge(*when("sA_free", N_UNITS * g + u + 2))
                        dve.reciprocal(c[:, 2:3], c[:, 1:2]).then_inc(sem("denA"), 1)
                    four, part = divmod(u - LEAD - 7, 4)
                    if four >= 0 and part == 0:
                        take_values(four)
            for k in range(KT):
                split_lo("OA_split", "OA_hi", k, O[:, k, :], TT)
            dve.wait_ge(*when("n5_res", KT))
            for j in range(8):
                if j % 2:
                    dve.wait_ge(*block_used(B_WOA + j // 2))
                else:
                    dve.wait_ge(*when("woA_done", j // 2 + 1))
                for c, (c0, n) in enumerate(X_CTX):
                    mm = dve.scalar_tensor_tensor(out=X[:, j, c0:c0 + n], in0=ps[:, 2 * (j % 4) + c, 0:n],
                                                  scalar=mod(0, 2, j, c), in1=X[:, j, c0:c0 + n], op0=ALU.mult, op1=ALU.add)
                mm.then_inc(sem("woA_evac"), 1)
            layernorm("l1", X_CTX, 0, 1)

            def mlp(l, name, cols):
                B0 = B_ML[l]
                width = sum(n for _, n in cols)
                dve.sem_inc(sem(f"{name}_dfree"), 8)

                def hidden(i, j, first=False):
                    dve.wait_ge(*when(f"{name}_relu", 2 * i + j + 1))
                    if not first:
                        dve.wait_ge(*when(f"{name}_h", 2 * i + j - 1))
                    r = tmp[:, 2 + j, 0:width]
                    dve.tensor_tensor(tmp[:, j, 0:width], r, r, ALU.mult).then_inc(sem(f"{name}_mul"), 1)

                def hidden_lo(i, slot, j):
                    dve.wait_ge(*when(f"{name}_hi", 2 * i + j + 1))
                    dve.tensor_tensor(hlo[:, slot, j, 0:width], tmp[:, j, 0:width], hhi[:, slot, j, 0:width],
                                      ALU.subtract).then_inc(sem(f"{name}_h"), 1)

                def add_down(i, b_d, m):
                    if m % 4 == 3:
                        dve.wait_ge(*when("w_used", 2 * b_d + (m // 4 + 1)))
                    else:
                        dve.wait_ge(*when(f"{name}_down", 6 * i + (m - m // 4 + 1)))
                    dve.wait_ge(*when(f"{name}_dfree", 8 * i + m + 1))
                    for c, (c0, n) in enumerate(cols):
                        mm = dve.scalar_tensor_tensor(out=X[:, m, c0:c0 + n], in0=ps[:, 4 + len(cols) * (m % (4 // len(cols))) + c, 0:n],
                                                      scalar=mod(l, 5, m, c), in1=X[:, m, c0:c0 + n],
                                                      op0=ALU.mult, op1=ALU.add)
                    mm.then_inc(sem(f"{name}_dfree"), 1)

                for j in range(2):
                    hidden(0, j, True)
                for j in range(2):
                    hidden_lo(0, 0, j)
                dve.wait_ge(*when("l1_res" if l == 0 else "l3_res", KT))
                with dve.Fori(0, (ML_IT - 1) // 3) as p:
                    for s in range(3):
                        i = 3 * p + s
                        for j in range(2):
                            hidden(i + 1, j)
                        for m in range(KT):
                            add_down(i, 6 * p + (B0 + 2 + 2 * s), m)
                            if m < 2:
                                hidden_lo(i + 1, (s + 1) % 3, m)
                for m in range(KT):
                    add_down(ML_IT - 1, B0 + ML_BLOCKS - 1, m)

            mlp(0, "ml0", X_CTX)
            dve.sem_inc(sem("qkB_free0"), 1)
            dve.sem_inc(sem("qkB_free1"), 1)
            dve.sem_inc(sem("qkB"), 2)
            dve.sem_inc(sem("oB"), 1)
            layernorm("l2", X_CTX, 0, 2)

            with dve.Fori(0, 4) as st:
                def turned(r, bank, scale, free):
                    dve.wait_ge(*when("swB", 4 * st + r + 1))
                    if r >= 2:
                        dve.wait_ge(*when("qkB_lo", 4 * st + r - 1))
                    rotate(rot[:, r % 2, 0:T], ps[:, bank, :], scale, swapB[:, r % 2, :], (f"qkB_free{bank - 6}", 3 * st + free),
                           ("sinB", 4 * st + r + 1), "qkB")

                def query_lo(m):
                    dve.wait_ge(*when("qkB_hi", 4 * st + m + 1))
                    for t in range(2):
                        rows = slice(DH * t, DH * t + DH)
                        q_two = rot[rows, m, 0:T].rearrange("p (a n) -> p a n", a=2)
                        for half in range(2):
                            mm = dve.tensor_tensor(qB[m][DH * half:DH * half + DH, 4 + 2 * t:6 + 2 * t, :], q_two,
                                                   qB[m][rows, 2 * t:2 * t + 2, :], ALU.subtract)
                    mm.then_inc(sem("qkB_lo"), 1)

                def key_lo(m):
                    dve.wait_ge(*when("qkB_hi", 4 * st + 3 + m))
                    for t in range(2):
                        rows, other = slice(DH * t, DH * t + DH), slice(DH - DH * t, 2 * DH - DH * t)
                        mm = dve.tensor_tensor(kB[m][t][other], rot[rows, m, :], kB[m][t][rows], ALU.subtract)
                    mm.then_inc(sem("qkB_lo"), 1)

                turned(0, 6, SCALE, 2)
                turned(1, 7, SCALE, 2)
                query_lo(0)
                turned(2, 6, 1.0, 3)
                query_lo(1)
                turned(3, 6, 1.0, 4)
                key_lo(0)
                key_lo(1)

                def divisors(u):
                    unit = 8 * st + u
                    c = sm[:, u % 4, :]
                    dve.wait_ge(*when("sB_free", 2 * unit + 4))
                    dve.reciprocal(c[:, 4:6], c[:, 2:4]).then_inc(sem("denB"), 1)
                    dve.wait_ge(*when("denB", 2 * unit + 1))
                    dve.tensor_tensor(c[:, 6:7], c[:, 5:6], lamt[:, 5:6], ALU.mult).then_inc(sem("denB"), 1)

                def finish(u):
                    unit = 8 * st + u
                    p0, p1 = probB[u % 3], probB2[u % 2]
                    dve.wait_ge(*when("denB", 2 * unit + 2))
                    dve.wait_ge(*when("p0B", unit + 1))
                    dve.scalar_tensor_tensor(out=p0, in0=p1, scalar=sm[:, u % 4, 6:7], in1=p0, op0=ALU.mult,
                                             op1=ALU.add).then_inc(sem("pB"), 1)

                def take_values(hh):
                    head = 2 * st + hh
                    dve.wait_ge(*when("oB_done", head + 2))
                    move(O[:, bass.ds(head, 1), 0:T].rearrange("p a t -> p (a t)"), ps[:, 6, :]).then_inc(sem("oB"), 1)

                for u in range(9):
                    if u >= 1:
                        divisors(u - 1)
                    if u < 8:
                        for t in range(2):
                            a = 2 * t * 512 + P
                            dve.wait_ge(*when("sB", 16 * st + 2 * u + t + 1))
                            dve.tensor_reduce(sm[:, u % 4, t:t + 1], psf[:, a:a + TT], AX_X, ALU.max,
                                              negate=True).then_inc(sem("nmB"), 1)
                    if u >= 1:
                        finish(u - 1)
                    if u == 7:
                        take_values(0)
                take_values(1)
            dve.wait_ge(*when("oB", 9))
            for i in range(9):
                if i < 8:
                    if i >= 4:
                        dve.wait_ge(*when("oB_ms", i - 3))
                    dve.tensor_scalar(tmp[:, i % 4, 0:T], O[:, i, 0:T], SUB_SCALE, SUB_CLAMP, ALU.mult, ALU.min).then_inc(sem("oB_small"), 1)
                if i >= 1:
                    h = i - 1
                    dve.wait_ge(*when("oB_small", h + 1))
                    dve.tensor_scalar(tmp[:, h % 4, 0:T], tmp[:, h % 4, 0:T], -SUB_CLAMP, None, ALU.max).then_inc(sem("oB_t"), 1)
            dve.wait_ge(*when("oB_ms", 8))
            dve.tensor_scalar(hnorm[:, 0, :], ps[:, 4, 0:8 * QT], SUB_OVER, None, ALU.is_lt).then_inc(sem("oB_flag"), 1)
            dve.wait_ge(*when("oB_std", 1))
            dve.reciprocal(hnorm[:, 1, :], hnorm[:, 1, :]).then_inc(sem("oB_r"), 1)
            dve.wait_ge(*when("oB_r", 1))
            dve.wait_ge(*when("oB_flag", 1))
            dve.tensor_tensor(hnorm[:, 1, :], hnorm[:, 1, :], hnorm[:, 0, :], ALU.mult).then_inc(sem("oB_r"), 1)
            for i in range(9):
                if i < 8:
                    dve.wait_ge(*when("oB_b", i + 1))
                    dve.scalar_tensor_tensor(out=O[:, i, 0:T], in0=O[:, i, 0:T], scalar=lamt[:, 6:7], in1=ps[:, 4 + i % 4, :],
                                             op0=ALU.mult, op1=ALU.mult).then_inc(sem("oB_n"), 1)
                if i >= 1:
                    split_lo("OB_split", "OB_hi", i - 1, O[:, i - 1, 0:T], T)
            dve.wait_ge(*when("l2_res", KT))
            for j in range(8):
                if j % 2:
                    dve.wait_ge(*block_used(B_WOB + j // 2))
                else:
                    dve.wait_ge(*when("woB_done", j // 2 + 1))
                dve.scalar_tensor_tensor(out=X[:, j, 0:T], in0=ps[:, j, :], scalar=mod(1, 2, j, 0), in1=X[:, j, 0:T],
                                         op0=ALU.mult, op1=ALU.add).then_inc(sem("woB_evac"), 1)
            layernorm("l3", X_ONLY, 0, 3)
            mlp(1, "ml1", X_ONLY)
            layernorm("l4", X_ONLY, 0, None)


def constants():
    f = np.float32
    out = {"ident": np.eye(P, dtype=f), "sel4": np.array([[1, 0], [0, 1], [1, 0], [0, 1]], f)}
    n = np.arange(P)
    ang = 2 * np.pi * (np.outer(n, n) % P) / P
    out["csd"] = (np.concatenate([np.cos(ang), np.sin(ang)], 1) / math.sqrt(T * P)).astype(f)
    n = np.arange(T)
    ang = 2 * np.pi * (np.outer(n, n) % T) / T
    both = np.stack([np.cos(ang), -np.sin(ang)])
    out["dft"] = both.reshape(2, QT, P, T).transpose(2, 0, 1, 3).reshape(P, -1).astype(f)
    pos = np.arange(T)
    cnt = [np.clip(pos - w // 2 + w, 0, T) - np.clip(pos - w // 2, 0, T) for w in (2, 4, 8, 16)]
    out["icnt"] = np.broadcast_to((1.0 / np.array(cnt)).astype(f).reshape(1, -1), (P, 4 * T))
    freqs = DH // 4
    inv = f(10000.0) ** (-np.arange(freqs, dtype=f) / f(freqs))
    row = np.repeat(np.arange(T // 64, dtype=f), 64)
    col = np.tile(np.arange(64, dtype=f), T // 64)
    ang = np.concatenate([row[:, None] * inv, col[:, None] * inv], 1).astype(f).T
    out["cosq"] = np.tile(np.cos(ang), (4, 1)).astype(f)
    out["sinq"] = np.tile(np.concatenate([-np.sin(ang), np.sin(ang)]), (2, 1)).astype(f)
    q, k = np.arange(P)[:, None], np.arange(P)[None, :]
    out["masks"] = np.concatenate([np.where(k >= q, 0, NEG), np.where(k <= q, 0, NEG)], 1).astype(f)
    return out


def by_inputs(w):
    return [w[:, m:m + 256].reshape(KT, P, 256).transpose(1, 0, 2).reshape(P, BLK) for m in range(0, w.shape[1], 256)]


def by_hidden(w):
    return [w[m:m + 256].reshape(2, P, 2, 512).transpose(1, 2, 0, 3).reshape(P, BLK) for m in range(0, w.shape[0], 256)]


def stream(a):
    blocks = []
    win = by_inputs(a["w_in_ab"][0])
    blocks += [win[2], win[4], win[3], win[5], win[0], win[1]]
    blocks += by_inputs(a["w_out_ab"][0])
    for f in range(2):
        ada = by_inputs(a["w_ada_2"][f])
        gate, up, down = by_inputs(a["ffn_w_gate"][f]), by_inputs(a["ffn_w_up"][f]), by_hidden(a["ffn_w_down"][f])
        blocks += ada[0:2] + [gate[0], up[0]]
        for i in range(FF_IT - 1):
            blocks += [ada[2 * i + 2], gate[i + 1], ada[2 * i + 3], up[i + 1], down[i]]
        blocks += ada[2 * FF_IT:2 * FF_IT + 2] + [down[FF_IT - 1]]
        if f == 0:
            blocks.append(a["pool_map"][0].reshape(2, 2, 2, P, 256).transpose(3, 0, 2, 1, 4).reshape(P, BLK))
    wk, wv = a["a_wk_2"][0], a["a_wv_2"][0]
    blocks += by_inputs(np.concatenate([wk[:, 0:DH], wk[:, 0:DH], wk[:, DH:], wk[:, DH:]], 1))
    blocks += by_inputs(np.concatenate([wv, np.zeros_like(wv)], 1))
    blocks += by_inputs(a["a_wq_2"][0]) + by_inputs(a["a_wo_2"][0])
    for l in range(2):
        w1, w2 = by_inputs(a["mlp_w1_2"][l]), by_hidden(a["mlp_w2_2"][l])
        blocks += [w1[0]]
        for i in range(ML_IT - 1):
            blocks += [w1[i + 1], w2[i]]
        blocks += [w2[ML_IT - 1]]
        if l == 0:
            for q, k, w in zip(by_inputs(a["b_wq_2"][0]), by_inputs(a["b_wk_2"][0]), by_inputs(a["b_wv_2"][0])):
                blocks += [q, k, w]
            blocks += by_inputs(a["b_wo_2"][0])
    assert len(blocks) == N_BLOCKS
    return np.stack(blocks)


def features(x):
    x = np.asarray(x)
    return np.ascontiguousarray(np.moveaxis(x.reshape(*x.shape[:-1], -1, P), -1, 0)).reshape(P, -1)


def vectors(a):
    every = lambda x: np.broadcast_to(np.asarray(x).reshape(1, -1), (P, np.asarray(x).size))
    parts = {
        "mix_g": features(a["norm_mix_g"]), "ffn_g": features(a["norm_ffn_g"]),
        "conv_w": features(a["conv_w"][0]).reshape(P, TAPS, 4).transpose(0, 2, 1).reshape(P, -1),
        "conv_b": features(a["conv_b"][0]), "conv_ln_g": features(a["conv_ln_g"][0]),
        "conv_ln_b": features(a["conv_ln_b"][0]), "pool_scale": features(a["pool_scale"][0]),
        "final_g": features(a["final_g"]), "b_ada": np.repeat(features(a["b_ada_2"]), 2, axis=1),
        "ln1_g": features(a["ln1_g_2"]), "ln1_b": features(a["ln1_b_2"]), "ln2_g": features(a["ln2_g_2"]),
        "ln2_b": features(a["ln2_b_2"]), "sink": every(a["a_sink_2"][0]), "subln_g": np.asarray(a["b_subln_g_2"][0])[:, None],
        "lq1": every(a["b_lq1_2"]), "lk1": every(a["b_lk1_2"]), "lq2": every(a["b_lq2_2"]), "lk2": every(a["b_lk2_2"]),
        "c": np.stack([features(a["c_2"][0]), features(a["c_ctx_2"])], 2).reshape(P, -1),
    }
    return np.ascontiguousarray(np.concatenate([parts[n] for n in _cols], 1))


def kernel(**inputs):
    import concourse.bacc as bacc
    from concourse.bass_utils import run_bass_kernel_spmd

    a = {n: np.asarray(x) for n, x in inputs.items()}
    arrays = {n: np.ascontiguousarray(x) for n, x in constants().items()}
    arrays["stream"] = stream(a)
    arrays["vec"] = vectors(a)
    arrays["xT"] = np.ascontiguousarray(a["x"][0].reshape(T, KT, P).transpose(2, 1, 0))
    arrays["ctxT"] = np.ascontiguousarray(a["ctx_2"][0].reshape(C, KT, P).transpose(2, 1, 0))
    arrays["fmap"] = np.ascontiguousarray(a["fnet_map"][0].transpose(1, 0, 2).reshape(P, HEADS_A * P))
    nc = bacc.Bacc("TRN2", target_bir_lowering=False, num_devices=1)
    ins = {n: nc.dram_tensor(f"in_{n}", x.shape, F32, kind="ExternalInput").ap() for n, x in arrays.items()}
    out = nc.dram_tensor("out_xT", (P, KT, T), F32, kind="ExternalOutput").ap()
    build(nc, ins, out)
    got = run_bass_kernel_spmd(nc, [{f"in_{n}": x for n, x in arrays.items()}], core_ids=[0]).results[0]["out_xT"]
    return np.ascontiguousarray(got.transpose(2, 1, 0)).reshape(1, T, D)
```
